# Optimizing a Trainium2 kernel written in Bass

```python
import jax, jax.numpy as jnp
from jax import lax
import numpy as np
import jax
import jax.numpy as jnp

D_MODEL = 1024
BATCH = 1
SEQ = 256
DEPTH = 2

BLOCK = 128
HEAD_DIM = 64
N_HEADS_FOX = 16
N_HEADS_DIL = 16
WIDTH_FOX = N_HEADS_FOX * HEAD_DIM
WIDTH_DIL = N_HEADS_DIL * HEAD_DIM
DIL_PATTERNS = ((128, 1), (512, 4), (2048, 16))
N_HEADS_RET = 4
RET_QK_DIM = 256
RET_V_DIM = 512
RET_CHUNK = 128
ROT_BASE = 10000.0
EPS = 1e-6
NEG = -1e30
N_EVEN = (DEPTH + 1) // 2
N_ODD = DEPTH // 2
EVEN_IN = 4 * WIDTH_FOX + N_HEADS_FOX + 4 * WIDTH_DIL
EVEN_MIX = WIDTH_FOX + WIDTH_DIL
ODD_IN = 2 * N_HEADS_RET * RET_QK_DIM + 2 * N_HEADS_RET * RET_V_DIM
ODD_MIX = N_HEADS_RET * RET_V_DIM


f32 = jnp.float32

def rms_norm(x, g):
    xf = x.astype(f32)
    y = xf * lax.rsqrt(jnp.mean(xf * xf, axis=-1, keepdims=True) + EPS)
    return (y * g.astype(f32)).astype(x.dtype)

def forgetting_attention(q, k, v, log_f):
    Bsz, S, H, hd = q.shape
    scale = hd ** -0.5
    c = jnp.cumsum(log_f, axis=1).transpose(0, 2, 1)
    outs = []
    for i in range(S // BLOCK):
        q0, e = i * BLOCK, (i + 1) * BLOCK
        s = jnp.einsum('bqhd,bkhd->bhqk', q[:, q0:e], k[:, :e]).astype(f32) * scale
        s = s + c[:, :, q0:e, None] - c[:, :, None, :e]
        causal = jnp.arange(e)[None, :] <= (q0 + jnp.arange(BLOCK))[:, None]
        p = jax.nn.softmax(jnp.where(causal, s, NEG), axis=-1)
        outs.append(jnp.einsum('bhqk,bkhd->bqhd', p.astype(v.dtype), v[:, :e]))
    return jnp.concatenate(outs, axis=1)

def dilated_pattern(q, k, v, window, dilation):
    Bsz, S, H, hd = q.shape
    n_keys = window // dilation
    span = dilation * BLOCK
    Sp = -(-S // span) * span
    L = Sp // dilation
    nb = L // BLOCK

    def streams(t):
        t = jnp.pad(t, ((0, 0), (0, Sp - S), (0, 0), (0, 0))).reshape(Bsz, L, dilation, H, hd)
        return t.transpose(0, 2, 3, 1, 4).reshape(Bsz, dilation, H, nb, BLOCK, hd)

    def with_prev(t):
        prev = jnp.pad(t, ((0, 0), (0, 0), (0, 0), (1, 0), (0, 0), (0, 0)))[:, :, :, :-1]
        return jnp.concatenate([prev, t], axis=4)

    qs = streams(q)
    kb, vb = with_prev(streams(k)), with_prev(streams(v))
    s = jnp.einsum('brhnqd,brhnkd->brhnqk', qs, kb).astype(f32) * (hd ** -0.5)
    qi = jnp.arange(BLOCK)[:, None]
    kj = jnp.arange(2 * BLOCK)[None, :]
    dist = BLOCK + qi - kj
    band = (dist >= 0) & (dist <= n_keys)
    has_prev = (jnp.arange(nb) > 0)[:, None, None] | (kj >= BLOCK)[None]
    mask = band[None] & has_prev
    s = jnp.where(mask, s, NEG)
    lse = jax.nn.logsumexp(s, axis=-1)
    p = jnp.exp(s - lse[..., None])
    o = jnp.einsum('brhnqk,brhnkd->brhnqd', p.astype(v.dtype), vb)
    o = o.reshape(Bsz, dilation, H, L, hd).transpose(0, 3, 1, 2, 4).reshape(Bsz, Sp, H, hd)[:, :S]
    lse = lse.reshape(Bsz, dilation, H, L).transpose(0, 3, 1, 2).reshape(Bsz, Sp, H)[:, :S]
    return o, lse

def dilated_attention(q, k, v):
    outs, lses = [], []
    for window, dilation in DIL_PATTERNS:
        o, lse = dilated_pattern(q, k, v, window, dilation)
        outs.append(o)
        lses.append(lse)
    wts = jax.nn.softmax(jnp.stack(lses), axis=0)
    return jnp.einsum('pbsh,pbshd->bshd', wts.astype(q.dtype), jnp.stack(outs))

def rotate(x):
    S, half = x.shape[1], x.shape[-1] // 2
    inv = 1.0 / (ROT_BASE ** jnp.linspace(0.0, 1.0, half, dtype=f32))
    ang = jnp.arange(S, dtype=f32)[:, None] * inv[None, :]
    cos, sin = jnp.cos(ang)[None, :, None, :], jnp.sin(ang)[None, :, None, :]
    x1, x2 = x[..., 0::2].astype(f32), x[..., 1::2].astype(f32)
    y = jnp.stack([x1 * cos - x2 * sin, x1 * sin + x2 * cos], axis=-1)
    return y.reshape(x.shape).astype(x.dtype)

def retention(q, k, v):
    Bsz, S, H, dk = q.shape
    dv = v.shape[-1]
    C = RET_CHUNK
    nC = S // C
    log_gamma = jnp.log1p(-jnp.power(2.0, -5.0 - jnp.arange(H, dtype=f32)))
    pos = jnp.arange(C, dtype=f32)
    rel = pos[:, None] - pos[None, :]
    intra = jnp.where(rel >= 0, jnp.exp(log_gamma[:, None, None] * jnp.maximum(rel, 0.0)), 0.0)
    chunks = lambda t: t.reshape(Bsz, nC, C, H, t.shape[-1]).transpose(1, 0, 3, 2, 4)
    qc, kc, vc = chunks(q), chunks(k), chunks(v)
    s = jnp.einsum('nbhqd,nbhkd->nbhqk', qc, kc).astype(f32) * intra
    inner = jnp.einsum('nbhqk,nbhkd->nbhqd', s.astype(v.dtype), vc).astype(f32)
    q_decay = jnp.exp(log_gamma[:, None] * (pos + 1.0))[None, :, :, None]
    k_decay = jnp.exp(log_gamma[:, None] * (C - 1.0 - pos))[None, :, :, None]
    chunk_decay = jnp.exp(log_gamma * C)[None, :, None, None]

    def step(state, inp):
        q_i, k_i, v_i = inp
        cross = jnp.einsum('bhqd,bhde->bhqe', q_i.astype(f32), state) * q_decay
        state = state * chunk_decay + jnp.einsum('bhkd,bhke->bhde', k_i.astype(f32) * k_decay, v_i.astype(f32))
        return state, cross

    _, cross = lax.scan(step, jnp.zeros((Bsz, H, dk, dv), f32), (qc, kc, vc))
    out = inner + cross
    return out.transpose(1, 0, 3, 2, 4).reshape(Bsz, S, H, dv)

def head_group_norm(y):
    mu = jnp.mean(y, axis=-1, keepdims=True)
    var = jnp.mean(jnp.square(y - mu), axis=-1, keepdims=True)
    return (y - mu) * lax.rsqrt(var + EPS)

def even_layer(x, g_norm, w_in, b_f, w_out):
    Bsz, S, _ = x.shape
    z = rms_norm(x, g_norm) @ w_in
    cuts = [WIDTH_FOX, 2 * WIDTH_FOX, 3 * WIDTH_FOX, 4 * WIDTH_FOX,
            4 * WIDTH_FOX + N_HEADS_FOX,
            4 * WIDTH_FOX + N_HEADS_FOX + WIDTH_DIL,
            4 * WIDTH_FOX + N_HEADS_FOX + 2 * WIDTH_DIL,
            4 * WIDTH_FOX + N_HEADS_FOX + 3 * WIDTH_DIL]
    qa, ka, va, ga, fa, qb, kb, vb, gb = jnp.split(z, cuts, axis=-1)
    hA = lambda t: t.reshape(Bsz, S, N_HEADS_FOX, HEAD_DIM)
    hB = lambda t: t.reshape(Bsz, S, N_HEADS_DIL, HEAD_DIM)
    log_f = jax.nn.log_sigmoid(fa.astype(f32) + b_f.astype(f32))
    ya = forgetting_attention(hA(qa), hA(ka), hA(va), log_f).reshape(Bsz, S, WIDTH_FOX)
    yb = dilated_attention(hB(qb), hB(kb), hB(vb)).reshape(Bsz, S, WIDTH_DIL)
    y = jnp.concatenate([ya * jax.nn.silu(ga), yb * jax.nn.silu(gb)], axis=-1)
    return x + y @ w_out

def odd_layer(x, g_norm, w_in, w_out):
    Bsz, S, _ = x.shape
    qk_w, v_w = N_HEADS_RET * RET_QK_DIM, N_HEADS_RET * RET_V_DIM
    z = rms_norm(x, g_norm) @ w_in
    q, k, v, g = jnp.split(z, [qk_w, 2 * qk_w, 2 * qk_w + v_w], axis=-1)
    q = rotate(q.reshape(Bsz, S, N_HEADS_RET, RET_QK_DIM))
    k = rotate(k.reshape(Bsz, S, N_HEADS_RET, RET_QK_DIM)) * (RET_QK_DIM ** -0.5)
    y = retention(q, k, v.reshape(Bsz, S, N_HEADS_RET, RET_V_DIM))
    y = head_group_norm(y).reshape(Bsz, S, v_w).astype(x.dtype)
    return x + (y * jax.nn.silu(g)) @ w_out

def first_inputs(seed: int = 0) -> dict:
    key = jax.random.key(seed)
    ks = jax.random.split(key, 12)
    x = jax.random.normal(ks[0], (BATCH, SEQ, D_MODEL), f32)
    even_norm = 1.0 + 0.02 * jax.random.normal(ks[1], (N_EVEN, D_MODEL), f32)
    even_w_in = jax.random.normal(ks[2], (N_EVEN, D_MODEL, EVEN_IN), f32) * D_MODEL ** -0.5
    even_b_f = jax.random.uniform(ks[3], (N_EVEN, N_HEADS_FOX), f32, 1.0, 5.0)
    even_w_out = jax.random.normal(ks[4], (N_EVEN, EVEN_MIX, D_MODEL), f32) * EVEN_MIX ** -0.5
    odd_norm = 1.0 + 0.02 * jax.random.normal(ks[5], (N_ODD, D_MODEL), f32)
    odd_w_in = jax.random.normal(ks[6], (N_ODD, D_MODEL, ODD_IN), f32) * D_MODEL ** -0.5
    odd_w_out = jax.random.normal(ks[7], (N_ODD, ODD_MIX, D_MODEL), f32) * ODD_MIX ** -0.5
    final_norm = 1.0 + 0.02 * jax.random.normal(ks[8], (D_MODEL,), f32)
    return {"x": x, "even_norm": even_norm, "even_w_in": even_w_in, "even_b_f": even_b_f,
            "even_w_out": even_w_out, "odd_norm": odd_norm, "odd_w_in": odd_w_in,
            "odd_w_out": odd_w_out, "final_norm": final_norm}

def first_block(x, even_norm, even_w_in, even_b_f, even_w_out, odd_norm, odd_w_in, odd_w_out, final_norm):
    for layer in range(DEPTH):
        j = layer // 2
        if layer % 2 == 0:
            x = even_layer(x, even_norm[j], even_w_in[j], even_b_f[j], even_w_out[j])
        else:
            x = odd_layer(x, odd_norm[j], odd_w_in[j], odd_w_out[j])
    return rms_norm(x, final_norm)


N_HEADS = 8
N_KV = 2
HPG = N_HEADS // N_KV
ATTN_W = N_HEADS * HEAD_DIM
KV_W = N_KV * HEAD_DIM
CONV_CH = D_MODEL - ATTN_W
CONV_W = 3
D_MIX = ATTN_W + CONV_CH
CMP_BLOCK = 32
CMP_STRIDE = 16
CMP_HIDDEN = 256
SEL_BLOCK = 64
SEL_TOPN = 16
WINDOW = 512
WIN_QBLOCK = 128
SEL_QCHUNK = 64
D_FF = 2816
N_EXPERTS = 8
TOP_K = 2
D_FF_EXPERT = 1408
N_DENSE = (DEPTH + 1) // 2
N_MOE = DEPTH // 2
ALPHA = (2 * DEPTH) ** 0.25
BETA = (8 * DEPTH) ** -0.25
LN_EPS = 1e-5
NEG_2 = -1e30
FORCE = 1e9
SPLIT_WIDTHS = (ATTN_W, KV_W, KV_W, KV_W, KV_W, KV_W, KV_W, 3 * N_HEADS, CONV_CH, CONV_CH, CONV_CH)
D_IN = sum(SPLIT_WIDTHS)


def layer_norm(x, g, b):
    xf = x.astype(jnp.float32)
    mu = jnp.mean(xf, -1, keepdims=True)
    var = jnp.mean(jnp.square(xf - mu), -1, keepdims=True)
    return ((xf - mu) * lax.rsqrt(var + LN_EPS) * g + b).astype(x.dtype)

def compress(k, pos, w1, b1, w2, b2):
    bsz, g, s, dh = k.shape
    ratio = CMP_BLOCK // CMP_STRIDE
    n_cmp = s // CMP_STRIDE - ratio + 1
    blocks = k.reshape(bsz, g, s // CMP_STRIDE, CMP_STRIDE, dh)
    win = jnp.concatenate([blocks[:, :, r:r + n_cmp] for r in range(ratio)], axis=3)
    win = (win + pos).reshape(bsz, g, n_cmp, CMP_BLOCK * dh)
    return jax.nn.gelu(win @ w1 + b1) @ w2 + b2

def cmp_attention(q, kc, vc):
    s_len = q.shape[3]
    n = kc.shape[2]
    t = jnp.arange(s_len)
    ends = jnp.arange(n) * CMP_STRIDE + CMP_BLOCK - 1
    mask = ends[None, :] <= t[:, None]
    sc = jnp.einsum('bghsd,bgnd->bghsn', q, kc).astype(jnp.float32) * HEAD_DIM ** -0.5
    p = jax.nn.softmax(jnp.where(mask, sc, NEG_2), axis=-1) * mask
    o = jnp.einsum('bghsn,bgnd->bghsd', p.astype(vc.dtype), vc)
    return o, p

def select_blocks(p_cmp, s_len):
    n = p_cmp.shape[-1]
    n_sel = s_len // SEL_BLOCK
    cs = jnp.arange(n) * CMP_STRIDE
    ss = jnp.arange(n_sel) * SEL_BLOCK
    overlap = ((cs[:, None] < ss[None, :] + SEL_BLOCK) & (cs[:, None] + CMP_BLOCK > ss[None, :])).astype(jnp.float32)
    imp = jnp.einsum('bghsn,nj->bgsj', p_cmp, overlap)
    t = jnp.arange(s_len)[:, None]
    j = jnp.arange(n_sel)[None, :]
    cur = t // SEL_BLOCK
    valid = j * SEL_BLOCK <= t
    forced = (j == 0) | (j == cur) | (j == cur - 1)
    score = jnp.where(forced, FORCE, jnp.where(valid, imp, NEG_2))
    _, idx = lax.top_k(score, min(SEL_TOPN, n_sel))
    return idx

def sel_attention(q, ks, vs, idx):
    bsz, g, hpg, s_len, dh = q.shape
    n_sel = s_len // SEL_BLOCK
    k_top = idx.shape[-1]
    nc = s_len // SEL_QCHUNK
    kb = ks.reshape(bsz, g, n_sel, SEL_BLOCK, dh)
    vb = vs.reshape(bsz, g, n_sel, SEL_BLOCK, dh)
    qc = q.reshape(bsz, g, hpg, nc, SEL_QCHUNK, dh).transpose(3, 0, 1, 2, 4, 5)
    ic = idx.reshape(bsz, g, nc, SEL_QCHUNK, k_top).transpose(2, 0, 1, 3, 4)
    starts = jnp.arange(nc) * SEL_QCHUNK
    gather = jax.vmap(jax.vmap(lambda blk, ix: blk[ix]))

    def chunk(args):
        qq, ii, start = args
        kg = gather(kb, ii)
        vg = gather(vb, ii)
        sc = jnp.einsum('bghqd,bgqkrd->bghqkr', qq, kg).astype(jnp.float32) * HEAD_DIM ** -0.5
        pos = ii[..., None] * SEL_BLOCK + jnp.arange(SEL_BLOCK)
        tq = start + jnp.arange(SEL_QCHUNK)
        mask = (pos <= tq[None, None, :, None, None])[:, :, None]
        sc = jnp.where(mask, sc, NEG_2).reshape(bsz, g, hpg, SEL_QCHUNK, k_top * SEL_BLOCK)
        p = jax.nn.softmax(sc, axis=-1).reshape(bsz, g, hpg, SEL_QCHUNK, k_top, SEL_BLOCK)
        return jnp.einsum('bghqkr,bgqkrd->bghqd', p.astype(vg.dtype), vg)

    o = lax.map(chunk, (qc, ic, starts))
    return o.transpose(1, 2, 3, 0, 4, 5).reshape(bsz, g, hpg, s_len, dh)

def win_attention(q, kw, vw):
    bsz, g, hpg, s_len, dh = q.shape
    nb = s_len // WIN_QBLOCK
    span = WINDOW // WIN_QBLOCK
    ksz = (span + 1) * WIN_QBLOCK
    padw = ((0, 0), (0, 0), (WINDOW, 0), (0, 0))
    kp = jnp.pad(kw, padw).reshape(bsz, g, nb + span, WIN_QBLOCK, dh)
    vp = jnp.pad(vw, padw).reshape(bsz, g, nb + span, WIN_QBLOCK, dh)
    kband = jnp.concatenate([kp[:, :, i:i + nb] for i in range(span + 1)], axis=3)
    vband = jnp.concatenate([vp[:, :, i:i + nb] for i in range(span + 1)], axis=3)
    qb = q.reshape(bsz, g, hpg, nb, WIN_QBLOCK, dh)
    sc = jnp.einsum('bghnqd,bgnkd->bghnqk', qb, kband).astype(jnp.float32) * HEAD_DIM ** -0.5
    blk = jnp.arange(nb)[:, None, None] * WIN_QBLOCK
    tq = blk + jnp.arange(WIN_QBLOCK)[None, :, None]
    sk = blk - WINDOW + jnp.arange(ksz)[None, None, :]
    mask = (sk <= tq) & (tq - sk < WINDOW) & (sk >= 0)
    p = jax.nn.softmax(jnp.where(mask, sc, NEG_2), axis=-1)
    o = jnp.einsum('bghnqk,bgnkd->bghnqd', p.astype(vband.dtype), vband)
    return o.reshape(bsz, g, hpg, s_len, dh)

def short_conv(u, b_gate, c_gate, w):
    s_len = u.shape[1]
    z = jnp.pad(c_gate * u, ((0, 0), (CONV_W - 1, 0), (0, 0)))
    y = z[:, 0:s_len] * w[0]
    for i in range(1, CONV_W):
        y = y + z[:, i:i + s_len] * w[i]
    return b_gate * y

def hybrid_mixer(h, w_in, cmp_pos, cmp_w1, cmp_b1, cmp_w2, cmp_b2, conv_w, w_o):
    bsz, s_len, _ = h.shape
    z = h @ w_in
    offsets = np.cumsum(SPLIT_WIDTHS)[:-1].tolist()
    q, kc, vc, ks, vs, kw, vw, gates, u, bg, cg = jnp.split(z, offsets, axis=-1)
    q = q.reshape(bsz, s_len, N_KV, HPG, HEAD_DIM).transpose(0, 2, 3, 1, 4)

    def kv(t):
        return t.reshape(bsz, s_len, N_KV, HEAD_DIM).transpose(0, 2, 1, 3)

    kc_c = compress(kv(kc), cmp_pos[0], cmp_w1[0], cmp_b1[0], cmp_w2[0], cmp_b2[0])
    vc_c = compress(kv(vc), cmp_pos[1], cmp_w1[1], cmp_b1[1], cmp_w2[1], cmp_b2[1])
    o_cmp, p_cmp = cmp_attention(q, kc_c, vc_c)
    idx = select_blocks(p_cmp, s_len)
    o_sel = sel_attention(q, kv(ks), kv(vs), idx)
    o_win = win_attention(q, kv(kw), kv(vw))
    g = jax.nn.sigmoid(gates).reshape(bsz, s_len, 3, N_KV, HPG).transpose(2, 0, 3, 4, 1)[..., None]
    o_attn = g[0] * o_cmp + g[1] * o_sel + g[2] * o_win
    o_attn = o_attn.transpose(0, 3, 1, 2, 4).reshape(bsz, s_len, ATTN_W)
    o_conv = short_conv(u, bg, cg, conv_w)
    return jnp.concatenate([o_attn, o_conv], axis=-1) @ w_o

def swiglu(h, wg, wu, wd):
    return (jax.nn.silu(h @ wg) * (h @ wu)) @ wd

def moe_swiglu(h, w_router, wg, wu, wd):
    logits = (h @ w_router).astype(jnp.float32)
    top_v, top_i = lax.top_k(logits, TOP_K)
    w_top = jax.nn.softmax(top_v, axis=-1)
    gate = jnp.sum(jax.nn.one_hot(top_i, N_EXPERTS, dtype=jnp.float32) * w_top[..., None], axis=-2)
    out = jnp.zeros_like(h)
    for e in range(N_EXPERTS):
        out = out + gate[..., e:e + 1].astype(h.dtype) * swiglu(h, wg[e], wu[e], wd[e])
    return out

def second_inputs(seed: int = 0) -> dict:
    key = jax.random.key(seed)
    ks = jax.random.split(key, 24)

    def nrm(k, shape, scale):
        return jax.random.normal(k, shape, jnp.float32) * scale

    return {
        'x': nrm(ks[0], (BATCH, SEQ, D_MODEL), 1.0),
        'ln_in_g': 1.0 + nrm(ks[1], (D_MODEL,), 0.02),
        'ln_in_b': nrm(ks[2], (D_MODEL,), 0.02),
        'w_in': nrm(ks[3], (DEPTH, D_MODEL, D_IN), D_MODEL ** -0.5),
        'cmp_pos': nrm(ks[4], (DEPTH, 2, CMP_BLOCK, HEAD_DIM), 0.1),
        'cmp_w1': nrm(ks[5], (DEPTH, 2, CMP_BLOCK * HEAD_DIM, CMP_HIDDEN), (CMP_BLOCK * HEAD_DIM) ** -0.5),
        'cmp_b1': nrm(ks[6], (DEPTH, 2, CMP_HIDDEN), 0.02),
        'cmp_w2': nrm(ks[7], (DEPTH, 2, CMP_HIDDEN, HEAD_DIM), CMP_HIDDEN ** -0.5),
        'cmp_b2': nrm(ks[8], (DEPTH, 2, HEAD_DIM), 0.02),
        'conv_w': nrm(ks[9], (DEPTH, CONV_W, CONV_CH), CONV_W ** -0.5),
        'w_o': nrm(ks[10], (DEPTH, D_MIX, D_MODEL), BETA * D_MIX ** -0.5),
        'ln1_g': 1.0 + nrm(ks[11], (DEPTH, D_MODEL), 0.02),
        'ln1_b': nrm(ks[12], (DEPTH, D_MODEL), 0.02),
        'ln2_g': 1.0 + nrm(ks[13], (DEPTH, D_MODEL), 0.02),
        'ln2_b': nrm(ks[14], (DEPTH, D_MODEL), 0.02),
        'ffn_wg': nrm(ks[15], (N_DENSE, D_MODEL, D_FF), D_MODEL ** -0.5),
        'ffn_wu': nrm(ks[16], (N_DENSE, D_MODEL, D_FF), D_MODEL ** -0.5),
        'ffn_wd': nrm(ks[17], (N_DENSE, D_FF, D_MODEL), BETA * D_FF ** -0.5),
        'moe_router': nrm(ks[18], (N_MOE, D_MODEL, N_EXPERTS), D_MODEL ** -0.5),
        'moe_wg': nrm(ks[19], (N_MOE, N_EXPERTS, D_MODEL, D_FF_EXPERT), D_MODEL ** -0.5),
        'moe_wu': nrm(ks[20], (N_MOE, N_EXPERTS, D_MODEL, D_FF_EXPERT), D_MODEL ** -0.5),
        'moe_wd': nrm(ks[21], (N_MOE, N_EXPERTS, D_FF_EXPERT, D_MODEL), BETA * D_FF_EXPERT ** -0.5),
    }

def second_block(x, ln_in_g, ln_in_b, w_in, cmp_pos, cmp_w1, cmp_b1, cmp_w2, cmp_b2, conv_w, w_o,
              ln1_g, ln1_b, ln2_g, ln2_b, ffn_wg, ffn_wu, ffn_wd,
              moe_router, moe_wg, moe_wu, moe_wd):
    h = layer_norm(x, ln_in_g, ln_in_b)
    for l in range(DEPTH):
        m = hybrid_mixer(h, w_in[l], cmp_pos[l], cmp_w1[l], cmp_b1[l], cmp_w2[l], cmp_b2[l],
                         conv_w[l], w_o[l])
        h = layer_norm(ALPHA * h + m, ln1_g[l], ln1_b[l])
        if l % 2 == 0:
            f = swiglu(h, ffn_wg[l // 2], ffn_wu[l // 2], ffn_wd[l // 2])
        else:
            f = moe_swiglu(h, moe_router[l // 2], moe_wg[l // 2], moe_wu[l // 2], moe_wd[l // 2])
        h = layer_norm(ALPHA * h + f, ln2_g[l], ln2_b[l])
    return h


def setup_inputs(seed=0):
    out = dict(first_inputs(seed))
    for name, value in second_inputs(seed + 1).items():
        if name != "x":
            out[name + "_2"] = value
    return out


def reference(
    x, even_norm, even_w_in, even_b_f, even_w_out, odd_norm, odd_w_in, odd_w_out, final_norm,
    ln_in_g_2, ln_in_b_2, w_in_2, cmp_pos_2, cmp_w1_2, cmp_b1_2, cmp_w2_2, cmp_b2_2, conv_w_2,
    w_o_2, ln1_g_2, ln1_b_2, ln2_g_2, ln2_b_2, ffn_wg_2, ffn_wu_2, ffn_wd_2, moe_router_2,
    moe_wg_2, moe_wu_2, moe_wd_2,
):
    x = first_block(
        x, even_norm, even_w_in, even_b_f, even_w_out, odd_norm, odd_w_in, odd_w_out,
        final_norm,
    )
    return second_block(
        x, ln_in_g_2, ln_in_b_2, w_in_2, cmp_pos_2, cmp_w1_2, cmp_b1_2, cmp_w2_2, cmp_b2_2,
        conv_w_2, w_o_2, ln1_g_2, ln1_b_2, ln2_g_2, ln2_b_2, ffn_wg_2, ffn_wu_2, ffn_wd_2,
        moe_router_2, moe_wg_2, moe_wu_2, moe_wd_2,
    )


_drawn_inputs = setup_inputs


def setup_inputs(seed=0):
    import zlib

    import numpy as np

    out = dict(_drawn_inputs(seed))
    spreads = {}
    factors = {'even_norm': 4.29, 'cmp_pos_2': 4.638, 'cmp_b1_2': 8.0, 'cmp_b2_2': 8.0, 'odd_norm': 8.0}
    for name, (base, spread) in spreads.items():
        noise = np.random.default_rng([zlib.crc32(name.encode()), seed]).standard_normal(out[name].shape)
        drawn = base * np.exp(spread * noise) if base else spread * noise
        out[name] = jnp.asarray(drawn.astype(out[name].dtype))
    for name, factor in factors.items():
        out[name] = (out[name] * factor).astype(out[name].dtype)
    return out
```

```python
from contextlib import ExitStack

import numpy as np

import concourse.bass as bass
from concourse import mybir

P = 128
S = 256
NT = S // P
D = 1024
KD = D // P
SLOT = 2048
RING = 3
HD = 64
HF = 16
RH, RQK, RV = 4, 256, 512
NH, NKV = 8, 2
NCMP = 15
CB, CS = 32, 16
DEPTH = 2
FT = 22
NE = 8
PAIRS = NE // 2
NSMALL = 16 + 2 * 24 + NE
NEG = -1e30
SCALE = HD ** -0.5
ALPHA = (2 * DEPTH) ** 0.25
EPS, LN_EPS = 1e-6, 1e-5

F32 = mybir.dt.float32
F32R = mybir.dt.float32r
ALU = mybir.AluOpType
ACT = mybir.ActivationFunctionType
AX = mybir.AxisListType

EV_QK, EV_V, EV_G = (0, 16), (8, 24), (12, 28)
EV_OUT = 32
OD_QK, OD_V, OD_G, OD_OUT = 40, 48, 56, 64
L_IN = (72, 124)
L_W1 = (83, 135)
L_WO = (87, 139)
FFN_IN, FFN_DOWN = 91, 113
MOE = 143
N_SLOTS = MOE + PAIRS * 33

C_ID = 0
C_CAUSAL = C_ID + P
C_CMP = C_CAUSAL + 384
C_ROW = C_CMP + 2 * NCMP
C_RANK = C_ROW + 2
N_CONST = C_RANK + NE
E_DIL = 0
E_CUM = E_DIL + 384
O_RET = 0
O_COS = O_RET + RH * 384
O_SIN = O_COS + S
N_EXTRA = O_SIN + S

V_EVEN, V_ODD = 0, 8
V_LN = 16
V_BF = V_LN + 4 * 16
V_POS = V_BF + 16
V_B1 = V_POS + 64
V_B2K = V_B1 + 8
V_B2V = V_B2K + 2
V_CONV = V_B2V + 128
N_VEC = V_CONV + 24


def shape_constants():
    c = np.zeros((P, N_CONST), np.float32)
    even = np.zeros((P, N_EXTRA), np.float32)
    odd = np.zeros((P, N_EXTRA), np.float32)
    p = np.arange(P)
    c[:, C_ID:C_ID + P] = np.eye(P)
    t = np.concatenate([np.broadcast_to(p[:, None], (P, P)), np.broadcast_to(P + p[:, None], (P, S))], 1)
    k = np.concatenate([np.arange(P), np.arange(S)])[None, :]
    dist = t - k
    c[:, C_CAUSAL:C_CAUSAL + 384] = np.where(dist >= 0, 0.0, NEG)
    count = sum(((dist >= 0) & (dist % r == 0) & (dist <= w)).astype(np.float64)
                for w, r in ((128, 1), (512, 4), (2048, 16)))
    even[:, E_DIL:E_DIL + 384] = np.where(count > 0, np.log(np.maximum(count, 1)) / SCALE, NEG)
    ends = np.arange(NCMP) * CS + CB - 1
    for i in range(NT):
        seen = ends[None, :] <= (i * P + p)[:, None]
        c[:, C_CMP + i * NCMP:C_CMP + (i + 1) * NCMP] = np.where(seen, 0.0, NEG)
        c[:, C_ROW + i] = seen.any(1)
        even[:, E_CUM + i * S:E_CUM + (i + 1) * S] = (i * P + p)[:, None] <= np.arange(S)[None, :]
    tt = np.concatenate([np.arange(S), np.arange(P, S)])[None, :]
    kk = np.concatenate([np.broadcast_to(p[:, None], (P, S)), np.broadcast_to(P + p[:, None], (P, P))], 1)
    for h in range(RH):
        lg = np.log1p(-(2.0 ** (-5.0 - h)))
        decay = np.where(tt >= kk, np.exp(lg * np.maximum(tt - kk, 0)), 0.0)
        odd[:, O_RET + 384 * h:O_RET + 384 * (h + 1)] = decay * RQK ** -0.5
    inv = (1.0 / (10000.0 ** np.linspace(0.0, 1.0, P))).astype(np.float32)
    ang = inv[:, None] * np.arange(S, dtype=np.float32)[None, :]
    odd[:, O_COS:O_COS + S] = np.cos(ang.astype(np.float64))
    odd[:, O_SIN:O_SIN + S] = np.sin(ang.astype(np.float64))
    c[:, C_RANK:C_RANK + NE] = NE - np.arange(NE)
    return c, np.stack([even, odd])


class Ticks:

    def __init__(self, eng, sem):
        self.eng, self.sem, self.n, self.i, self.per = eng, sem, 0, None, 0

    def __call__(self, ins):
        ins.then_inc(self.sem, 1)
        self.n += 1

    def at(self):
        return self.n if self.i is None else self.i * self.per + self.n

    def sync(self):
        self.eng.wait_ge(self.sem, self.at())

    def loop(self, count, per):
        began = self.n
        with self.eng.Fori(0, count) as i:
            self.i, self.per = i, per
            yield i
            assert self.n - began == per, (self.n - began, per)
        self.i, self.n = None, began + per * count


def build(nc, a, out, stop=99):
    ctx = ExitStack()
    with ctx:
        def sb(name, shape, dt=F32):
            return ctx.enter_context(nc.sbuf_tensor(name, shape, dt))

        def sem(name):
            return ctx.enter_context(nc.semaphore(name))

        raw = [sb(f"raw{j}", [P, SLOT]) for j in range(RING)]
        w_hi = [sb(f"w_hi{j}", [P, SLOT], F32R) for j in range(RING)]
        w_lo = [sb(f"w_lo{j}", [P, SLOT], F32R) for j in range(RING)]
        x_hi, x_lo = sb("x_hi", [P, KD, S], F32R), sb("x_lo", [P, KD, S], F32R)
        y_hi, y_lo = sb("y_hi", [P, FT, S], F32R), sb("y_lo", [P, FT, S], F32R)
        x = sb("x", [P, NT, D])
        const = sb("const", [P, N_CONST])
        vec = sb("vec", [P, N_VEC])
        small_hi, small_lo = sb("small_hi", [P, KD, NSMALL], F32R), sb("small_lo", [P, KD, NSMALL], F32R)
        arena = sb("arena", [P, 8192])
        prob = sb("prob", [P, 4, 384])
        probT = sb("probT", [P, 2, 384])
        stat = sb("stat", [P, 4, 8])
        tiny = sb("tiny", [P, 256])
        part = sb("part", [P, 2, 512])
        extra = sb("extra", [P, N_EXTRA])

        def view(at, shape):
            n = int(np.prod(shape))
            names = " ".join("abc"[:len(shape)])
            return arena[:, at:at + n].rearrange(f"p ({names}) -> p {names}", **dict(zip("abc", shape)))

        qT, kT = view(0, (KD, S)), view(2048, (KD, S))
        v = view(4096, (NT, D))
        oT = view(6144, (KD, S))
        z = view(0, (NT, D))
        xT = view(2048, (KD, S))
        row = view(4096, (2, D))
        rq, rk = view(0, (RH, 2, S)), view(2048, (RH, 2, S))
        rv = view(4096, (NT, 2 * D))
        sq = view(0, (4, S))
        skd = view(1024, (2, NKV, S))
        sv = view(2048, (NT, 2, P))
        xc = view(2560, (2, 16, NKV * NCMP))
        soT = view(3520, (8, S))
        cu = view(5568, (4, S))
        cz = view(6592, (4, S + 2))
        small_raw = view(0, (KD, NSMALL))
        w2 = view(7624, (2, 2, 128))
        assert 7624 + 512 <= 8192
        xc_hi, xc_lo = (t[:, 8:12, :].rearrange("p a b -> p (a b)")[:, 0:960]
                        .rearrange("p (a b c) -> p a b c", a=2, b=16) for t in (y_hi, y_lo))
        hid = sb("hid", [P, 2, 2, 30])
        kc2 = sb("kc2", [P, 30])
        vc2 = sb("vc2", [NCMP, 2, HD])
        gates = sb("gates", [P, NT, 24])
        c8 = sb("c8", [HF, S])

        g_ps = [ctx.enter_context(nc.psum_tensor(f"g_ps{j}", [P, 512], F32)) for j in range(3)]
        a_ps = [ctx.enter_context(nc.psum_tensor(f"a_ps{j}", [P, 512], F32)) for j in range(4)]
        o_ps = ctx.enter_context(nc.psum_tensor("o_ps", [P, 512], F32))

        zero = sb("zero", [1, 512])
        zero_col = sb("zero_col", [P, 1])
        gate_rows = extra[:, :].rearrange("p (e t) -> p e t", e=NE)

        def gate_view(s):
            flat = prob[:, :, :].rearrange("p a b -> p (a b)")
            return flat[:, (s % 3) * 512:(s % 3 + 1) * 512]

        oyT = view(0, (16, S))

        def cols(t, at, n):
            return t[:, at:at + n]

        ident = cols(const, C_ID, P)

        raw_in = [sem(f"raw_in{j}") for j in range(RING)]
        hi_done, lo_done = sem("hi_done"), sem("lo_done")
        used = sem("used")
        g_free = [sem(f"g_free{j}") for j in range(3)]
        const_in, vec_in, small_in, x_in = sem("const_in"), sem("vec_in"), sem("small_in"), sem("x_in")
        extra_in, rows_in, w2_in, final_in = sem("extra_in"), sem("rows_in"), sem("w2_in"), sem("final_in")
        small_hi_done, small_done = sem("small_hi_done"), sem("small_done")
        act_own, dve_own, pool_own = sem("act_own"), sem("dve_own"), sem("pool_own")
        n_var, n_sqrt, n_z = sem("n_var"), sem("n_sqrt"), sem("n_z")
        n_tr, n_ev, n_hi, n_lo, h_done = sem("n_tr"), sem("n_ev"), sem("n_hi"), sem("n_lo"), sem("h_done")
        narrow_full, narrow_read = sem("narrow_full"), sem("narrow_read")
        f_in, f_exp, f_ln, f_log, f_cum, f_c8 = (sem("f_" + n) for n in ("in", "exp", "ln", "log", "cum", "c8"))
        sc_full, mx_done, ex_done, rc_done, pn_done = (sem(n) for n in ("sc_full", "mx_done", "ex_done", "rc_done", "pn_done"))
        tr_done, pt_done, pv_done, o_free = (sem(n) for n in ("tr_done", "pt_done", "pv_done", "o_free"))
        gate_done, y_made, y_split = sem("gate_done"), sem("y_made"), sem("y_split")
        r_sc, r_dec, r_out, r_var, r_sqrt, r_norm, r_tr, r_hi, r_lo = (
            sem("r_" + n) for n in ("sc", "dec", "out", "var", "sqrt", "norm", "tr", "hi", "lo"))
        r_y, r_ev = sem("r_y"), sem("r_ev")
        res_done = sem("res_done")
        z_pad, xc_made, xc_hi_done, xc_split = sem("z_pad"), sem("xc_made"), sem("xc_hi_done"), sem("xc_split")
        hid_full, hid_done, kv_full, kc_done, vc_done, gates_done = (
            sem(n) for n in ("hid_full", "hid_done", "kv_full", "kc_done", "vc_done", "gates_done"))
        m_log, m_d, m_exp, m_gate, m_tr, m_gT, m_full, m_rows = (
            sem("m_" + n) for n in ("log", "d", "exp", "gate", "tr", "gT", "full", "rows"))
        out_done = sem("out_done")

        g_slots = [s for a0, n in ([(0, 32), (40, 24), (72, 11), (91, 22), (124, 11)]
                                   + [(MOE + 33 * i, 22) for i in range(PAIRS)]) for s in range(a0, a0 + n)]
        g_nth = {s: sum(1 for r in g_slots if r < s and r % 3 == s % 3) for s in g_slots}
        MOE_G = len(g_slots) - 22 * PAIRS
        A_FOX, A_DIL, A_L = 0, 16, (32, 56)
        Y_EV, Y_L, Y_FFN, Y_MOE = 0, (8, 8 + 6 + FT), 8 + 6, 8 + 6 + FT + 6

        def heads_even(h0):
            return [dict(q=qT[64 * (h % 2):64 * (h % 2) + 64, h // 2, :], k=kT[64 * (h % 2):64 * (h % 2) + 64, h // 2, :],
                         v=[v[:, t, HD * h:HD * h + HD] for t in range(NT)], base=64 * (h % 2),
                         mask="causal" if h0 else "dil", fox=h if h0 else None, gate=None, group=h // 2,
                         first=True, last=True) for h in range(HF)]

        def heads_sparse():
            jobs = []
            for h in range(NH):
                b, g = 64 * (h % 2), h // 4
                for br in range(3):
                    k = skd[b:b + 64, br, g, :] if br < 2 else kc2[b:b + 64, g * NCMP:(g + 1) * NCMP]
                    vv = ([sv[:, t, br, g * HD:(g + 1) * HD] for t in range(NT)] if br < 2 else [vc2[0:NCMP, g, :]])
                    gate = 8 * (1 + br) + h if br < 2 else h
                    jobs.append(dict(q=sq[b:b + 64, h // 2, :], k=k, v=vv, base=b, mask="causal" if br < 2 else "cmp",
                                     fox=None, gate=gate, group=h // 2, first=br == 0, last=br == 2))
            return jobs

        pair_g = [sum(1 for m in range(FT) if (MOE + m) % 3 == j) for j in range(3)]

        def run(eng, s0, n, body):
            turns = n // RING if n >= 3 * RING else 0
            if turns:
                with eng.Fori(0, turns) as i:
                    for s in range(s0, s0 + RING):
                        body(s, i, s + RING * i, g_nth[s] + i)
            for s in range(s0 + turns * RING, s0 + n):
                body(s, 0, s, g_nth.get(s))

        block = ctx.enter_context(nc.Block())
        from_x, from_y = (x_hi, x_lo), (y_hi, y_lo)

        @block.sync
        def _(sp):
            sp.dma_start(x[:, :, :], a["x"].rearrange("(t p) d -> p t d", p=P)).then_inc(x_in, 16)
            n_load = {0: 40, 1: 72, 2: 72, 3: 91, 4: 91, 5: 124, 6: 124, 7: 143, 8: 143}.get(int(stop), N_SLOTS - 3) + 3
            for s in range(RING):
                sp.dma_start(raw[s][:, :], a["w"][s]).then_inc(raw_in[s], 16)
            with sp.Fori(1, n_load // RING) as i:
                for j in range(RING):
                    sp.wait_ge(lo_done, RING * (i - 1) + j + 1)
                    sp.dma_start(raw[j][:, :], a["w"][RING * i + j]).then_inc(raw_in[j], 16)
            for s in range(n_load // RING * RING, n_load):
                sp.wait_ge(lo_done, s - RING + 1)
                sp.dma_start(raw[s % RING][:, :], a["w"][s]).then_inc(raw_in[s % RING], 16)
            if stop < 99:
                return
            sp.wait_ge(h_done, 5)
            sp.dma_start(out.rearrange("b (t p) d -> p (b t) d", p=P), x[:, :, :]).then_inc(out_done, 16)
            sp.wait_ge(out_done, 16)

        @block.gpsimd
        def _(pool):
            own = Ticks(pool, pool_own)
            pool.dma_start(const[:, :], a["const"]).then_inc(const_in, 16)
            pool.dma_start(small_raw, a["small"]).then_inc(small_in, 16)
            pool.dma_start(vec[:, :], a["vec"]).then_inc(vec_in, 16)
            pool.dma_start(extra[:, :], a["extra"][0]).then_inc(extra_in, 16)
            own(pool.memset(zero_col[:, :], 0.0))
            own.sync()
            pool.memset(zero[:, :], 0.0).then_inc(z_pad, 1)

            def split_x(i):
                for b in range(4):
                    pool.wait_ge(n_hi, 4 * i + b + 1)
                    pool.tensor_tensor(x_lo[:, 2 * b:2 * b + 2, :], xT[:, 2 * b:2 * b + 2, :],
                                       x_hi[:, 2 * b:2 * b + 2, :].bitcast(F32), ALU.subtract).then_inc(n_lo, 1)

            def split_y(made, count, src, at, n, turn=0):
                pool.wait_ge(made, count)
                own(pool.tensor_tensor(y_hi[:, at:at + n, :], src,
                                       zero_col[:, 0:1].unsqueeze(2).to_broadcast([P, n, S]), ALU.add))
                pool.wait_ge(pool_own, own.n + FT * turn)
                pool.tensor_tensor(y_lo[:, at:at + n, :], src, y_hi[:, at:at + n, :].bitcast(F32),
                                   ALU.subtract).then_inc(y_split, 1)

            def wide(u):
                return part[:, u % 2, :].rearrange("p (a b) -> p a b", a=2)

            def narrow(u):
                return part[:, u % 2:u % 2 + 1, 0:S]

            def token_h(i):
                pool.wait_ge(rows_in, 16 * (i - 1))
                pool.wait_ge(n_z, 2 * (i + 1))
                for t in range(NT):
                    own(pool.tensor_tensor(x[:, t, :], z[:, t, :], row[:, 0, :], ALU.mult))
                own.sync()
                for t in range(NT):
                    ins = pool.tensor_tensor(x[:, t, :], x[:, t, :], row[:, 1, :], ALU.add)
                ins.then_inc(h_done, 1)

            def load_rows(i):
                pool.dma_start(row[:, :, :], a["rows"][i - 2].rearrange("a p d -> p a d")).then_inc(rows_in, 16)

            def normalise(jobs, a0, group_out=None):
                for i, jb in enumerate(jobs):
                    n = a0 + i
                    pool.wait_ge(rc_done, n + 1)
                    for t in range(NT):
                        at, keys = (t * NCMP, NCMP) if jb["mask"] == "cmp" else ((0, P), (P, S))[t]
                        pr = prob[:, n % 4, at:at + keys]
                        ins = pool.tensor_scalar(pr, pr, stat[:, n % 4, 4 + t:5 + t], None, ALU.mult)
                    ins.then_inc(pn_done, 1)
                    if group_out and i >= 3 and jobs[i - 3]["last"] and jobs[i - 3]["base"]:
                        group_out(jobs[i - 3]["group"])
                if group_out:
                    group_out(jobs[-1]["group"])

            split_x(0)
            for b in range(2):
                normalise(heads_even(b == 0), 16 * b)
                for u in range(4 * b, 4 * b + 4):
                    split_y(y_made, u + 1, wide(u), 2 * u, 2)
            if stop < 1:
                return
            pool.wait_ge(used, EV_OUT)
            pool.dma_start(extra[:, :], a["extra"][1]).then_inc(extra_in, 16)
            split_x(1)
            if stop < 2:
                return
            for b in range(8):
                pool.wait_ge(r_hi, b + 1)
                pool.tensor_tensor(y_lo[:, 2 * b:2 * b + 2, :], oyT[:, 2 * b:2 * b + 2, :],
                                   y_hi[:, 2 * b:2 * b + 2, :].bitcast(F32), ALU.subtract).then_inc(r_lo, 1)
            pool.wait_ge(used, OD_OUT + 8)
            pool.dma_start(view(6144, (D,)), a["rows_final"]).then_inc(final_in, 16)
            load_rows(2)
            split_x(2)
            token_h(2)
            for l in range(DEPTH):
                if stop < 3 + 4 * l:
                    return
                pool.wait_ge(n_lo, 4 * (3 + 2 * l))
                pool.wait_ge(h_done, 1 + 2 * l)
                pool.memset(cz[:, :, 0:2], 0.0).then_inc(z_pad, 1)
                pool.dma_start(w2[:, :, :, :], a["w2"][l]).then_inc(w2_in, 16)
                pool.wait_ge(xc_hi_done, l + 1)
                pool.tensor_tensor(xc_lo, xc, xc_hi.bitcast(F32), ALU.subtract).then_inc(xc_split, 1)
                for j in range(2):
                    s = L_IN[l] + 9 + j
                    split_y(g_free[s % 3], g_nth[s] + 1, wide(j), 4 + 2 * j, 2)
                normalise(heads_sparse(), A_L[l],
                          lambda g: split_y(y_made, 8 + 4 * l + g + 1, narrow(g), g, 1))
                if stop < 4 + 4 * l:
                    return
                pool.wait_ge(used, L_WO[l] + 4)
                load_rows(3 + 2 * l)
                split_x(3 + 2 * l)
                token_h(3 + 2 * l)
                if stop < 5 + 4 * l:
                    return
                if l == 0:
                    for m in range(FT):
                        s = FFN_IN + m
                        split_y(g_free[s % 3], g_nth[s] + 1, narrow(m), m, 1)
                    pool.wait_ge(used, FFN_DOWN + 11)
                    load_rows(4)
                    split_x(4)
                    token_h(4)
                else:
                    began = own.n
                    with pool.Fori(0, PAIRS) as i:
                        pool.wait_ge(used, MOE + 33 * i)
                        for m in range(FT):
                            split_y(y_made, 16 + FT * i + m + 1, narrow(m), m, 1, i)
                    own.n = began + FT * PAIRS
                    pool.wait_ge(used, N_SLOTS)
                    load_rows(6)
                    token_h(6)

        @block.tensor
        def _(pe):
            def parts_mm(ps, lhs, rhs, start, stop):
                (lh, ll), (rh, rl) = lhs, rhs
                pe.matmul(ps, lh, rh, start=start, stop=False, skip_group_check=True)
                pe.matmul(ps, lh, rl, start=False, stop=False, skip_group_check=True)
                return pe.matmul(ps, ll, rh, start=False, stop=stop, skip_group_check=True)

            def mm32(ps, lhs, rhs, start=True, stop=True):
                return pe.matmul(ps, lhs, rhs, start=start, stop=stop, skip_group_check=True)

            def pick(pair, f):
                return [f(t) for t in pair]

            def weights(s, shape):
                kw = dict(zip("kc", shape))
                return pick((w_hi[s % RING], w_lo[s % RING]), lambda t: t[:, :].rearrange("p (k c) -> p k c", **kw))

            def rows_slot(s, turn, slot, uses, src=from_x):
                pe.wait_ge(lo_done, slot + 1)
                if g_nth[s] > 0:
                    pe.wait_ge(g_free[s % 3], uses)
                w = weights(s, (KD, S))
                for m in range(2):
                    for k in range(KD):
                        mm = parts_mm(g_ps[s % 3][:, m * S:(m + 1) * S],
                                      pick(w, lambda t: t[:, k, m * P:(m + 1) * P]),
                                      pick(src, lambda t: t[:, k, :]), k == 0, k == KD - 1)
                mm.then_inc(used, 1)

            def token_mm(s, ps, src, k0, first, last):
                w = weights(s, (KD, S))
                for t in range(NT):
                    for k in range(KD):
                        mm = parts_mm(ps[:, t * S:(t + 1) * S], pick(src, lambda u: u[:, k0 + k, t * P:(t + 1) * P]),
                                      pick(w, lambda u: u[:, k, :]), first and k == 0 and t == 0, last and k == KD - 1)
                return mm

            def token_slot(s, turn, slot, uses):
                pe.wait_ge(lo_done, slot + 1)
                if g_nth[s] > 0:
                    pe.wait_ge(g_free[s % 3], uses)
                token_mm(s, g_ps[s % 3], from_x, 0, True, True).then_inc(used, 1)

            def out_slots(s0, halves, ready):
                for c in range(4):
                    for h in range(halves):
                        s = s0 + halves * c + h
                        pe.wait_ge(lo_done, s + 1)
                        if c == 0:
                            pe.wait_ge(*ready[h])
                        token_mm(s, a_ps[c], from_y, KD * h, h == 0, h == halves - 1).then_inc(used, 1)

            def transposed_norm(i):
                for b in range(4):
                    for j in range(2):
                        for t in range(NT):
                            if b == 0 and j == 0:
                                pe.wait_ge(n_z, 2 * i + t + 1)
                            k = 2 * b + j
                            tr = pe.transpose(a_ps[b][:, j * S + t * P:j * S + (t + 1) * P],
                                              z[:, t, k * P:(k + 1) * P], ident)
                    tr.then_inc(n_tr, 1)
                pe.wait_ge(n_lo, 4 * (i + 1))

            def narrow_product(at, n):
                for t in range(NT):
                    for k in range(KD):
                        mm = parts_mm(a_ps[0][:, t * 32:t * 32 + n], pick(from_x, lambda u: u[:, k, t * P:(t + 1) * P]),
                                      pick((small_hi, small_lo), lambda u: u[:, k, at:at + n]),
                                      k == 0 and t == 0, k == KD - 1)
                mm.then_inc(narrow_full, 1)

            def attention(jobs, a0, outs_read):
                def scores(i, jb):
                    n = a0 + i
                    if n >= 2:
                        pe.wait_ge(mx_done, n - 1)
                    ps, cmp = a_ps[n % 2], jb["mask"] == "cmp"
                    for t in range(NT):
                        at, keys = (t * NCMP, NCMP) if cmp else ((0, P), (P, S))[t]
                        mm = mm32(ps[:, at:at + keys], jb["q"][:, t * P:(t + 1) * P],
                                  jb["k"][:, 0:keys], stop=jb["fox"] is None)
                        if jb["fox"] is not None:
                            mm = mm32(ps[:, at:at + keys],
                                      const[0:HF, C_ID + jb["fox"]:C_ID + jb["fox"] + 1].to_broadcast([HF, P]),
                                      c8[:, 0:keys], start=False)
                    mm.then_inc(sc_full, 1)

                def turn(i, jb):
                    n = a0 + i
                    pe.wait_ge(pn_done, n + 1)
                    if n >= 2:
                        pe.wait_ge(pt_done, n - 1)
                    ps, pr = a_ps[2 + n % 2], prob[:, n % 4, :]
                    if jb["mask"] == "cmp":
                        for t in range(NT):
                            tr = pe.transpose(ps[0:NCMP, t * P:(t + 1) * P], pr[:, t * NCMP:(t + 1) * NCMP], ident)
                    else:
                        for c in range(3):
                            tr = pe.transpose(ps[:, c * P:(c + 1) * P], pr[:, c * P:(c + 1) * P], ident)
                    tr.then_inc(tr_done, 1)

                def values(i, jb):
                    n, b = a0 + i, jb["base"]
                    pe.wait_ge(pt_done, n + 1)
                    if jb["first"] and jb["group"] >= 1 and b == 0:
                        pe.wait_ge(*outs_read(jb["group"] - 1))
                    pT = probT[:, n % 2, :]
                    if jb["mask"] == "cmp":
                        mm = mm32(o_ps[b:b + HD, 0:S], jb["v"][0], pT[0:NCMP, 0:S], jb["first"], jb["last"])
                    else:
                        mm32(o_ps[b:b + HD, 0:S], jb["v"][0], pT[:, 0:S], jb["first"], False)
                        mm = mm32(o_ps[b:b + HD, P:S], jb["v"][1], pT[:, S:S + P], False, jb["last"])
                    mm.then_inc(pv_done, 1)

                for i in range(len(jobs) + 3):
                    if i < len(jobs):
                        scores(i, jobs[i])
                    if 0 <= i - 2 < len(jobs):
                        turn(i - 2, jobs[i - 2])
                    if i >= 3:
                        values(i - 3, jobs[i - 3])

            pe.wait_ge(const_in, 16)
            pe.wait_ge(z_pad, 1)
            transposed_norm(0)
            pe.wait_ge(small_done, 1)
            narrow_product(0, HF)
            pe.wait_ge(extra_in, 16)
            pe.wait_ge(f_log, 1)
            for t in range(NT):
                mm = mm32(a_ps[1][0:HF, 0:S], tiny[:, 160 + HF * t:160 + HF * (t + 1)],
                          extra[:, E_CUM + t * S:E_CUM + (t + 1) * S], t == 0, t == 1)
            mm.then_inc(f_cum, 1)
            pe.wait_ge(f_c8, 1)
            for b in range(2):
                for s in range(EV_QK[b], EV_QK[b] + 8):
                    rows_slot(s, 0, s, g_nth[s])
                for s in range(EV_V[b], EV_V[b] + 4):
                    token_slot(s, 0, s, g_nth[s])
                for s in range(EV_V[b] + 1, EV_V[b] + 4):
                    pe.wait_ge(g_free[s % 3], g_nth[s] + 1)
                attention(heads_even(b == 0), 16 * b, lambda g: (o_free, 8 * b + g + 1))
                for s in range(EV_G[b], EV_G[b] + 4):
                    rows_slot(s, 0, s, g_nth[s])
            pe.wait_ge(pt_done, 32)
            out_slots(EV_OUT, 2, ((y_split, 4), (y_split, 8)))
            if stop < 1:
                return

            transposed_norm(1)
            run(pe, OD_QK, 8, rows_slot)
            run(pe, OD_V, 8, token_slot)
            for s in range(OD_V + 5, OD_V + 8):
                pe.wait_ge(g_free[s % 3], g_nth[s] + 1)
            for h in range(RH):
                if h:
                    pe.wait_ge(r_dec, h)
                for half in range(2):
                    mm32(a_ps[0][:, 0:S], rk[:, h, half, 0:P], rq[:, h, half, :], half == 0, half == 1)
                for half in range(2):
                    mm = mm32(a_ps[0][:, S:S + P], rk[:, h, half, P:S], rq[:, h, half, P:S], half == 0, half == 1)
                mm.then_inc(r_sc, 1)
                pe.wait_ge(r_dec, h + 1)
                if h:
                    pe.wait_ge(r_norm, h)
                sT, hv = prob[:, h % 2, :], slice(h * RV, (h + 1) * RV)
                mm32(a_ps[1][:, :], sT[:, 0:P], rv[:, 0, hv])
                mm32(a_ps[2][:, :], sT[:, P:S], rv[:, 0, hv], True, False)
                mm32(a_ps[2][:, :], sT[:, S:S + P], rv[:, 1, hv], False, True).then_inc(r_out, 1)
            run(pe, OD_G, 8, token_slot)
            for b in range(8):
                pe.wait_ge(r_y, b + 1)
                if b >= 4:
                    pe.wait_ge(r_ev, b - 3)
                for j in range(2):
                    for t in range(NT):
                        k = 2 * b + j
                        tr = pe.transpose(a_ps[b % 4][:, j * S + t * P:j * S + (t + 1) * P],
                                          rv[:, t, k * P:(k + 1) * P], ident)
                tr.then_inc(r_tr, 1)
            pe.wait_ge(r_ev, 8)
            out_slots(OD_OUT, 2, ((r_lo, 4), (r_lo, 8)))
            if stop < 2:
                return

            def feed_forward(s0, off, i, uses):
                for m in range(FT):
                    rows_slot(s0 + m, 0, s0 + m + off, uses(s0 + m))
                for c in range(FT // 2):
                    s = s0 + FT + c
                    pe.wait_ge(lo_done, s + off + 1)
                    if c == 0:
                        pe.wait_ge(y_split, (Y_FFN if s0 == FFN_IN else Y_MOE) + FT + FT * i)
                    w = weights(s, (2, D))
                    for k in range(2):
                        for t in range(NT):
                            for n in range(2):
                                first = s0 == FFN_IN and c == 0 and k == 0
                                mm = parts_mm(a_ps[2 * t + n][:, :],
                                              pick(from_y, lambda u: u[:, 2 * c + k, t * P:(t + 1) * P]),
                                              pick(w, lambda u: u[:, k, n * 512:(n + 1) * 512]), first,
                                              c == FT // 2 - 1 and k == 1)
                    mm.then_inc(used, 1)

            transposed_norm(2)
            if stop < 3:
                return
            for l in range(DEPTH):
                s0 = L_IN[l]
                if l:
                    transposed_norm(4)
                narrow_product(HF + 24 * l, 24)
                for s in range(s0, s0 + 11):
                    (token_slot if s == s0 + 4 else rows_slot)(s, 0, s, g_nth[s])
                pe.wait_ge(xc_split, l + 1)
                for kind in range(2):
                    for h in range(2):
                        s = L_W1[l] + 2 * kind + h
                        pe.wait_ge(lo_done, s + 1)
                        w = weights(s, (KD, S))
                        for m in range(2):
                            for k in range(KD):
                                mm = parts_mm(o_ps[:, (2 * kind + m) * 32:(2 * kind + m) * 32 + 30],
                                              pick(w, lambda t: t[:, k, m * P:(m + 1) * P]),
                                              pick((xc_hi, xc_lo), lambda t: t[:, kind, KD * h + k, :]),
                                              kind == 0 and h == 0 and m == 0 and k == 0, h == 1 and k == KD - 1)
                        mm.then_inc(used, 1)
                pe.wait_ge(w2_in, 16 * (l + 1))
                pe.wait_ge(hid_done, l + 1)
                for m in range(2):
                    mm32(a_ps[1][:, 0:30], w2[:, 0, m, :], hid[:, 0, m, :], m == 0, m == 1)
                for g in range(NKV):
                    for m in range(2):
                        mm = mm32(a_ps[2][0:NCMP, g * HD:(g + 1) * HD], hid[:, 1, m, g * NCMP:(g + 1) * NCMP],
                                  w2[:, 1, m, 0:HD], m == 0, m == 1)
                mm.then_inc(kv_full, 1)
                pe.wait_ge(kc_done, l + 1)
                pe.wait_ge(vc_done, l + 1)
                pe.wait_ge(gates_done, l + 1)
                attention(heads_sparse(), A_L[l], lambda g: (y_made, 8 + 4 * l + g + 1))
                pe.wait_ge(pt_done, A_L[l] + 24)
                out_slots(L_WO[l], 1, ((y_split, Y_L[l] + 6),))
                if stop < 4 + 4 * l:
                    return
                transposed_norm(3 + 2 * l)
                if stop < 5 + 4 * l:
                    return
                if l == 0:
                    feed_forward(FFN_IN, 0, 0, lambda s: g_nth[s])
                    if stop < 6:
                        return
            narrow_product(HF + 48, NE)
            pe.wait_ge(m_gate, 1)
            for t in range(NT):
                tr = pe.transpose(a_ps[1][0:NE, t * P:(t + 1) * P], tiny[:, t * NE:t * NE + NE], ident)
            tr.then_inc(m_tr, 1)
            pe.wait_ge(m_gT, 1)
            for e in range(NE):
                mm = mm32(a_ps[e // 2][:, (e % 2) * S:(e % 2 + 1) * S],
                          const[0:NE, C_ID + e:C_ID + e + 1].to_broadcast([NE, P]), c8[0:NE, :])
            mm.then_inc(m_full, 1)
            pe.wait_ge(m_rows, 1)
            for n in range(4):
                mm32(a_ps[n][:, :], zero[0:1, 0:P], zero[0:1, :], True, False)
            with pe.Fori(0, PAIRS) as i:
                feed_forward(MOE, 33 * i, i, lambda s: g_nth[s] + pair_g[s % 3] * i)

        @block.scalar
        def _(act):
            own = Ticks(act, act_own)

            def split_hi(s, turn, slot):
                if s >= N_SLOTS:
                    return
                act.wait_ge(raw_in[s % RING], 16 * (s // RING + 1) + 16 * turn)
                if s >= RING:
                    act.wait_ge(used, slot - RING + 1)
                act.activation(w_hi[s % RING][:, :], raw[s % RING][:, :], ACT.Copy).then_inc(hi_done, 1)

            def ahead(s, turn=0):
                split_hi(s + RING, turn, s + RING * (1 + turn))

            def copy_slot(dst):
                def body(s, turn, slot, uses):
                    act.wait_ge(used, slot + 1)
                    src = g_ps[s % 3][:, :].rearrange("p (a b) -> p a b", a=2)
                    act.activation(dst(s, turn), src, ACT.Copy).then_inc(g_free[s % 3], 1)
                    ahead(s, turn)
                return body

            def root(count, done):
                act.wait_ge(n_var, count)
                act.activation(tiny[:, 226:228], tiny[:, 224:226], ACT.Sqrt).then_inc(done, 1)

            def hi_x(i):
                for b in range(4):
                    act.wait_ge(n_ev, 4 * i + b + 1)
                    act.activation(x_hi[:, 2 * b:2 * b + 2, :], xT[:, 2 * b:2 * b + 2, :], ACT.Copy).then_inc(n_hi, 1)

            def attention(jobs, a0):
                for i in range(len(jobs) + 2):
                    n = a0 + i
                    if i < len(jobs):
                        cmp = jobs[i]["mask"] == "cmp"
                        act.wait_ge(mx_done, n + 1)
                        for t in range(NT):
                            at, keys = (t * NCMP, NCMP) if cmp else ((0, P), (P, S))[t]
                            pr = prob[:, n % 4, at:at + keys]
                            ins = act.activation(pr, pr, ACT.Exp, bias=stat[:, n % 4, t:t + 1], scale=-1.0,
                                                 accum_out=stat[:, n % 4, 2 + t:3 + t])
                        ins.then_inc(ex_done, 1)
                    if i >= 2:
                        n, cmp = n - 2, jobs[i - 2]["mask"] == "cmp"
                        act.wait_ge(tr_done, n + 1)
                        if n >= 2:
                            act.wait_ge(pv_done, n - 1)
                        m, w = (NCMP, S) if cmp else (P, 384)
                        act.activation(probT[0:m, n % 2, 0:w], a_ps[2 + n % 2][0:m, 0:w], ACT.Copy).then_inc(pt_done, 1)

            for s in range(RING):
                split_hi(s, 0, s)
            act.wait_ge(small_in, 16)
            act.activation(small_hi[:, :, :], small_raw, ACT.Copy).then_inc(small_hi_done, 1)
            root(1, n_sqrt)
            hi_x(0)
            act.wait_ge(f_in, 1)
            act.activation(tiny[:, 96:128], tiny[:, 64:96], ACT.Exp, scale=-1.0).then_inc(f_exp, 1)
            act.wait_ge(f_ln, 1)
            act.activation(tiny[:, 128:160], tiny[:, 96:128], ACT.Ln).then_inc(f_exp, 1)
            act.wait_ge(f_cum, 1)
            act.activation(c8[:, :], a_ps[1][0:HF, 0:S], ACT.Copy, scale=-1.0 / SCALE).then_inc(f_c8, 1)
            act.wait_ge(n_lo, 4)
            for b in range(2):
                for s in range(EV_QK[b], EV_QK[b] + 8):
                    m = s - EV_QK[b]
                    copy_slot(lambda s, t: (qT if m < 4 else kT)[:, 2 * (m % 4):2 * (m % 4) + 2, :])(s, 0, s, 0)
                for s in range(EV_V[b], EV_V[b] + 4):
                    m = s - EV_V[b]
                    copy_slot(lambda s, t: v[:, :, m * S:(m + 1) * S])(s, 0, s, 0)
                attention(heads_even(b == 0), 16 * b)
                for s in range(EV_G[b], EV_G[b] + 4):
                    u = 4 * b + s - EV_G[b]
                    act.wait_ge(used, s + 1)
                    if u >= 3:
                        act.wait_ge(y_made, u - 2)
                    act.activation(gate_view(s), g_ps[s % 3][:, :], ACT.Silu).then_inc(g_free[s % 3], 1)
                    ahead(s)
            for s in range(EV_OUT, EV_OUT + 8):
                ahead(s)
            if stop < 1:
                return

            root(2, n_sqrt)
            hi_x(1)
            act.wait_ge(n_lo, 8)
            for s0, dst in ((OD_QK, None), (OD_V, lambda m, t: rv[:, :, m * S:(m + 1) * S])):
                for s in range(s0, s0 + 8):
                    if dst is None:
                        ahead(s)
                    else:
                        copy_slot(lambda s, t: dst(s - s0, t))(s, 0, s, 0)
            for h in range(RH):
                act.wait_ge(r_var, h + 1)
                act.activation(tiny[:, 226:228], tiny[:, 224:226], ACT.Sqrt).then_inc(r_sqrt, 1)
            for s in range(OD_G, OD_G + 8):
                u = s - OD_G
                act.wait_ge(used, s + 1)
                if u >= 3:
                    act.wait_ge(r_y, u - 2)
                act.activation(gate_view(s), g_ps[s % 3][:, :], ACT.Silu).then_inc(g_free[s % 3], 1)
                ahead(s)
            for b in range(8):
                act.wait_ge(r_tr, b + 1)
                act.activation(oyT[:, 2 * b:2 * b + 2, :], a_ps[b % 4][:, :].rearrange("p (a b) -> p a b", a=2),
                               ACT.Copy).then_inc(r_ev, 1)
            for s in range(OD_OUT, OD_OUT + 8):
                ahead(s)
            if stop < 2:
                return

            root(3, n_sqrt)
            root(4, n_sqrt)
            hi_x(2)
            if stop < 3:
                return
            for l in range(DEPTH):
                s0 = L_IN[l]
                if l:
                    root(6, n_sqrt)
                    hi_x(4)
                act.wait_ge(n_lo, 4 * (3 + 2 * l))
                act.wait_ge(h_done, 1 + 2 * l)
                act.wait_ge(narrow_full, 2 + l)
                act.activation(gates[:, :, :], a_ps[0][:, 0:64].rearrange("p (a b) -> p a b", a=2)[:, :, 0:24],
                               ACT.Sigmoid).then_inc(gates_done, 1)
                for s in range(s0, s0 + 11):
                    m = s - s0
                    if m < 2:
                        copy_slot(lambda s, t: sq[:, 2 * m:2 * m + 2, :])(s, 0, s, 0)
                    elif m == 3:
                        act.wait_ge(used, s + 1)
                        for g in range(NKV):
                            for d in range(2):
                                ins = act.activation(skd[64 * d:64 * d + 64, :, g, :],
                                                     g_ps[s % 3][64 * g:64 * g + 64, :].rearrange("p (a b) -> p a b", a=2),
                                                     ACT.Copy)
                        ins.then_inc(g_free[s % 3], 1)
                        ahead(s)
                    elif m == 4:
                        copy_slot(lambda s, t: sv[:, :, :, :].rearrange("p t b d -> p t (b d)"))(s, 0, s, 0)
                        act.wait_ge(xc_made, l + 1)
                        act.activation(xc_hi, xc, ACT.Copy).then_inc(xc_hi_done, 1)
                    elif m in (5, 6):
                        copy_slot(lambda s, t: cu[:, 2 * m - 10:2 * m - 8, :])(s, 0, s, 0)
                    else:
                        ahead(s)
                for s in range(L_W1[l], L_W1[l] + 4):
                    ahead(s)
                act.wait_ge(used, L_W1[l] + 4)
                for kind in range(2):
                    for m in range(2):
                        b1 = V_B1 + 4 * l + 2 * kind + m
                        ins = act.activation(hid[:, kind, m, :], o_ps[:, (2 * kind + m) * 32:(2 * kind + m) * 32 + 30],
                                             ACT.Gelu_apprx_tanh, bias=vec[:, b1:b1 + 1])
                ins.then_inc(hid_done, 1)
                attention(heads_sparse(), A_L[l])
                for s in range(L_WO[l], L_WO[l] + 4):
                    ahead(s)
                if stop < 4 + 4 * l:
                    return
                root(5 + 2 * l, n_sqrt)
                hi_x(3 + 2 * l)
                if stop < 5 + 4 * l:
                    return

                def hidden(s, slot):
                    act.wait_ge(used, slot + 1)
                    act.activation(gate_view(s)[:, 0:S], g_ps[s % 3][:, 0:S], ACT.Silu).then_inc(gate_done, 1)

                if l == 0:
                    for m in range(FT):
                        hidden(FFN_IN + m, FFN_IN + m)
                        ahead(FFN_IN + m)
                    for s in range(FFN_DOWN, FFN_DOWN + 11):
                        ahead(s)
                    if stop < 6:
                        return
                else:
                    act.wait_ge(m_d, 1)
                    act.activation(tiny[:, 100:102], tiny[:, 98:100], ACT.Exp).then_inc(m_exp, 1)
                    act.wait_ge(m_tr, 1)
                    act.activation(c8[0:NE, :], a_ps[1][0:NE, 0:S], ACT.Copy).then_inc(m_gT, 1)
                    act.wait_ge(m_full, 1)
                    for n in range(4):
                        ins = act.activation(gate_rows[:, 2 * n:2 * n + 2, :],
                                             a_ps[n][:, :].rearrange("p (a b) -> p a b", a=2), ACT.Copy)
                    ins.then_inc(m_rows, 1)

                    def pair(i, turn, last):
                        for m in range(FT):
                            hidden(MOE + m, MOE + 33 * i + m)
                            ahead(MOE + m, turn)
                        for c in range(11):
                            if not (last and c >= 8):
                                ahead(MOE + FT + c, turn)

                    with act.Fori(0, PAIRS - 1) as i:
                        pair(i, 11 * i, False)
                    pair(PAIRS - 1, 11 * (PAIRS - 1), True)
            root(8, n_sqrt)

        @block.vector
        def _(dve):
            own = Ticks(dve, dve_own)

            def split_lo(s, turn, slot):
                if s >= N_SLOTS:
                    return
                dve.wait_ge(hi_done, slot + 1)
                if s >= RING:
                    dve.wait_ge(used, slot - RING + 1)
                dve.tensor_tensor(w_lo[s % RING][:, :], raw[s % RING][:, :], w_hi[s % RING][:, :].bitcast(F32),
                                  ALU.subtract).then_inc(lo_done, 1)

            def ahead(s, turn=0):
                split_lo(s + RING, turn, s + RING * (1 + turn))

            def chain(*steps):
                for step in steps:
                    own(step())
                    own.sync()

            def inverse_root(sqrt_done, count):
                a_, r, y, t = (tiny[:, c:c + 2] for c in (224, 226, 228, 230))
                dve.wait_ge(sqrt_done, count)
                chain(lambda: dve.reciprocal(y, r),
                      lambda: dve.tensor_tensor(t, y, y, ALU.mult),
                      lambda: dve.tensor_tensor(t, t, a_, ALU.mult),
                      lambda: dve.tensor_scalar(t, t, -0.5, 1.5, ALU.mult, ALU.add),
                      lambda: dve.tensor_tensor(y, y, t, ALU.mult))
                return y

            def rms(count):
                for t in range(NT):
                    own(dve.tensor_tensor_reduce(z[:, t, :], x[:, t, :], x[:, t, :], 1.0, 0.0, ALU.mult, ALU.add,
                                                 tiny[:, 192 + t:193 + t]))
                own.sync()
                dve.tensor_scalar(tiny[:, 224:226], tiny[:, 192:194], 1.0 / D, EPS, ALU.mult, ALU.add).then_inc(n_var, 1)
                return inverse_root(n_sqrt, count)

            def moments(src, eps, done):
                stats = tiny[:, 200:224]
                for t in range(NT):
                    for c, piece in enumerate(src(t)):
                        own(dve.bn_stats(stats[:, 12 * t + 6 * c:12 * t + 6 * c + 6], piece))
                own.sync()
                for t in range(NT):
                    own(dve.bn_aggr(tiny[:, 192 + 2 * t:194 + 2 * t], stats[:, 12 * t:12 * t + 6 * len(src(t))]))
                own.sync()
                var = tiny[:, 192:196].rearrange("p (t two) -> p t two", two=2)[:, :, 1]
                dve.tensor_scalar(tiny[:, 224:226], var, eps, None, ALU.add).then_inc(done, 1)

            def layer_norm(count):
                moments(lambda t: [x[:, t, 0:512], x[:, t, 512:D]], LN_EPS, n_var)
                y = inverse_root(n_sqrt, count)
                for t in range(NT):
                    dve.tensor_scalar(z[:, t, :], x[:, t, :], tiny[:, 192 + 2 * t:193 + 2 * t], y[:, t:t + 1],
                                      ALU.subtract, ALU.mult).then_inc(n_z, 1)

            def gain_rows(i, gain, bias):
                for b in range(4):
                    dve.wait_ge(n_tr, 4 * i + b + 1)
                    for j in range(2):
                        k = 2 * b + j
                        ins = dve.tensor_scalar(xT[:, k, :], a_ps[b][:, j * S:(j + 1) * S], vec[:, gain + k:gain + k + 1],
                                                None if bias is None else vec[:, bias + k:bias + k + 1],
                                                ALU.mult, *(() if bias is None else (ALU.add,)))
                    ins.then_inc(n_ev, 1)

            def add_residual(s0, halves, scale):
                for s in range(s0, s0 + 4 * halves):
                    if (s - s0) % halves == halves - 1:
                        c = (s - s0) // halves
                        dve.wait_ge(used, s + 1)
                        xs = x[:, :, c * S:(c + 1) * S]
                        own(dve.scalar_tensor_tensor(xs, xs, scale, a_ps[c][:, :].rearrange("p (a b) -> p a b", a=2),
                                                     ALU.mult, ALU.add))
                    ahead(s)
                own.sync()

            def router():
                def t3(at):
                    return tiny[:, at:at + 2 * NE].rearrange("p (t e) -> p t e", e=NE)

                lg, on1, on2, eq, gate = t3(16), t3(32), t3(48), t3(64), t3(0)
                mx = [tiny[:, c:c + 2] for c in (92, 94)]
                rank = const[:, C_RANK:C_RANK + NE].unsqueeze(1).to_broadcast([P, NT, NE])

                def wide(c):
                    return c.unsqueeze(2).to_broadcast([P, NT, NE])

                def best(on, m):
                    r = tiny[:, 96:98]
                    chain(lambda: dve.tensor_reduce(m, lg, AX.X, ALU.max),
                          lambda: dve.tensor_tensor(eq, lg, wide(m), ALU.is_equal),
                          lambda: dve.tensor_tensor(eq, eq, rank, ALU.mult),
                          lambda: dve.tensor_reduce(r, eq, AX.X, ALU.max),
                          lambda: dve.tensor_tensor(on, eq, wide(r), ALU.is_equal))

                dve.wait_ge(narrow_full, 4)
                chain(lambda: dve.tensor_copy(lg, a_ps[0][:, 0:64].rearrange("p (a b) -> p a b", a=2)[:, :, 0:NE]))
                best(on1, mx[0])
                chain(lambda: dve.scalar_tensor_tensor(lg, on1, NEG, lg, ALU.mult, ALU.add))
                best(on2, mx[1])
                dve.tensor_tensor(tiny[:, 98:100], mx[1], mx[0], ALU.subtract).then_inc(m_d, 1)
                dve.wait_ge(m_exp, 1)
                w1_, w2_, den = tiny[:, 102:104], tiny[:, 104:106], tiny[:, 106:108]
                chain(lambda: dve.tensor_scalar(den, tiny[:, 100:102], 1.0, None, ALU.add),
                      lambda: dve.reciprocal(w1_, den),
                      lambda: dve.tensor_tensor(w2_, w1_, tiny[:, 100:102], ALU.mult),
                      lambda: dve.tensor_tensor(on1, on1, wide(w1_), ALU.mult),
                      lambda: dve.tensor_tensor(on2, on2, wide(w2_), ALU.mult))
                dve.tensor_tensor(gate, on1, on2, ALU.add).then_inc(m_gate, 1)

            def attention(jobs, a0, group_out):
                for i in range(len(jobs) + 4):
                    n = a0 + i
                    if i < len(jobs):
                        jb = jobs[i]
                        dve.wait_ge(sc_full, n + 1)
                        if n >= 4:
                            dve.wait_ge(tr_done, n - 3)
                        for t in range(NT):
                            cmp = jb["mask"] == "cmp"
                            at, keys = (t * NCMP, NCMP) if cmp else ((0, P), (P, S))[t]
                            table = {"causal": const[:, C_CAUSAL:C_CAUSAL + 384], "dil": extra[:, E_DIL:E_DIL + 384],
                                     "cmp": const[:, C_CMP:C_CMP + 2 * NCMP]}[jb["mask"]]
                            ins = dve.tensor_tensor_reduce(prob[:, n % 4, at:at + keys], a_ps[n % 2][:, at:at + keys],
                                                           table[:, at:at + keys], -SCALE, 3e38, ALU.add, ALU.min,
                                                           stat[:, n % 4, t:t + 1])
                        ins.then_inc(mx_done, 1)
                    if 1 <= i <= len(jobs):
                        m, jb = n - 1, jobs[i - 1]
                        dve.wait_ge(ex_done, m + 1)
                        rs = stat[:, m % 4, 4:6]
                        if jb["gate"] is None:
                            dve.reciprocal(rs, stat[:, m % 4, 2:4]).then_inc(rc_done, 1)
                        else:
                            own(dve.reciprocal(rs, stat[:, m % 4, 2:4]))
                            own.sync()
                            dve.tensor_tensor(rs, rs, gates[:, :, jb["gate"]], ALU.mult).then_inc(rc_done, 1)
                    if i >= 4 and jobs[i - 4]["last"] and jobs[i - 4]["base"]:
                        dve.wait_ge(pv_done, n - 3)
                        group_out(jobs[i - 4]["group"])

            def part_free(u):
                if u >= 2:
                    dve.wait_ge(y_split, u - 1)

            dve.wait_ge(small_hi_done, 1)
            dve.tensor_tensor(small_lo[:, :, :], small_raw, small_hi[:, :, :].bitcast(F32), ALU.subtract).then_inc(small_done, 1)
            dve.wait_ge(small_done, 1)
            dve.wait_ge(x_in, 16)
            y = rms(1)
            for t in range(NT):
                dve.tensor_scalar(z[:, t, :], x[:, t, :], y[:, t:t + 1], None, ALU.mult).then_inc(n_z, 1)
            dve.wait_ge(vec_in, 16)
            dve.wait_ge(const_in, 16)
            gain_rows(0, V_EVEN, None)
            for s in range(RING):
                split_lo(s, 0, s)
            f, u_, ab, e_, l_, lf = (tiny[:, c:c + 32] for c in (0, 32, 64, 96, 128, 160))
            dve.wait_ge(narrow_full, 1)
            for t in range(NT):
                own(dve.tensor_tensor(f[:, HF * t:HF * t + HF], a_ps[0][:, 32 * t:32 * t + HF], vec[:, V_BF:V_BF + HF], ALU.add))
            own.sync()
            chain(lambda: dve.tensor_scalar(ab, f, -1.0, None, ALU.mult),
                  lambda: dve.tensor_tensor(ab, ab, f, ALU.max))
            dve.tensor_scalar(u_, f, 0.0, None, ALU.min).then_inc(f_in, 1)
            dve.wait_ge(f_exp, 1)
            dve.tensor_scalar(e_, e_, 1.0, None, ALU.add).then_inc(f_ln, 1)
            dve.wait_ge(f_exp, 2)
            dve.tensor_tensor(lf, u_, l_, ALU.subtract).then_inc(f_log, 1)
            dve.wait_ge(extra_in, 16)
            for b in range(2):
                for s in range(EV_QK[b], EV_QK[b] + 12):
                    ahead(s)

                def to_oT(g):
                    dve.tensor_copy(oT[:, g, :], o_ps[:, 0:S]).then_inc(o_free, 1)

                attention(heads_even(b == 0), 16 * b, to_oT)
                dve.wait_ge(o_free, 8 * (b + 1))
                for s in range(EV_G[b], EV_G[b] + 4):
                    u, m = 4 * b + s - EV_G[b], s - EV_G[b]
                    dve.wait_ge(g_free[s % 3], g_nth[s] + 1)
                    part_free(u)
                    dve.tensor_tensor(part[:, u % 2, :], oT[:, 2 * m:2 * m + 2, :].rearrange("p a b -> p (a b)"),
                                      gate_view(s), ALU.mult).then_inc(y_made, 1)
                    ahead(s)
            add_residual(EV_OUT, 2, 1.0)
            if stop < 1:
                return

            y = rms(2)
            for t in range(NT):
                dve.tensor_scalar(z[:, t, :], x[:, t, :], y[:, t:t + 1], None, ALU.mult).then_inc(n_z, 1)
            gain_rows(1, V_ODD, None)
            dve.wait_ge(extra_in, 32)
            dve.wait_ge(n_lo, 8)
            cos, sin = (extra[:, c:c + S].unsqueeze(1).to_broadcast([P, 2, S]) for c in (O_COS, O_SIN))
            for s in range(OD_QK, OD_QK + 8):
                m, j = s - OD_QK, s % 3
                dst = (rq if m < 4 else rk)[:, m % 4, :, :]
                ps = g_ps[j][:, :].rearrange("p (a b) -> p a b", a=2)
                cc, ss = (part[:, c, :].rearrange("p (a b) -> p a b", a=2) for c in range(2))
                dve.wait_ge(used, s + 1)
                own(dve.tensor_tensor(cc, ps, cos, ALU.mult))
                dve.tensor_tensor(ss, ps, sin, ALU.mult).then_inc(g_free[j], 1)
                own.sync()
                dve.wait_ge(g_free[j], g_nth[s] + 1)
                own(dve.tensor_tensor(dst[:, 0, :], cc[:, 0, :], ss[:, 1, :], ALU.subtract))
                own(dve.tensor_tensor(dst[:, 1, :], ss[:, 0, :], cc[:, 1, :], ALU.add))
                own.sync()
                ahead(s)
            for s in range(OD_V, OD_V + 8):
                ahead(s)
            for h in range(RH):
                dve.wait_ge(r_sc, h + 1)
                dve.tensor_tensor(prob[:, h % 2, :], a_ps[0][:, 0:384], extra[:, O_RET + 384 * h:O_RET + 384 * (h + 1)],
                                  ALU.mult).then_inc(r_dec, 1)
                dve.wait_ge(r_out, h + 1)
                moments(lambda t: [a_ps[1 + t][:, :]], EPS, r_var)
                y = inverse_root(r_sqrt, h + 1)
                for t in range(NT):
                    ins = dve.tensor_scalar(rv[:, t, h * RV:(h + 1) * RV], a_ps[1 + t][:, :],
                                            tiny[:, 192 + 2 * t:193 + 2 * t], y[:, t:t + 1], ALU.subtract, ALU.mult)
                ins.then_inc(r_norm, 1)
            dve.wait_ge(r_norm, RH)
            for s in range(OD_G, OD_G + 8):
                m = s - OD_G
                dve.wait_ge(g_free[s % 3], g_nth[s] + 1)
                dst = rv[:, :, m * S:(m + 1) * S]
                dve.tensor_tensor(dst, dst, gate_view(s).rearrange("p (a b) -> p a b", a=2), ALU.mult).then_inc(r_y, 1)
                ahead(s)
            for b in range(8):
                dve.wait_ge(r_ev, b + 1)
                dve.tensor_copy(y_hi[:, 2 * b:2 * b + 2, :], oyT[:, 2 * b:2 * b + 2, :]).then_inc(r_hi, 1)
            add_residual(OD_OUT, 2, 1.0)
            if stop < 2:
                return

            y = rms(3)
            dve.wait_ge(final_in, 16)
            for t in range(NT):
                own(dve.scalar_tensor_tensor(x[:, t, :], x[:, t, :], y[:, t:t + 1], view(6144, (D,)), ALU.mult, ALU.mult))
            own.sync()
            if stop < 2.5:
                return
            layer_norm(4)
            gain_rows(2, V_LN, V_LN + 8)
            if stop < 3:
                return
            for l in range(DEPTH):
                s0 = L_IN[l]
                if l:
                    layer_norm(6)
                    gain_rows(4, V_LN + 32, V_LN + 40)
                dve.wait_ge(gates_done, l + 1)
                for t in range(NT):
                    own(dve.tensor_scalar(gates[:, t, 0:NH], gates[:, t, 0:NH], const[:, C_ROW + t:C_ROW + t + 1],
                                          None, ALU.mult))
                dve.wait_ge(n_lo, 4 * (3 + 2 * l))
                dve.wait_ge(h_done, 1 + 2 * l)
                for s in range(s0, s0 + 11):
                    m, j = s - s0, s % 3
                    ps = g_ps[j][:, :].rearrange("p (a b) -> p a b", a=2)
                    if m == 2:
                        dve.wait_ge(used, s + 1)
                        for kind in range(2):
                            pos = V_POS + 32 * l + 16 * kind
                            for g in range(NKV):
                                for par in range(2):
                                    for half in range(2):
                                        src = ps[64 * g:64 * g + 64, kind, :].rearrange(
                                            "p (n r two) -> p r n two", two=2, r=8)[:, :, half:half + NCMP, par]
                                        to = slice(64 * par, 64 * par + 64)
                                        ins = dve.tensor_tensor(
                                            xc[to, kind, 8 * half:8 * half + 8, g * NCMP:(g + 1) * NCMP], src,
                                            vec[to, pos + 8 * half:pos + 8 * half + 8].unsqueeze(2)
                                            .to_broadcast([64, 8, NCMP]), ALU.add)
                                        if kind + g + par + half < 4:
                                            own(ins)
                        ins.then_inc(g_free[j], 1)
                        dve.wait_ge(g_free[j], g_nth[s] + 1)
                        dve.tensor_scalar(tiny[:, 250:251], tiny[:, 192:193], 0.0, None, ALU.mult).then_inc(xc_made, 1)
                    elif m in (7, 8):
                        k = 2 * (m - 7)
                        dve.wait_ge(used, s + 1)
                        dve.wait_ge(g_free[(s - 2) % 3], g_nth[s - 2] + 1)
                        dve.tensor_tensor(cz[:, k:k + 2, 2:2 + S], ps, cu[:, k:k + 2, :], ALU.mult).then_inc(g_free[j], 1)
                        dve.wait_ge(g_free[j], g_nth[s] + 1)
                    elif m in (9, 10):
                        k = 2 * (m - 9)
                        yp = part[:, m - 9, :].rearrange("p (a b) -> p a b", a=2)
                        part_free(Y_L[l] + m - 9)
                        dve.wait_ge(z_pad, 2 + l)
                        for tap in range(3):
                            for q in range(2):
                                w = vec[:, V_CONV + 12 * l + 4 * tap + k + q:V_CONV + 12 * l + 4 * tap + k + q + 1]
                                src = cz[:, k + q, tap:tap + S]
                                if tap == 0:
                                    own(dve.tensor_scalar(yp[:, q, :], src, w, None, ALU.mult))
                                else:
                                    own(dve.scalar_tensor_tensor(yp[:, q, :], src, w, yp[:, q, :], ALU.mult, ALU.add))
                            own.sync()
                        dve.wait_ge(used, s + 1)
                        dve.tensor_tensor(yp, yp, ps, ALU.mult).then_inc(g_free[j], 1)
                    ahead(s)
                for s in range(L_W1[l], L_W1[l] + 4):
                    ahead(s)
                dve.wait_ge(kv_full, l + 1)
                dve.tensor_scalar(kc2[:, :], a_ps[1][:, 0:30], vec[:, V_B2K + l:V_B2K + l + 1], None, ALU.add).then_inc(kc_done, 1)
                dve.tensor_tensor(vc2[:, :, :], a_ps[2][0:NCMP, 0:128].rearrange("p (a b) -> p a b", a=2),
                                  vec[0:NCMP, V_B2V + 64 * l:V_B2V + 64 * (l + 1)].unsqueeze(1).to_broadcast([NCMP, 2, HD]),
                                  ALU.add).then_inc(vc_done, 1)

                def to_part(g):
                    part_free(Y_L[l] + 2 + g)
                    dve.tensor_copy(part[:, g % 2, 0:S], o_ps[:, 0:S]).then_inc(y_made, 1)

                own.sync()
                attention(heads_sparse(), A_L[l], to_part)
                add_residual(L_WO[l], 1, ALPHA)
                if stop < 4 + 4 * l:
                    return
                layer_norm(5 + 2 * l)
                gain_rows(3 + 2 * l, V_LN + 16 + 32 * l, V_LN + 24 + 32 * l)
                if stop < 5 + 4 * l:
                    return

                def hidden(s, u0, m, i, count, uses):
                    j, yp = s % 3, part[:, m % 2, 0:S]
                    dve.wait_ge(gate_done, count)
                    dve.wait_ge(y_split, u0 - 1)
                    dve.tensor_tensor(yp, gate_view(s)[:, 0:S], g_ps[j][:, S:2 * S], ALU.mult).then_inc(g_free[j], 1)
                    if i is not None:
                        dve.wait_ge(g_free[j], uses + 1)
                        dve.tensor_tensor(yp, yp, gate_rows[:, 2 * i + m // 11, :], ALU.mult).then_inc(y_made, 1)

                if l == 0:
                    for m in range(FT):
                        hidden(FFN_IN + m, Y_FFN + m, m, None, m + 1, None)
                        ahead(FFN_IN + m)
                    dve.wait_ge(h_done, 2)
                    for s in range(FFN_DOWN, FFN_DOWN + 11):
                        ahead(s)
                    end = FFN_DOWN + 11
                else:
                    router()
                    dve.wait_ge(m_rows, 1)

                    def pair(i, turn, last):
                        for m in range(FT):
                            s = MOE + m
                            hidden(s, Y_MOE + m + FT * i, m, i, FT + m + 1 + FT * i, g_nth[s] + pair_g[s % 3] * i)
                            ahead(s, turn)
                        for c in range(11):
                            if not (last and c >= 8):
                                ahead(MOE + FT + c, turn)

                    with dve.Fori(0, PAIRS - 1) as i:
                        pair(i, 11 * i, False)
                    pair(PAIRS - 1, 11 * (PAIRS - 1), True)
                    dve.wait_ge(h_done, 4)
                    end = N_SLOTS
                dve.wait_ge(used, end)
                for t in range(NT):
                    for n in range(2):
                        xs = x[:, t, n * 512:(n + 1) * 512]
                        own(dve.scalar_tensor_tensor(xs, xs, ALPHA, a_ps[2 * t + n][:, :], ALU.mult, ALU.add))
                own.sync()
                if l == 0 and stop < 6:
                    return
            layer_norm(8)


def in_slots(w):
    n = w.shape[1] // S
    return w.reshape(KD, P, n, S).transpose(2, 1, 0, 3).reshape(n, P, SLOT)


def out_slots_of(w):
    h = w.shape[0] // D
    return w.reshape(h, KD, P, 4, S).transpose(3, 0, 2, 1, 4).reshape(4 * h, P, SLOT)


def ffn_slots(wg, wu, wd):
    gu = np.stack([wg.reshape(KD, P, FT, P), wu.reshape(KD, P, FT, P)], 3)
    return np.concatenate([gu.transpose(2, 1, 0, 3, 4).reshape(FT, P, SLOT),
                           wd.reshape(FT // 2, 2, P, D).transpose(0, 2, 1, 3).reshape(FT // 2, P, SLOT)])


def lay_out(i):
    i = {k: np.asarray(v, np.float32) if np.asarray(v).dtype != np.float32 else np.asarray(v) for k, v in i.items()}
    ev, od = i["even_w_in"][0], i["odd_w_in"][0]
    w = []
    for at in (0, 4096 + HF):
        w.append(in_slots(ev[:, at:at + 4096]))
    w.append(out_slots_of(i["even_w_out"][0]))
    qk = od[:, :2048].reshape(D, 8, P, 2).transpose(0, 1, 3, 2).reshape(D, 2048)
    w += [in_slots(np.ascontiguousarray(qk)), in_slots(od[:, 2048:]), out_slots_of(i["odd_w_out"][0])]
    small = [ev[:, 4096:4096 + HF]]
    for l in range(DEPTH):
        wi = i["w_in_2"][l]
        q, kc, vc, ks, vs, kw, vw, gt, u, bg, cg = np.split(wi, np.cumsum([512, 128, 128, 128, 128, 128, 128, 24, 512, 512]), 1)
        small.append(gt)
        w.append(in_slots(np.concatenate([q, kc, vc, ks, kw, vs, vw, u, cg, bg], 1)))
        for kind in range(2):
            w.append(i["cmp_w1_2"][l, kind].reshape(2, KD, P, S).transpose(0, 2, 1, 3).reshape(2, P, SLOT))
        w.append(out_slots_of(i["w_o_2"][l]))
        if l == 0:
            w.append(ffn_slots(i["ffn_wg_2"][0], i["ffn_wu_2"][0], i["ffn_wd_2"][0]))
        else:
            for e in range(0, NE, 2):
                wg, wu = (np.concatenate([i[k][0, e], i[k][0, e + 1]], 1) for k in ("moe_wg_2", "moe_wu_2"))
                w.append(ffn_slots(wg, wu, i["moe_wd_2"][0, e:e + 2].reshape(-1, D)))
    small.append(i["moe_router_2"][0])
    vec = np.zeros((P, N_VEC), np.float32)

    def tiles(a):
        return a.reshape(-1, P).T

    vec[:, V_EVEN:V_EVEN + 8], vec[:, V_ODD:V_ODD + 8] = tiles(i["even_norm"][0]), tiles(i["odd_norm"][0])
    norms = [("ln_in", None), ("ln1", 0), ("ln2", 0), ("ln1", 1), ("ln2", 1)]
    pick = [[i[f"{n}_{c}_2"] if l is None else i[f"{n}_{c}_2"][l] for c in "gb"] for n, l in norms]
    for j in range(4):
        for c in range(2):
            vec[:, V_LN + 16 * j + 8 * c:V_LN + 16 * j + 8 * c + 8] = tiles(pick[j][c])
    vec[:, V_BF:V_BF + HF] = i["even_b_f"][0][None]
    w2 = np.zeros((DEPTH, P, 2, 2, P), np.float32)
    for l in range(DEPTH):
        for kind in range(2):
            vec[:, V_POS + 32 * l + 16 * kind:V_POS + 32 * l + 16 * kind + 16] = tiles(i["cmp_pos_2"][l, kind])
            vec[:, V_B1 + 4 * l + 2 * kind:V_B1 + 4 * l + 2 * kind + 2] = tiles(i["cmp_b1_2"][l, kind])
            two = i["cmp_w2_2"][l, kind].reshape(2, P, HD).transpose(1, 0, 2)
            w2[l, :, kind, :, :HD] = two
            if kind == 0:
                w2[l, :, kind, :, HD:] = two
        vec[:, V_B2K + l] = np.tile(i["cmp_b2_2"][l, 0], 2)
        vec[:, V_B2V + 64 * l:V_B2V + 64 * (l + 1)] = i["cmp_b2_2"][l, 1][None]
        for tap in range(3):
            vec[:, V_CONV + 12 * l + 4 * tap:V_CONV + 12 * l + 4 * tap + 4] = tiles(i["conv_w_2"][l, tap])
    const, extra = shape_constants()
    return {
        "x": i["x"][0], "w": np.concatenate(w), "const": const, "extra": extra, "vec": vec, "w2": w2,
        "small": np.ascontiguousarray(np.concatenate(small, 1).reshape(KD, P, NSMALL).transpose(1, 0, 2)),
        "rows_final": np.ascontiguousarray(np.broadcast_to(i["final_norm"], (P, D))),
        "rows": np.ascontiguousarray(np.broadcast_to(np.array(pick)[:, :, None], (5, 2, P, D))),
    }


def kernel(**inputs):
    import concourse.bacc as bacc
    from concourse.bass_utils import run_bass_kernel_spmd

    arrays = lay_out(inputs)
    nc = bacc.Bacc("TRN2", target_bir_lowering=False, num_devices=1)
    aps = {k: nc.dram_tensor(k + "_dram", v.shape, F32, kind="ExternalInput").ap() for k, v in arrays.items()}
    out = nc.dram_tensor("out_dram", (1, S, D), F32, kind="ExternalOutput").ap()
    build(nc, aps, out)
    r = run_bass_kernel_spmd(nc, [{k + "_dram": v for k, v in arrays.items()}], core_ids=[0])
    return r.results[0]["out_dram"]
```

```python
from contextlib import ExitStack

import numpy as np

import concourse.bass as bass
from concourse import mybir

P = 128
S = 256
NT = S // P
D = 1024
KD = D // P
SLOT = 2048
RING = 3
HD = 64
HF = 16
RH, RQK, RV = 4, 256, 512
NH, NKV = 8, 2
NCMP = 15
CB, CS = 32, 16
DEPTH = 2
FT = 22
NE = 8
PAIRS = NE // 2
NSMALL = 16 + 2 * 24 + NE
NEG = -1e30
SCALE = HD ** -0.5
ALPHA = (2 * DEPTH) ** 0.25
EPS, LN_EPS = 1e-6, 1e-5

F32 = mybir.dt.float32
F32R = mybir.dt.float32r
ALU = mybir.AluOpType
ACT = mybir.ActivationFunctionType
AX = mybir.AxisListType

EV_QK, EV_V, EV_G = (0, 16), (8, 24), (12, 28)
EV_OUT = 32
OD_QK, OD_V, OD_G, OD_OUT = 40, 48, 56, 64
L_IN = (72, 124)
L_W1 = (83, 135)
L_WO = (87, 139)
FFN_IN, FFN_DOWN = 91, 113
MOE = 143
N_SLOTS = MOE + PAIRS * 33

C_ID = 0
C_CAUSAL = C_ID + P
C_CMP = C_CAUSAL + 384
C_ROW = C_CMP + 2 * NCMP
C_RANK = C_ROW + 2
C_IOTA = C_RANK + NE
N_CONST = C_IOTA + P
E_DIL = 0
E_CUM = E_DIL + 384
O_RET = 0
O_COS = O_RET + RH * 384
O_SIN = O_COS + S
N_EXTRA = O_SIN + S

V_EVEN, V_ODD = 0, 8
V_LN = 16
V_BF = V_LN + 4 * 16
V_POS = V_BF + 16
V_B1 = V_POS + 64
V_B2K = V_B1 + 8
V_B2V = V_B2K + 2
V_CONV = V_B2V + 128
N_VEC = V_CONV + 24


def shape_constants():
    c = np.zeros((P, N_CONST), np.float32)
    even = np.zeros((P, N_EXTRA), np.float32)
    odd = np.zeros((P, N_EXTRA), np.float32)
    p = np.arange(P)
    c[:, C_ID:C_ID + P] = np.eye(P)
    t = np.concatenate([np.broadcast_to(p[:, None], (P, P)), np.broadcast_to(P + p[:, None], (P, S))], 1)
    k = np.concatenate([np.arange(P), np.arange(S)])[None, :]
    dist = t - k
    c[:, C_CAUSAL:C_CAUSAL + 384] = np.where(dist >= 0, 0.0, NEG)
    count = sum(((dist >= 0) & (dist % r == 0) & (dist <= w)).astype(np.float64)
                for w, r in ((128, 1), (512, 4), (2048, 16)))
    even[:, E_DIL:E_DIL + 384] = np.where(count > 0, np.log(np.maximum(count, 1)) / SCALE, NEG)
    ends = np.arange(NCMP) * CS + CB - 1
    for i in range(NT):
        seen = ends[None, :] <= (i * P + p)[:, None]
        c[:, C_CMP + i * NCMP:C_CMP + (i + 1) * NCMP] = np.where(seen, 0.0, NEG)
        c[:, C_ROW + i] = seen.any(1)
        even[:, E_CUM + i * S:E_CUM + (i + 1) * S] = (i * P + p)[:, None] <= np.arange(S)[None, :]
    tt = np.concatenate([np.arange(S), np.arange(P, S)])[None, :]
    kk = np.concatenate([np.broadcast_to(p[:, None], (P, S)), np.broadcast_to(P + p[:, None], (P, P))], 1)
    for h in range(RH):
        lg = np.log1p(-(2.0 ** (-5.0 - h)))
        decay = np.where(tt >= kk, np.exp(lg * np.maximum(tt - kk, 0)), 0.0)
        odd[:, O_RET + 384 * h:O_RET + 384 * (h + 1)] = decay * RQK ** -0.5
    inv = (1.0 / (10000.0 ** np.linspace(0.0, 1.0, P))).astype(np.float32)
    ang = inv[:, None] * np.arange(S, dtype=np.float32)[None, :]
    odd[:, O_COS:O_COS + S] = np.cos(ang.astype(np.float64))
    odd[:, O_SIN:O_SIN + S] = np.sin(ang.astype(np.float64))
    c[:, C_RANK:C_RANK + NE] = NE - np.arange(NE)
    c[:, C_IOTA:C_IOTA + P] = np.arange(P)
    return c, np.stack([even, odd])


class Ticks:

    def __init__(self, eng, sem):
        self.eng, self.sem, self.n, self.i, self.per = eng, sem, 0, None, 0

    def __call__(self, ins):
        ins.then_inc(self.sem, 1)
        self.n += 1

    def at(self):
        return self.n if self.i is None else self.i * self.per + self.n

    def sync(self):
        self.eng.wait_ge(self.sem, self.at())

    def loop(self, count, per):
        began = self.n
        with self.eng.Fori(0, count) as i:
            self.i, self.per = i, per
            yield i
            assert self.n - began == per, (self.n - began, per)
        self.i, self.n = None, began + per * count


def build(nc, a, out, stop=99):
    ctx = ExitStack()
    with ctx:
        def sb(name, shape, dt=F32):
            return ctx.enter_context(nc.sbuf_tensor(name, shape, dt))

        def sem(name):
            return ctx.enter_context(nc.semaphore(name))

        raw = [sb(f"raw{j}", [P, SLOT]) for j in range(RING)]
        w_hi = [sb(f"w_hi{j}", [P, SLOT], F32R) for j in range(RING)]
        w_lo = [sb(f"w_lo{j}", [P, SLOT], F32R) for j in range(RING)]
        x_hi, x_lo = sb("x_hi", [P, KD, S], F32R), sb("x_lo", [P, KD, S], F32R)
        y_hi, y_lo = sb("y_hi", [P, FT, S], F32R), sb("y_lo", [P, FT, S], F32R)
        x = sb("x", [P, NT, D])
        const = sb("const", [P, N_CONST])
        vec = sb("vec", [P, N_VEC])
        small_hi, small_lo = sb("small_hi", [P, KD, NSMALL], F32R), sb("small_lo", [P, KD, NSMALL], F32R)
        arena = sb("arena", [P, 8192])
        prob = sb("prob", [P, 4, 384])
        probT = sb("probT", [P, 2, 384])
        stat = sb("stat", [P, 4, 8])
        tiny = sb("tiny", [P, 256])
        part = sb("part", [P, 2, 512])
        extra = sb("extra", [P, N_EXTRA])

        def view(at, shape):
            n = int(np.prod(shape))
            names = " ".join("abc"[:len(shape)])
            return arena[:, at:at + n].rearrange(f"p ({names}) -> p {names}", **dict(zip("abc", shape)))

        qT, kT = view(0, (KD, S)), view(2048, (KD, S))
        v = view(4096, (NT, D))
        oT = view(6144, (KD, S))
        z = view(0, (NT, D))
        xT = view(2048, (KD, S))
        row = view(4096, (2, D))
        rq, rk = view(0, (RH, 2, S)), view(2048, (RH, 2, S))
        rv = view(4096, (NT, 2 * D))
        sq = view(0, (4, S))
        skd = view(1024, (2, NKV, S))
        sv = view(2048, (NT, 2, P))
        xc = view(2560, (2, 16, NKV * NCMP))
        soT = view(3520, (8, S))
        cu = view(5568, (4, S))
        cz = view(6592, (4, S + 2))
        small_raw = view(0, (KD, NSMALL))
        w2 = view(7624, (2, 2, 128))
        assert 7624 + 512 <= 8192
        xc_hi, xc_lo = (t[:, 8:12, :].rearrange("p a b -> p (a b)")[:, 0:960]
                        .rearrange("p (a b c) -> p a b c", a=2, b=16) for t in (y_hi, y_lo))
        hid = sb("hid", [P, 2, 2, 30])
        kc2 = sb("kc2", [P, 30])
        vc2 = sb("vc2", [NCMP, 2, HD])
        gates = sb("gates", [P, NT, 24])
        c8 = sb("c8", [P, S])

        g_ps = [ctx.enter_context(nc.psum_tensor(f"g_ps{j}", [P, 512], F32)) for j in range(3)]
        a_ps = [ctx.enter_context(nc.psum_tensor(f"a_ps{j}", [P, 512], F32)) for j in range(4)]
        o_ps = ctx.enter_context(nc.psum_tensor("o_ps", [P, 512], F32))

        zero = sb("zero", [1, 512])
        zero_col = sb("zero_col", [P, 1])
        f_acc = view(0, (NT, D))
        o_sb = view(2048, (2, D))
        upto = view(6144, (NT, S))
        sel = view(6656, (NT, 2, P))
        sel_g = view(7168, (NT, 2, P))
        back = view(7680, (2, S))
        ranks = sb("ranks", [P, 2, NT, 2 * NE])
        ranks_now = sb("ranks_now", [P, 2, NT, 2])
        loops = sb("loops", [1, 1], mybir.dt.int32)

        def gate_view(s):
            flat = prob[:, :, :].rearrange("p a b -> p (a b)")
            return flat[:, (s % 3) * 512:(s % 3 + 1) * 512]

        oyT = view(0, (16, S))

        def hidden_at(m):
            return part[:, m % 8 // 4, (m % 4) * P:(m % 4 + 1) * P]

        def cols(t, at, n):
            return t[:, at:at + n]

        ident = cols(const, C_ID, P)

        raw_in = [sem(f"raw_in{j}") for j in range(RING)]
        hi_done, lo_done = sem("hi_done"), sem("lo_done")
        used = sem("used")
        g_free = [sem(f"g_free{j}") for j in range(3)]
        const_in, vec_in, small_in, x_in = sem("const_in"), sem("vec_in"), sem("small_in"), sem("x_in")
        extra_in, rows_in, w2_in, final_in = sem("extra_in"), sem("rows_in"), sem("w2_in"), sem("final_in")
        small_hi_done, small_done = sem("small_hi_done"), sem("small_done")
        act_own, dve_own, pool_own = sem("act_own"), sem("dve_own"), sem("pool_own")
        n_var, n_sqrt, n_z = sem("n_var"), sem("n_sqrt"), sem("n_z")
        n_tr, n_ev, n_hi, n_lo, h_done = sem("n_tr"), sem("n_ev"), sem("n_hi"), sem("n_lo"), sem("h_done")
        narrow_full, narrow_read = sem("narrow_full"), sem("narrow_read")
        f_in, f_exp, f_ln, f_log, f_cum, f_c8 = (sem("f_" + n) for n in ("in", "exp", "ln", "log", "cum", "c8"))
        sc_full, mx_done, ex_done, rc_done, pn_done = (sem(n) for n in ("sc_full", "mx_done", "ex_done", "rc_done", "pn_done"))
        tr_done, pv_done, o_free = (sem(n) for n in ("tr_done", "pv_done", "o_free"))
        pt_done = [sem("pt_even"), sem("pt_odd")]
        gate_done, y_made, y_split = sem("gate_done"), sem("y_made"), sem("y_split")
        r_sc, r_dec, r_out, r_var, r_sqrt, r_norm, r_tr, r_hi, r_lo = (
            sem("r_" + n) for n in ("sc", "dec", "out", "var", "sqrt", "norm", "tr", "hi", "lo"))
        r_y, r_ev = sem("r_y"), sem("r_ev")
        res_done = sem("res_done")
        z_pad, xc_made, xc_hi_done, xc_split = sem("z_pad"), sem("xc_made"), sem("xc_hi_done"), sem("xc_split")
        hid_full, hid_done, kv_full, kc_done, vc_done, gates_done = (
            sem(n) for n in ("hid_full", "hid_done", "kv_full", "kc_done", "vc_done", "gates_done"))
        m_d, m_exp, m_on, m_rank, upto_in, m_loops = (sem("m_" + n) for n in ("d", "exp", "on", "rank", "upto_in", "loops"))
        m_now, m_sel, m_x, m_xhi, m_xlo = (sem("m_" + n) for n in ("now", "sel", "x", "xhi", "xlo"))
        m_tr, m_back, m_ytr, m_yhi, m_y, m_osb, m_sct, m_acc = (
            sem("m_" + n) for n in ("tr", "back", "ytr", "yhi", "y", "osb", "sct", "acc"))
        out_done = sem("out_done")

        g_slots = [s for a0, n in ([(0, 32), (40, 24), (72, 11), (91, 22), (124, 11)]
                                   + [(MOE + 33 * i, 22) for i in range(PAIRS)]) for s in range(a0, a0 + n)]
        g_nth = {s: sum(1 for r in g_slots if r < s and r % 3 == s % 3) for s in g_slots}
        MOE_G = len(g_slots) - 22 * PAIRS
        A_FOX, A_DIL, A_L = 0, 8, (16, 28)
        Y_L, Y_FFN = (8, 8 + 6 + FT), 8 + 6

        def pairs_even(fox):
            return [dict(q=[qT[b:b + 64, p, :] for b in (0, 64)], k=[kT[b:b + 64, p, :] for b in (0, 64)],
                         v=[[v[:, t, HD * h:HD * h + HD] for t in range(NT)] for h in (2 * p, 2 * p + 1)],
                         mask="causal" if fox else "dil", fox=2 * p if fox else None, gate=None, group=p,
                         first=True, last=True) for p in range(HF // 2)]

        def pairs_sparse():
            jobs = []
            for p in range(NH // 2):
                g = p // 2
                for br in range(3):
                    k = [skd[b:b + 64, br, g, :] if br < 2 else kc2[b:b + 64, g * NCMP:(g + 1) * NCMP] for b in (0, 64)]
                    vv = ([sv[:, t, br, g * HD:(g + 1) * HD] for t in range(NT)] if br < 2 else [vc2[0:NCMP, g, :]])
                    gate = 8 * (1 + br) + 2 * p if br < 2 else 2 * p
                    jobs.append(dict(q=[sq[b:b + 64, p, :] for b in (0, 64)], k=k, v=[vv, vv],
                                     mask="causal" if br < 2 else "cmp", fox=None, gate=gate, group=p,
                                     first=br == 0, last=br == 2))
            return jobs

        def spans(jb):
            return ((0, NCMP), (NCMP, NCMP)) if jb["mask"] == "cmp" else ((0, P), (P, S))

        pair_g = [sum(1 for m in range(FT) if (MOE + m) % 3 == j) for j in range(3)]

        def loops_of(eng):
            eng.wait_ge(m_loops, 1)
            return eng.value_load(loops[0:1, 0:1], min_val=PAIRS - 1, max_val=2 * PAIRS - 1)

        def run(eng, s0, n, body):
            turns = n // RING if n >= 3 * RING else 0
            if turns:
                with eng.Fori(0, turns) as i:
                    for s in range(s0, s0 + RING):
                        body(s, i, s + RING * i, g_nth[s] + i)
            for s in range(s0 + turns * RING, s0 + n):
                body(s, 0, s, g_nth.get(s))

        GATHER = (1, 3, 5, 7)
        block = ctx.enter_context(nc.Block())
        from_x, from_y = (x_hi, x_lo), (y_hi, y_lo)

        @block.sync
        def _(sp):
            sp.dma_start(x[:, :, :], a["x"].rearrange("(t p) d -> p t d", p=P)).then_inc(x_in, 16)
            n_load = {0: 40, 1: 72, 2: 72, 3: 91, 4: 91, 5: 124, 6: 124, 7: 143, 8: 143}.get(int(stop), N_SLOTS - 3) + 3
            for s in range(RING):
                sp.dma_start(raw[s][:, :], a["w"][s]).then_inc(raw_in[s], 16)
            with sp.Fori(1, n_load // RING) as i:
                for j in range(RING):
                    sp.wait_ge(lo_done, RING * (i - 1) + j + 1)
                    sp.dma_start(raw[j][:, :], a["w"][RING * i + j]).then_inc(raw_in[j], 16)
            for s in range(n_load // RING * RING, n_load):
                sp.wait_ge(lo_done, s - RING + 1)
                sp.dma_start(raw[s % RING][:, :], a["w"][s]).then_inc(raw_in[s % RING], 16)
            if stop < 99:
                return
            more = loops_of(sp) - (PAIRS - 1)
            with sp.Fori(0, more * (33 // RING)) as i:
                for j in range(RING):
                    sp.wait_ge(lo_done, N_SLOTS - RING + j + 1 + RING * i)
                    sp.dma_start(raw[(N_SLOTS + j) % RING][:, :], a["w"][MOE + j + RING * i]).then_inc(raw_in[(N_SLOTS + j) % RING], 16)
            sp.wait_ge(h_done, 5)
            sp.dma_start(out.rearrange("b (t p) d -> p (b t) d", p=P), x[:, :, :]).then_inc(out_done, 16)
            sp.wait_ge(out_done, 16)

        @block.gpsimd
        def _(pool):
            own = Ticks(pool, pool_own)
            pool.dma_start(const[:, :], a["const"]).then_inc(const_in, 16)
            pool.dma_start(small_raw, a["small"]).then_inc(small_in, 16)
            pool.dma_start(vec[:, :], a["vec"]).then_inc(vec_in, 16)
            pool.dma_start(extra[:, :], a["extra"][0]).then_inc(extra_in, 16)
            own(pool.memset(zero_col[:, :], 0.0))
            own(pool.memset(c8[:, :], 0.0))
            own.sync()
            pool.memset(zero[:, :], 0.0).then_inc(z_pad, 1)

            def split_x(i):
                for b in range(4):
                    pool.wait_ge(n_hi, 4 * i + b + 1)
                    pool.tensor_tensor(x_lo[:, 2 * b:2 * b + 2, :], xT[:, 2 * b:2 * b + 2, :],
                                       x_hi[:, 2 * b:2 * b + 2, :].bitcast(F32), ALU.subtract).then_inc(n_lo, 1)

            def split_y(made, count, src, at, n, turn=0):
                pool.wait_ge(made, count)
                own(pool.tensor_tensor(y_hi[:, at:at + n, :], src,
                                       zero_col[:, 0:1].unsqueeze(2).to_broadcast([P, n, S]), ALU.add))
                pool.wait_ge(pool_own, own.n + FT * turn)
                pool.tensor_tensor(y_lo[:, at:at + n, :], src, y_hi[:, at:at + n, :].bitcast(F32),
                                   ALU.subtract).then_inc(y_split, 1)

            def wide(u):
                return part[:, u % 2, :].rearrange("p (a b) -> p a b", a=2)

            def narrow(u):
                return part[:, u % 2:u % 2 + 1, 0:S]

            def token_h(i):
                pool.wait_ge(rows_in, 16 * (i - 1))
                pool.wait_ge(n_z, 2 * (i + 1))
                for t in range(NT):
                    own(pool.tensor_tensor(x[:, t, :], z[:, t, :], row[:, 0, :], ALU.mult))
                own.sync()
                for t in range(NT):
                    ins = pool.tensor_tensor(x[:, t, :], x[:, t, :], row[:, 1, :], ALU.add)
                ins.then_inc(h_done, 1)

            def load_rows(i):
                pool.dma_start(row[:, :, :], a["rows"][i - 2].rearrange("a p d -> p a d")).then_inc(rows_in, 16)

            def normalise(jobs, a0, group_out=None):
                for i, jb in enumerate(jobs):
                    for h in range(2):
                        n = 2 * (a0 + i) + h
                        pool.wait_ge(rc_done, n + 1)
                        for t, (at, keys) in enumerate(spans(jb)):
                            pr = prob[:, n % 4, at:at + keys]
                            ins = pool.tensor_scalar(pr, pr, stat[:, n % 4, 4 + t:5 + t], None, ALU.mult)
                        ins.then_inc(pn_done, 1)
                    if group_out and i >= 2 and jobs[i - 2]["last"]:
                        group_out(jobs[i - 2]["group"])
                if group_out:
                    group_out(jobs[-1]["group"])

            split_x(0)
            for b in range(2):
                normalise(pairs_even(b == 0), 8 * b)
                for u in range(4 * b, 4 * b + 4):
                    split_y(y_made, u + 1, wide(u), 2 * u, 2)
            if stop < 1:
                return
            pool.wait_ge(used, EV_OUT)
            pool.dma_start(extra[:, :], a["extra"][1]).then_inc(extra_in, 16)
            split_x(1)
            if stop < 2:
                return
            for b in range(8):
                pool.wait_ge(r_hi, b + 1)
                pool.tensor_tensor(y_lo[:, 2 * b:2 * b + 2, :], oyT[:, 2 * b:2 * b + 2, :],
                                   y_hi[:, 2 * b:2 * b + 2, :].bitcast(F32), ALU.subtract).then_inc(r_lo, 1)
            pool.wait_ge(used, OD_OUT + 8)
            pool.dma_start(view(6144, (D,)), a["rows_final"]).then_inc(final_in, 16)
            load_rows(2)
            split_x(2)
            token_h(2)
            for l in range(DEPTH):
                if stop < 3 + 4 * l:
                    return
                pool.wait_ge(n_lo, 4 * (3 + 2 * l))
                pool.wait_ge(h_done, 1 + 2 * l)
                pool.memset(cz[:, :, 0:2], 0.0).then_inc(z_pad, 1)
                pool.dma_start(w2[:, :, :, :], a["w2"][l]).then_inc(w2_in, 16)
                pool.wait_ge(xc_hi_done, l + 1)
                pool.tensor_tensor(xc_lo, xc, xc_hi.bitcast(F32), ALU.subtract).then_inc(xc_split, 1)
                for j in range(2):
                    s = L_IN[l] + 9 + j
                    split_y(g_free[s % 3], g_nth[s] + 1, wide(j), 4 + 2 * j, 2)
                normalise(pairs_sparse(), A_L[l],
                          lambda g: split_y(y_made, 8 + 4 * l + g + 1, narrow(g), g, 1))
                if stop < 4 + 4 * l:
                    return
                pool.wait_ge(used, L_WO[l] + 4)
                load_rows(3 + 2 * l)
                split_x(3 + 2 * l)
                token_h(3 + 2 * l)
                if stop < 5 + 4 * l:
                    return
                if l == 0:
                    for m in range(FT):
                        s = FFN_IN + m
                        split_y(g_free[s % 3], g_nth[s] + 1, narrow(m), m, 1)
                    pool.wait_ge(used, FFN_DOWN + 11)
                    load_rows(4)
                    split_x(4)
                    token_h(4)
                else:
                    pool.dma_start(upto[:, :, :], a["extra"][0][:, E_CUM:E_CUM + NT * S]
                                   .rearrange("p (a b) -> p a b", a=NT)).then_inc(upto_in, 16)

                    pool.wait_ge(h_done, 4)
                    load_rows(6)
                    token_h(6)

        @block.tensor
        def _(pe):
            def parts_mm(ps, lhs, rhs, start, stop):
                (lh, ll), (rh, rl) = lhs, rhs
                pe.matmul(ps, lh, rh, start=start, stop=False, skip_group_check=True)
                pe.matmul(ps, lh, rl, start=False, stop=False, skip_group_check=True)
                return pe.matmul(ps, ll, rh, start=False, stop=stop, skip_group_check=True)

            def mm32(ps, lhs, rhs, start=True, stop=True):
                return pe.matmul(ps, lhs, rhs, start=start, stop=stop, skip_group_check=True)

            def turned(ps, src):
                return pe.transpose(ps, src, ident)

            def pick(pair, f):
                return [f(t) for t in pair]

            def weights(s, shape):
                kw = dict(zip("kc", shape))
                return pick((w_hi[s % RING], w_lo[s % RING]), lambda t: t[:, :].rearrange("p (k c) -> p k c", **kw))

            def rows_slot(s, turn, slot, uses, src=from_x):
                pe.wait_ge(lo_done, slot + 1)
                if g_nth[s] > 0:
                    pe.wait_ge(g_free[s % 3], uses)
                w = weights(s, (KD, S))
                for m in range(2):
                    for k in range(KD):
                        mm = parts_mm(g_ps[s % 3][:, m * S:(m + 1) * S],
                                      pick(w, lambda t: t[:, k, m * P:(m + 1) * P]),
                                      pick(src, lambda t: t[:, k, :]), k == 0, k == KD - 1)
                mm.then_inc(used, 1)

            def token_mm(s, ps, src, k0, first, last):
                w = weights(s, (KD, S))
                for t in range(NT):
                    for k in range(KD):
                        mm = parts_mm(ps[:, t * S:(t + 1) * S], pick(src, lambda u: u[:, k0 + k, t * P:(t + 1) * P]),
                                      pick(w, lambda u: u[:, k, :]), first and k == 0 and t == 0, last and k == KD - 1)
                return mm

            def token_slot(s, turn, slot, uses):
                pe.wait_ge(lo_done, slot + 1)
                if g_nth[s] > 0:
                    pe.wait_ge(g_free[s % 3], uses)
                token_mm(s, g_ps[s % 3], from_x, 0, True, True).then_inc(used, 1)

            def out_slots(s0, halves, ready):
                for c in range(4):
                    for h in range(halves):
                        s = s0 + halves * c + h
                        pe.wait_ge(lo_done, s + 1)
                        if c == 0:
                            pe.wait_ge(*ready[h])
                        token_mm(s, a_ps[c], from_y, KD * h, h == 0, h == halves - 1).then_inc(used, 1)

            def transposed_norm(i):
                for b in range(4):
                    for j in range(2):
                        for t in range(NT):
                            if b == 0 and j == 0:
                                pe.wait_ge(n_z, 2 * i + t + 1)
                            k = 2 * b + j
                            tr = turned(a_ps[b][:, j * S + t * P:j * S + (t + 1) * P], z[:, t, k * P:(k + 1) * P])
                    tr.then_inc(n_tr, 1)
                pe.wait_ge(n_lo, 4 * (i + 1))

            def narrow_product(at, n):
                for t in range(NT):
                    for k in range(KD):
                        mm = parts_mm(a_ps[0][:, t * 32:t * 32 + n], pick(from_x, lambda u: u[:, k, t * P:(t + 1) * P]),
                                      pick((small_hi, small_lo), lambda u: u[:, k, at:at + n]),
                                      k == 0 and t == 0, k == KD - 1)
                mm.then_inc(narrow_full, 1)

            def attention(jobs, a0, outs_read):
                def scores(i, jb):
                    n = a0 + i
                    if n >= 1:
                        pe.wait_ge(mx_done, 2 * n)
                    for t, (at, keys) in enumerate(spans(jb)):
                        for h in range(2):
                            mm = mm32(a_ps[h][:, at:at + keys], jb["q"][h][:, t * P:(t + 1) * P],
                                      jb["k"][h][:, 0:keys], stop=jb["fox"] is None)
                        if jb["fox"] is not None:
                            for h in range(2):
                                col = C_ID + 64 * h + jb["fox"] + h
                                mm = mm32(a_ps[h][:, at:at + keys],
                                          const[64 * h:64 * h + 64, col:col + 1].to_broadcast([64, P]),
                                          c8[64 * h:64 * h + 64, 0:keys], start=False)
                    mm.then_inc(sc_full, 1)

                def turn(i, jb):
                    for h in range(2):
                        n = 2 * (a0 + i) + h
                        pe.wait_ge(pn_done, n + 1)
                        if a0 + i >= 1:
                            pe.wait_ge(pt_done[h], a0 + i)
                        ps, pr = a_ps[2 + h], prob[:, n % 4, :]
                        if jb["mask"] == "cmp":
                            for t in range(NT):
                                tr = turned(ps[0:NCMP, t * P:(t + 1) * P], pr[:, t * NCMP:(t + 1) * NCMP])
                        else:
                            for c in range(3):
                                tr = turned(ps[:, c * P:(c + 1) * P], pr[:, c * P:(c + 1) * P])
                        tr.then_inc(tr_done, 1)

                def values(i, jb):
                    for h in range(2):
                        pe.wait_ge(pt_done[h], a0 + i + 1)
                    if jb["first"] and jb["group"] >= 1:
                        pe.wait_ge(*outs_read(jb["group"] - 1))
                    for t in range(len(jb["v"][0])):
                        for h in range(2):
                            out_ = o_ps[64 * h:64 * h + 64, t * P:S]
                            if jb["mask"] == "cmp":
                                mm = mm32(out_, jb["v"][h][0], probT[0:NCMP, h, 0:S], False, jb["last"])
                            else:
                                mm = mm32(out_, jb["v"][h][t], probT[:, h, t * S:S + t * P],
                                          jb["first"] and t == 0, jb["last"] and t == 1)
                    mm.then_inc(pv_done, 1)

                for i in range(len(jobs) + 2):
                    if i < len(jobs):
                        scores(i, jobs[i])
                    if i >= 2:
                        values(i - 2, jobs[i - 2])
                    if 1 <= i <= len(jobs):
                        turn(i - 1, jobs[i - 1])

            pe.wait_ge(const_in, 16)
            pe.wait_ge(z_pad, 1)
            transposed_norm(0)
            pe.wait_ge(small_done, 1)
            narrow_product(0, HF)
            pe.wait_ge(extra_in, 16)
            pe.wait_ge(f_log, 1)
            for t in range(NT):
                mm = mm32(a_ps[1][0:HF, 0:S], tiny[:, 160 + HF * t:160 + HF * (t + 1)],
                          extra[:, E_CUM + t * S:E_CUM + (t + 1) * S], t == 0, t == 1)
            mm.then_inc(f_cum, 1)
            pe.wait_ge(f_c8, 1)
            for b in range(2):
                for s in range(EV_QK[b], EV_QK[b] + 8):
                    rows_slot(s, 0, s, g_nth[s])
                for s in range(EV_V[b], EV_V[b] + 4):
                    token_slot(s, 0, s, g_nth[s])
                for s in range(EV_V[b] + 1, EV_V[b] + 4):
                    pe.wait_ge(g_free[s % 3], g_nth[s] + 1)
                attention(pairs_even(b == 0), 8 * b, lambda g: (o_free, 8 * b + g + 1))
                for s in range(EV_G[b], EV_G[b] + 4):
                    rows_slot(s, 0, s, g_nth[s])
            for h in range(2):
                pe.wait_ge(pt_done[h], 16)
            out_slots(EV_OUT, 2, ((y_split, 4), (y_split, 8)))
            if stop < 1:
                return

            transposed_norm(1)
            run(pe, OD_QK, 8, rows_slot)
            run(pe, OD_V, 8, token_slot)
            for s in range(OD_V + 5, OD_V + 8):
                pe.wait_ge(g_free[s % 3], g_nth[s] + 1)
            for h in range(RH):
                if h:
                    pe.wait_ge(r_dec, h)
                for half in range(2):
                    mm32(a_ps[0][:, 0:S], rk[:, h, half, 0:P], rq[:, h, half, :], half == 0, half == 1)
                for half in range(2):
                    mm = mm32(a_ps[0][:, S:S + P], rk[:, h, half, P:S], rq[:, h, half, P:S], half == 0, half == 1)
                mm.then_inc(r_sc, 1)
                pe.wait_ge(r_dec, h + 1)
                if h:
                    pe.wait_ge(r_norm, h)
                sT, hv = prob[:, h % 2, :], slice(h * RV, (h + 1) * RV)
                mm32(a_ps[1][:, :], sT[:, 0:P], rv[:, 0, hv])
                mm32(a_ps[2][:, :], sT[:, P:S], rv[:, 0, hv], True, False)
                mm32(a_ps[2][:, :], sT[:, S:S + P], rv[:, 1, hv], False, True).then_inc(r_out, 1)
            run(pe, OD_G, 8, token_slot)
            for b in range(8):
                pe.wait_ge(r_y, b + 1)
                if b >= 4:
                    pe.wait_ge(r_ev, b - 3)
                for j in range(2):
                    for t in range(NT):
                        k = 2 * b + j
                        tr = turned(a_ps[b % 4][:, j * S + t * P:j * S + (t + 1) * P], rv[:, t, k * P:(k + 1) * P])
                tr.then_inc(r_tr, 1)
            pe.wait_ge(r_ev, 8)
            out_slots(OD_OUT, 2, ((r_lo, 4), (r_lo, 8)))
            if stop < 2:
                return

            def feed_forward(s0):
                for m in range(FT):
                    rows_slot(s0 + m, 0, s0 + m, g_nth[s0 + m])
                for c in range(FT // 2):
                    s = s0 + FT + c
                    pe.wait_ge(lo_done, s + 1)
                    pe.wait_ge(y_split, Y_FFN + 2 * c + 2)
                    w = weights(s, (2, D))
                    for k in range(2):
                        for t in range(NT):
                            for n in range(2):
                                mm = parts_mm(a_ps[2 * t + n][:, :],
                                              pick(from_y, lambda u: u[:, 2 * c + k, t * P:(t + 1) * P]),
                                              pick(w, lambda u: u[:, k, n * 512:(n + 1) * 512]), c == 0 and k == 0,
                                              c == FT // 2 - 1 and k == 1)
                    mm.then_inc(used, 1)

            transposed_norm(2)
            if stop < 3:
                return
            for l in range(DEPTH):
                s0 = L_IN[l]
                if l:
                    transposed_norm(4)
                narrow_product(HF + 24 * l, 24)
                for s in range(s0, s0 + 11):
                    (token_slot if s == s0 + 4 else rows_slot)(s, 0, s, g_nth[s])
                pe.wait_ge(xc_split, l + 1)
                for kind in range(2):
                    for h in range(2):
                        s = L_W1[l] + 2 * kind + h
                        pe.wait_ge(lo_done, s + 1)
                        w = weights(s, (KD, S))
                        for m in range(2):
                            for k in range(KD):
                                mm = parts_mm(o_ps[:, (2 * kind + m) * 32:(2 * kind + m) * 32 + 30],
                                              pick(w, lambda t: t[:, k, m * P:(m + 1) * P]),
                                              pick((xc_hi, xc_lo), lambda t: t[:, kind, KD * h + k, :]),
                                              kind == 0 and h == 0 and m == 0 and k == 0, h == 1 and k == KD - 1)
                        mm.then_inc(used, 1)
                pe.wait_ge(w2_in, 16 * (l + 1))
                pe.wait_ge(hid_done, l + 1)
                for m in range(2):
                    mm32(a_ps[1][:, 0:30], w2[:, 0, m, :], hid[:, 0, m, :], m == 0, m == 1)
                for g in range(NKV):
                    for m in range(2):
                        mm = mm32(a_ps[2][0:NCMP, g * HD:(g + 1) * HD], hid[:, 1, m, g * NCMP:(g + 1) * NCMP],
                                  w2[:, 1, m, 0:HD], m == 0, m == 1)
                mm.then_inc(kv_full, 1)
                pe.wait_ge(kc_done, l + 1)
                pe.wait_ge(vc_done, l + 1)
                pe.wait_ge(gates_done, l + 1)
                attention(pairs_sparse(), A_L[l], lambda g: (y_made, 8 + 4 * l + g + 1))
                for h in range(2):
                    pe.wait_ge(pt_done[h], A_L[l] + 12)
                out_slots(L_WO[l], 1, ((y_split, Y_L[l] + 6),))
                if stop < 4 + 4 * l:
                    return
                transposed_norm(3 + 2 * l)
                if stop < 5 + 4 * l:
                    return
                if l == 0:
                    feed_forward(FFN_IN)
                    if stop < 6:
                        return
            narrow_product(HF + 48, NE)
            on = [tiny[:, 16 + NE * t:16 + NE * (t + 1)] for t in range(NT)]
            pe.wait_ge(upto_in, 16)
            pe.wait_ge(m_on, 1)
            for t in range(NT):
                for u in range(t + 1):
                    mm32(a_ps[1][:, 16 * t:16 * t + NE], upto[:, u, t * P:(t + 1) * P], on[u], u == 0, u == t)
            for u in range(NT):
                mm = mm32(a_ps[1][0:1, 32:32 + NE], upto[:, u, S - 1:S], on[u], u == 0, u == NT - 1)
            mm.then_inc(m_rank, 1)

            def gather(q):
                for k in (0, 1):
                    for t in range(NT):
                        mm = mm32(o_ps[:, k * S:(k + 1) * S], x[:, t, (2 * q + k) * P:(2 * q + k + 1) * P],
                                  sel[:, t, :, :].rearrange("p e r -> p (e r)"), t == 0, t == NT - 1)
                mm.then_inc(m_x, 1)

            pe.wait_ge(m_sel, 8)
            pe.wait_ge(h_done, 4)
            for q in range(4):
                if q:
                    pe.wait_ge(m_xlo, q)
                gather(q)

            def experts(i, last):
                pe.wait_ge(m_xlo, 4 + 4 * i)
                for e in range(2):
                    for t in range(NT):
                        tr = turned(o_ps[:, e * S + t * P:e * S + (t + 1) * P], sel_g[:, t, e, :])
                tr.then_inc(m_tr, 1)

                def turn_hidden(c):
                    if c == 0:
                        pe.wait_ge(m_acc, 1 + 4 * i)
                    if c >= 2:
                        pe.wait_ge(m_y, c - 1 + FT // 2 * i)
                    for m in (2 * c, 2 * c + 1):
                        j = (MOE + m) % 3
                        pe.wait_ge(g_free[j], g_nth[MOE + m] + 1 + pair_g[j] * i)
                        tr = turned(a_ps[2 + c % 2][:, (m % 2) * P:(m % 2 + 1) * P], hidden_at(m))
                    tr.then_inc(m_ytr, 1)

                for m in range(FT):
                    s, e = MOE + m, m // 11
                    pe.wait_ge(lo_done, s + 1 + 33 * i)
                    pe.wait_ge(g_free[s % 3], g_nth[s] + pair_g[s % 3] * i)
                    w = weights(s, (KD, S))
                    for k in range(KD):
                        mm = parts_mm(g_ps[s % 3][:, 0:S], pick(from_x, lambda u: u[:, k, e * P:(e + 1) * P]),
                                      pick(w, lambda u: u[:, k, :]), k == 0, k == KD - 1)
                    mm.then_inc(used, 1)
                    if m % 2 and m >= 3:
                        turn_hidden((m - 3) // 2)
                for c in range(FT // 2):
                    s = MOE + FT + c
                    pe.wait_ge(lo_done, s + 1 + 33 * i)
                    pe.wait_ge(m_y, c + 1 + FT // 2 * i)
                    w = weights(s, (2, D))
                    for k in range(2):
                        m = 2 * c + k
                        for n in range(2):
                            mm = parts_mm(a_ps[2 * (m // 11) + n][:, :], pick(from_y, lambda u: u[:, m, 0:P]),
                                          pick(w, lambda u: u[:, k, n * 512:(n + 1) * 512]), m % 11 == 0, m % 11 == 10)
                    mm.then_inc(used, 1)
                    if c == 0:
                        turn_hidden(FT // 2 - 1)
                    if c in GATHER and not last:
                        q = GATHER.index(c)
                        if q == 0:
                            pe.wait_ge(m_sel, 16 + 8 * i)
                            pe.wait_ge(m_back, 1 + i)
                        else:
                            pe.wait_ge(m_xlo, 4 + q + 4 * i)
                        gather(q)
                pe.wait_ge(m_back, 1 + i)
                pe.wait_ge(m_osb, 4 + 4 * i)
                for t in range(NT):
                    for n in range(2):
                        for e in range(2):
                            mm = mm32(a_ps[2 * t + n][:, :], back[:, e, t * P:(t + 1) * P],
                                      o_sb[:, e, n * 512:(n + 1) * 512], e == 0, e == 1)
                mm.then_inc(m_sct, 1)

            before = loops_of(pe)
            with pe.Fori(0, before) as i:
                experts(i, False)
            experts(before, True)

        @block.scalar
        def _(act):
            own = Ticks(act, act_own)

            def split_hi(s, turn, slot):
                if s >= N_SLOTS:
                    return
                act.wait_ge(raw_in[s % RING], 16 * (s // RING + 1) + 16 * turn)
                if s >= RING:
                    act.wait_ge(used, slot - RING + 1)
                act.activation(w_hi[s % RING][:, :], raw[s % RING][:, :], ACT.Copy).then_inc(hi_done, 1)

            def ahead(s, turn=0):
                split_hi(s + RING, turn, s + RING * (1 + turn))

            def copy_slot(dst):
                def body(s, turn, slot, uses):
                    act.wait_ge(used, slot + 1)
                    src = g_ps[s % 3][:, :].rearrange("p (a b) -> p a b", a=2)
                    act.activation(dst(s, turn), src, ACT.Copy).then_inc(g_free[s % 3], 1)
                    ahead(s, turn)
                return body

            def root(count, done):
                act.wait_ge(n_var, count)
                act.activation(tiny[:, 226:228], tiny[:, 224:226], ACT.Sqrt).then_inc(done, 1)

            def hi_x(i):
                for b in range(4):
                    act.wait_ge(n_ev, 4 * i + b + 1)
                    act.activation(x_hi[:, 2 * b:2 * b + 2, :], xT[:, 2 * b:2 * b + 2, :], ACT.Copy).then_inc(n_hi, 1)

            def attention(jobs, a0):
                for i in range(len(jobs) + 1):
                    for h in range(2 if i < len(jobs) else 0):
                        n = 2 * (a0 + i) + h
                        act.wait_ge(mx_done, n + 1)
                        for t, (at, keys) in enumerate(spans(jobs[i])):
                            pr = prob[:, n % 4, at:at + keys]
                            ins = act.activation(pr, pr, ACT.Exp, bias=stat[:, n % 4, t:t + 1], scale=-1.0,
                                                 accum_out=stat[:, n % 4, 2 + t:3 + t])
                        ins.then_inc(ex_done, 1)
                    if i >= 1:
                        m = a0 + i - 1
                        act.wait_ge(tr_done, 2 * m + 2)
                        if m >= 1:
                            act.wait_ge(pv_done, m)
                        p, w = (NCMP, S) if jobs[i - 1]["mask"] == "cmp" else (P, 384)
                        act.activation(probT[0:p, 1, 0:w], a_ps[3][0:p, 0:w], ACT.Copy).then_inc(pt_done[1], 1)

            for s in range(RING):
                split_hi(s, 0, s)
            act.wait_ge(small_in, 16)
            act.activation(small_hi[:, :, :], small_raw, ACT.Copy).then_inc(small_hi_done, 1)
            root(1, n_sqrt)
            hi_x(0)
            act.wait_ge(f_in, 1)
            act.activation(tiny[:, 96:128], tiny[:, 64:96], ACT.Exp, scale=-1.0).then_inc(f_exp, 1)
            act.wait_ge(f_ln, 1)
            act.activation(tiny[:, 128:160], tiny[:, 96:128], ACT.Ln).then_inc(f_exp, 1)
            act.wait_ge(f_cum, 1)
            act.wait_ge(z_pad, 1)
            for b in (0, 64):
                ins = act.activation(c8[b:b + HF, :], a_ps[1][0:HF, 0:S], ACT.Copy, scale=-1.0 / SCALE)
            ins.then_inc(f_c8, 1)
            act.wait_ge(n_lo, 4)
            for b in range(2):
                for s in range(EV_QK[b], EV_QK[b] + 8):
                    m = s - EV_QK[b]
                    copy_slot(lambda s, t: (qT if m < 4 else kT)[:, 2 * (m % 4):2 * (m % 4) + 2, :])(s, 0, s, 0)
                for s in range(EV_V[b], EV_V[b] + 4):
                    m = s - EV_V[b]
                    copy_slot(lambda s, t: v[:, :, m * S:(m + 1) * S])(s, 0, s, 0)
                attention(pairs_even(b == 0), 8 * b)
                for s in range(EV_G[b], EV_G[b] + 4):
                    u = 4 * b + s - EV_G[b]
                    act.wait_ge(used, s + 1)
                    if u >= 3:
                        act.wait_ge(y_made, u - 2)
                    act.activation(gate_view(s), g_ps[s % 3][:, :], ACT.Silu).then_inc(g_free[s % 3], 1)
                    ahead(s)
            for s in range(EV_OUT, EV_OUT + 8):
                ahead(s)
            if stop < 1:
                return

            root(2, n_sqrt)
            hi_x(1)
            act.wait_ge(n_lo, 8)
            for s0, dst in ((OD_QK, None), (OD_V, lambda m, t: rv[:, :, m * S:(m + 1) * S])):
                for s in range(s0, s0 + 8):
                    if dst is None:
                        ahead(s)
                    else:
                        copy_slot(lambda s, t: dst(s - s0, t))(s, 0, s, 0)
            for h in range(RH):
                act.wait_ge(r_var, h + 1)
                act.activation(tiny[:, 226:228], tiny[:, 224:226], ACT.Sqrt).then_inc(r_sqrt, 1)
            for s in range(OD_G, OD_G + 8):
                u = s - OD_G
                act.wait_ge(used, s + 1)
                if u >= 3:
                    act.wait_ge(r_y, u - 2)
                act.activation(gate_view(s), g_ps[s % 3][:, :], ACT.Silu).then_inc(g_free[s % 3], 1)
                ahead(s)
            for b in range(8):
                act.wait_ge(r_tr, b + 1)
                act.activation(oyT[:, 2 * b:2 * b + 2, :], a_ps[b % 4][:, :].rearrange("p (a b) -> p a b", a=2),
                               ACT.Copy).then_inc(r_ev, 1)
            for s in range(OD_OUT, OD_OUT + 8):
                ahead(s)
            if stop < 2:
                return

            root(3, n_sqrt)
            root(4, n_sqrt)
            hi_x(2)
            if stop < 3:
                return
            for l in range(DEPTH):
                s0 = L_IN[l]
                if l:
                    root(6, n_sqrt)
                    hi_x(4)
                act.wait_ge(n_lo, 4 * (3 + 2 * l))
                act.wait_ge(h_done, 1 + 2 * l)
                act.wait_ge(narrow_full, 2 + l)
                act.activation(gates[:, :, :], a_ps[0][:, 0:64].rearrange("p (a b) -> p a b", a=2)[:, :, 0:24],
                               ACT.Sigmoid).then_inc(gates_done, 1)
                for s in range(s0, s0 + 11):
                    m = s - s0
                    if m < 2:
                        copy_slot(lambda s, t: sq[:, 2 * m:2 * m + 2, :])(s, 0, s, 0)
                    elif m == 3:
                        act.wait_ge(used, s + 1)
                        for g in range(NKV):
                            for d in range(2):
                                ins = act.activation(skd[64 * d:64 * d + 64, :, g, :],
                                                     g_ps[s % 3][64 * g:64 * g + 64, :].rearrange("p (a b) -> p a b", a=2),
                                                     ACT.Copy)
                        ins.then_inc(g_free[s % 3], 1)
                        ahead(s)
                    elif m == 4:
                        copy_slot(lambda s, t: sv[:, :, :, :].rearrange("p t b d -> p t (b d)"))(s, 0, s, 0)
                        act.wait_ge(xc_made, l + 1)
                        act.activation(xc_hi, xc, ACT.Copy).then_inc(xc_hi_done, 1)
                    elif m in (5, 6):
                        copy_slot(lambda s, t: cu[:, 2 * m - 10:2 * m - 8, :])(s, 0, s, 0)
                    else:
                        ahead(s)
                for s in range(L_W1[l], L_W1[l] + 4):
                    ahead(s)
                act.wait_ge(used, L_W1[l] + 4)
                for kind in range(2):
                    for m in range(2):
                        b1 = V_B1 + 4 * l + 2 * kind + m
                        ins = act.activation(hid[:, kind, m, :], o_ps[:, (2 * kind + m) * 32:(2 * kind + m) * 32 + 30],
                                             ACT.Gelu_apprx_tanh, bias=vec[:, b1:b1 + 1])
                ins.then_inc(hid_done, 1)
                attention(pairs_sparse(), A_L[l])
                for s in range(L_WO[l], L_WO[l] + 4):
                    ahead(s)
                if stop < 4 + 4 * l:
                    return
                root(5 + 2 * l, n_sqrt)
                hi_x(3 + 2 * l)
                if stop < 5 + 4 * l:
                    return

                def hidden(s, slot):
                    act.wait_ge(used, slot + 1)
                    act.activation(gate_view(s)[:, 0:S], g_ps[s % 3][:, 0:S], ACT.Silu).then_inc(gate_done, 1)

                if l == 0:
                    for m in range(FT):
                        hidden(FFN_IN + m, FFN_IN + m)
                        ahead(FFN_IN + m)
                    for s in range(FFN_DOWN, FFN_DOWN + 11):
                        ahead(s)
                    if stop < 6:
                        return
                else:
                    act.wait_ge(m_d, 1)
                    act.activation(tiny[:, 100:102], tiny[:, 98:100], ACT.Exp).then_inc(m_exp, 1)
                    def next_x(q, count):
                        act.wait_ge(m_x, count)
                        act.activation(x_hi[:, 2 * q:2 * q + 2, :], o_ps[:, :].rearrange("p (a b) -> p a b", a=2),
                                       ACT.Copy).then_inc(m_xhi, 1)

                    for q in range(4):
                        next_x(q, q + 1)

                    def experts(i, last):
                        act.wait_ge(m_tr, 1 + i)
                        act.activation(back[:, :, :], o_ps[:, :].rearrange("p (a b) -> p a b", a=2), ACT.Copy).then_inc(m_back, 1)

                        def y_high(c):
                            act.wait_ge(m_ytr, c + 1 + FT // 2 * i)
                            act.activation(y_hi[:, 2 * c:2 * c + 2, 0:P],
                                           a_ps[2 + c % 2][:, 0:S].rearrange("p (a b) -> p a b", a=2), ACT.Copy).then_inc(m_yhi, 1)

                        for m in range(FT):
                            s = MOE + m
                            if m % 2 == 0 and m >= 4:
                                y_high((m - 4) // 2)
                            act.wait_ge(used, s + 1 + 33 * i)
                            act.activation(gate_view(s)[:, 0:P], g_ps[s % 3][:, 0:P], ACT.Silu).then_inc(gate_done, 1)
                            ahead(s, 11 * i)
                        for c in range(11):
                            if c < 2:
                                y_high(9 + c)
                            if not (last and c >= 8):
                                ahead(MOE + FT + c, 11 * i)
                            if c in GATHER and not last:
                                q = GATHER.index(c)
                                next_x(q, 5 + q + 4 * i)
                            if c in (6, 10):
                                e = c // 10
                                act.wait_ge(used, MOE + FT + (6 if e == 0 else 11) + 33 * i)
                                for n in range(2):
                                    act.activation(o_sb[:, e, n * 512:(n + 1) * 512], a_ps[2 * e + n][:, :],
                                                   ACT.Copy).then_inc(m_osb, 1)

                    before = loops_of(act)
                    with act.Fori(0, before) as i:
                        experts(i, False)
                    experts(before, True)
            root(8, n_sqrt)

        @block.vector
        def _(dve):
            own = Ticks(dve, dve_own)

            def split_lo(s, turn, slot):
                if s >= N_SLOTS:
                    return
                dve.wait_ge(hi_done, slot + 1)
                if s >= RING:
                    dve.wait_ge(used, slot - RING + 1)
                dve.tensor_tensor(w_lo[s % RING][:, :], raw[s % RING][:, :], w_hi[s % RING][:, :].bitcast(F32),
                                  ALU.subtract).then_inc(lo_done, 1)

            def ahead(s, turn=0):
                split_lo(s + RING, turn, s + RING * (1 + turn))

            def chain(*steps):
                for step in steps:
                    own(step())
                    own.sync()

            def inverse_root(sqrt_done, count):
                a_, r, y, t = (tiny[:, c:c + 2] for c in (224, 226, 228, 230))
                dve.wait_ge(sqrt_done, count)
                chain(lambda: dve.reciprocal(y, r),
                      lambda: dve.tensor_tensor(t, y, y, ALU.mult),
                      lambda: dve.tensor_tensor(t, t, a_, ALU.mult),
                      lambda: dve.tensor_scalar(t, t, -0.5, 1.5, ALU.mult, ALU.add),
                      lambda: dve.tensor_tensor(y, y, t, ALU.mult))
                return y

            def rms(count):
                for t in range(NT):
                    own(dve.tensor_tensor_reduce(z[:, t, :], x[:, t, :], x[:, t, :], 1.0, 0.0, ALU.mult, ALU.add,
                                                 tiny[:, 192 + t:193 + t]))
                own.sync()
                dve.tensor_scalar(tiny[:, 224:226], tiny[:, 192:194], 1.0 / D, EPS, ALU.mult, ALU.add).then_inc(n_var, 1)
                return inverse_root(n_sqrt, count)

            def moments(src, eps, done):
                stats = tiny[:, 200:224]
                for t in range(NT):
                    for c, piece in enumerate(src(t)):
                        own(dve.bn_stats(stats[:, 12 * t + 6 * c:12 * t + 6 * c + 6], piece))
                own.sync()
                for t in range(NT):
                    own(dve.bn_aggr(tiny[:, 192 + 2 * t:194 + 2 * t], stats[:, 12 * t:12 * t + 6 * len(src(t))]))
                own.sync()
                var = tiny[:, 192:196].rearrange("p (t two) -> p t two", two=2)[:, :, 1]
                dve.tensor_scalar(tiny[:, 224:226], var, eps, None, ALU.add).then_inc(done, 1)

            def layer_norm(count):
                moments(lambda t: [x[:, t, 0:512], x[:, t, 512:D]], LN_EPS, n_var)
                y = inverse_root(n_sqrt, count)
                for t in range(NT):
                    dve.tensor_scalar(z[:, t, :], x[:, t, :], tiny[:, 192 + 2 * t:193 + 2 * t], y[:, t:t + 1],
                                      ALU.subtract, ALU.mult).then_inc(n_z, 1)

            def gain_rows(i, gain, bias):
                for b in range(4):
                    dve.wait_ge(n_tr, 4 * i + b + 1)
                    for j in range(2):
                        k = 2 * b + j
                        ins = dve.tensor_scalar(xT[:, k, :], a_ps[b][:, j * S:(j + 1) * S], vec[:, gain + k:gain + k + 1],
                                                None if bias is None else vec[:, bias + k:bias + k + 1],
                                                ALU.mult, *(() if bias is None else (ALU.add,)))
                    ins.then_inc(n_ev, 1)

            def add_residual(s0, halves, scale):
                for s in range(s0, s0 + 4 * halves):
                    if (s - s0) % halves == halves - 1:
                        c = (s - s0) // halves
                        dve.wait_ge(used, s + 1)
                        xs = x[:, :, c * S:(c + 1) * S]
                        own(dve.scalar_tensor_tensor(xs, xs, scale, a_ps[c][:, :].rearrange("p (a b) -> p a b", a=2),
                                                     ALU.mult, ALU.add))
                    ahead(s)
                own.sync()

            def router():
                def t3(at):
                    return tiny[:, at:at + 2 * NE].rearrange("p (t e) -> p t e", e=NE)

                lg, on1, on2, eq, gate = t3(16), t3(32), t3(48), t3(64), t3(0)
                mx = [tiny[:, c:c + 2] for c in (92, 94)]
                rank = const[:, C_RANK:C_RANK + NE].unsqueeze(1).to_broadcast([P, NT, NE])

                def wide(c):
                    return c.unsqueeze(2).to_broadcast([P, NT, NE])

                def best(on, m):
                    r = tiny[:, 96:98]
                    chain(lambda: dve.tensor_reduce(m, lg, AX.X, ALU.max),
                          lambda: dve.tensor_tensor(eq, lg, wide(m), ALU.is_equal),
                          lambda: dve.tensor_tensor(eq, eq, rank, ALU.mult),
                          lambda: dve.tensor_reduce(r, eq, AX.X, ALU.max),
                          lambda: dve.tensor_tensor(on, eq, wide(r), ALU.is_equal))

                dve.wait_ge(narrow_full, 4)
                chain(lambda: dve.tensor_copy(lg, a_ps[0][:, 0:64].rearrange("p (a b) -> p a b", a=2)[:, :, 0:NE]))
                best(on1, mx[0])
                chain(lambda: dve.scalar_tensor_tensor(lg, on1, NEG, lg, ALU.mult, ALU.add))
                best(on2, mx[1])
                dve.tensor_tensor(tiny[:, 98:100], mx[1], mx[0], ALU.subtract).then_inc(m_d, 1)
                dve.tensor_tensor(lg, on1, on2, ALU.add).then_inc(m_on, 1)
                dve.wait_ge(m_exp, 1)
                w1_, w2_, den = tiny[:, 102:104], tiny[:, 104:106], tiny[:, 106:108]
                chain(lambda: dve.tensor_scalar(den, tiny[:, 100:102], 1.0, None, ALU.add),
                      lambda: dve.reciprocal(w1_, den),
                      lambda: dve.tensor_tensor(w2_, w1_, tiny[:, 100:102], ALU.mult),
                      lambda: dve.tensor_tensor(on1, on1, wide(w1_), ALU.mult),
                      lambda: dve.tensor_tensor(on2, on2, wide(w2_), ALU.mult))
                for half in range(2):
                    own(dve.tensor_tensor(ranks[:, 1, :, half * NE:(half + 1) * NE], on1, on2, ALU.add))
                dve.wait_ge(m_rank, 1)
                most = tiny[0:1, 110:111]
                chain(lambda: dve.tensor_tensor(gate, a_ps[1][:, 0:32].rearrange("p (a b) -> p a b", a=2)[:, :, 0:NE], lg, ALU.mult),
                      lambda: dve.tensor_scalar(ranks[:, 0, :, 0:NE], gate, -1.0, None, ALU.add),
                      lambda: dve.tensor_scalar(ranks[:, 0, :, NE:2 * NE], gate, -1.0 - P, None, ALU.add),
                      lambda: dve.tensor_reduce(most, a_ps[1][0:1, 32:32 + NE], AX.X, ALU.max),
                      lambda: dve.tensor_scalar(most, most, P + 0.5, float(PAIRS), ALU.is_gt, ALU.mult))
                dve.tensor_scalar(loops[0:1, 0:1], most, float(PAIRS - 1), None, ALU.add).then_inc(m_loops, 1)

            def select(at, count):
                dve.tensor_copy(ranks_now[:, :, :, :], ranks[:, :, :, at]).then_inc(m_now, 1)
                dve.wait_ge(m_now, 1 + count)
                iota = const[:, C_IOTA:C_IOTA + P]
                for t in range(NT):
                    for e in range(2):
                        r, g = (ranks_now[:, c, t, e:e + 1] for c in range(2))
                        dve.tensor_scalar(sel[:, t, e, :], iota, r, None, ALU.is_equal).then_inc(m_sel, 1)
                        dve.tensor_scalar(sel_g[:, t, e, :], iota, r, g, ALU.is_equal, ALU.mult).then_inc(m_sel, 1)

            def attention(jobs, a0, group_out):
                def largest(i, jb):
                    dve.wait_ge(sc_full, a0 + i + 1)
                    table = {"causal": const[:, C_CAUSAL:C_CAUSAL + 384], "dil": extra[:, E_DIL:E_DIL + 384],
                             "cmp": const[:, C_CMP:C_CMP + 2 * NCMP]}[jb["mask"]]
                    for h in range(2):
                        n = 2 * (a0 + i) + h
                        if n >= 4:
                            dve.wait_ge(tr_done, n - 3)
                        for t, (at, keys) in enumerate(spans(jb)):
                            ins = dve.tensor_tensor_reduce(prob[:, n % 4, at:at + keys], a_ps[h][:, at:at + keys],
                                                           table[:, at:at + keys], -SCALE, 3e38, ALU.add, ALU.min,
                                                           stat[:, n % 4, t:t + 1])
                        ins.then_inc(mx_done, 1)

                def inverse_sums(i, jb):
                    for h in range(2):
                        m = 2 * (a0 + i) + h
                        dve.wait_ge(ex_done, m + 1)
                        rs = stat[:, m % 4, 4:6]
                        if jb["gate"] is None:
                            dve.reciprocal(rs, stat[:, m % 4, 2:4]).then_inc(rc_done, 1)
                        else:
                            own(dve.reciprocal(rs, stat[:, m % 4, 2:4]))
                            own.sync()
                            dve.tensor_tensor(rs, rs, gates[:, :, jb["gate"] + h], ALU.mult).then_inc(rc_done, 1)

                def copy_even(i, jb):
                    m = a0 + i
                    dve.wait_ge(tr_done, 2 * m + 1)
                    if m >= 1:
                        dve.wait_ge(pv_done, m)
                    p, w = (NCMP, S) if jb["mask"] == "cmp" else (P, 384)
                    dve.tensor_copy(probT[0:p, 0, 0:w], a_ps[2][0:p, 0:w]).then_inc(pt_done[0], 1)

                for i in range(len(jobs) + 2):
                    if i < len(jobs):
                        largest(i, jobs[i])
                    if i >= 2 and jobs[i - 2]["last"]:
                        dve.wait_ge(pv_done, a0 + i - 1)
                        group_out(jobs[i - 2]["group"])
                    if i < len(jobs):
                        inverse_sums(i, jobs[i])
                    if 1 <= i <= len(jobs):
                        copy_even(i - 1, jobs[i - 1])

            def part_free(u):
                if u >= 2:
                    dve.wait_ge(y_split, u - 1)

            dve.wait_ge(small_hi_done, 1)
            dve.tensor_tensor(small_lo[:, :, :], small_raw, small_hi[:, :, :].bitcast(F32), ALU.subtract).then_inc(small_done, 1)
            dve.wait_ge(small_done, 1)
            dve.wait_ge(x_in, 16)
            y = rms(1)
            for t in range(NT):
                dve.tensor_scalar(z[:, t, :], x[:, t, :], y[:, t:t + 1], None, ALU.mult).then_inc(n_z, 1)
            dve.wait_ge(vec_in, 16)
            dve.wait_ge(const_in, 16)
            gain_rows(0, V_EVEN, None)
            for s in range(RING):
                split_lo(s, 0, s)
            f, u_, ab, e_, l_, lf = (tiny[:, c:c + 32] for c in (0, 32, 64, 96, 128, 160))
            dve.wait_ge(narrow_full, 1)
            for t in range(NT):
                own(dve.tensor_tensor(f[:, HF * t:HF * t + HF], a_ps[0][:, 32 * t:32 * t + HF], vec[:, V_BF:V_BF + HF], ALU.add))
            own.sync()
            chain(lambda: dve.tensor_scalar(ab, f, -1.0, None, ALU.mult),
                  lambda: dve.tensor_tensor(ab, ab, f, ALU.max))
            dve.tensor_scalar(u_, f, 0.0, None, ALU.min).then_inc(f_in, 1)
            dve.wait_ge(f_exp, 1)
            dve.tensor_scalar(e_, e_, 1.0, None, ALU.add).then_inc(f_ln, 1)
            dve.wait_ge(f_exp, 2)
            dve.tensor_tensor(lf, u_, l_, ALU.subtract).then_inc(f_log, 1)
            dve.wait_ge(extra_in, 16)
            for b in range(2):
                for s in range(EV_QK[b], EV_QK[b] + 12):
                    ahead(s)

                def to_oT(g):
                    dve.tensor_copy(oT[:, g, :], o_ps[:, 0:S]).then_inc(o_free, 1)

                attention(pairs_even(b == 0), 8 * b, to_oT)
                dve.wait_ge(o_free, 8 * (b + 1))
                for s in range(EV_G[b], EV_G[b] + 4):
                    u, m = 4 * b + s - EV_G[b], s - EV_G[b]
                    dve.wait_ge(g_free[s % 3], g_nth[s] + 1)
                    part_free(u)
                    dve.tensor_tensor(part[:, u % 2, :], oT[:, 2 * m:2 * m + 2, :].rearrange("p a b -> p (a b)"),
                                      gate_view(s), ALU.mult).then_inc(y_made, 1)
                    ahead(s)
            add_residual(EV_OUT, 2, 1.0)
            if stop < 1:
                return

            y = rms(2)
            for t in range(NT):
                dve.tensor_scalar(z[:, t, :], x[:, t, :], y[:, t:t + 1], None, ALU.mult).then_inc(n_z, 1)
            gain_rows(1, V_ODD, None)
            dve.wait_ge(extra_in, 32)
            dve.wait_ge(n_lo, 8)
            cos, sin = (extra[:, c:c + S].unsqueeze(1).to_broadcast([P, 2, S]) for c in (O_COS, O_SIN))
            for s in range(OD_QK, OD_QK + 8):
                m, j = s - OD_QK, s % 3
                dst = (rq if m < 4 else rk)[:, m % 4, :, :]
                ps = g_ps[j][:, :].rearrange("p (a b) -> p a b", a=2)
                cc, ss = (part[:, c, :].rearrange("p (a b) -> p a b", a=2) for c in range(2))
                dve.wait_ge(used, s + 1)
                own(dve.tensor_tensor(cc, ps, cos, ALU.mult))
                dve.tensor_tensor(ss, ps, sin, ALU.mult).then_inc(g_free[j], 1)
                own.sync()
                dve.wait_ge(g_free[j], g_nth[s] + 1)
                own(dve.tensor_tensor(dst[:, 0, :], cc[:, 0, :], ss[:, 1, :], ALU.subtract))
                own(dve.tensor_tensor(dst[:, 1, :], ss[:, 0, :], cc[:, 1, :], ALU.add))
                own.sync()
                ahead(s)
            for s in range(OD_V, OD_V + 8):
                ahead(s)
            for h in range(RH):
                dve.wait_ge(r_sc, h + 1)
                dve.tensor_tensor(prob[:, h % 2, :], a_ps[0][:, 0:384], extra[:, O_RET + 384 * h:O_RET + 384 * (h + 1)],
                                  ALU.mult).then_inc(r_dec, 1)
                dve.wait_ge(r_out, h + 1)
                moments(lambda t: [a_ps[1 + t][:, :]], EPS, r_var)
                y = inverse_root(r_sqrt, h + 1)
                for t in range(NT):
                    ins = dve.tensor_scalar(rv[:, t, h * RV:(h + 1) * RV], a_ps[1 + t][:, :],
                                            tiny[:, 192 + 2 * t:193 + 2 * t], y[:, t:t + 1], ALU.subtract, ALU.mult)
                ins.then_inc(r_norm, 1)
            dve.wait_ge(r_norm, RH)
            for s in range(OD_G, OD_G + 8):
                m = s - OD_G
                dve.wait_ge(g_free[s % 3], g_nth[s] + 1)
                dst = rv[:, :, m * S:(m + 1) * S]
                dve.tensor_tensor(dst, dst, gate_view(s).rearrange("p (a b) -> p a b", a=2), ALU.mult).then_inc(r_y, 1)
                ahead(s)
            for b in range(8):
                dve.wait_ge(r_ev, b + 1)
                dve.tensor_copy(y_hi[:, 2 * b:2 * b + 2, :], oyT[:, 2 * b:2 * b + 2, :]).then_inc(r_hi, 1)
            add_residual(OD_OUT, 2, 1.0)
            if stop < 2:
                return

            y = rms(3)
            dve.wait_ge(final_in, 16)
            for t in range(NT):
                own(dve.scalar_tensor_tensor(x[:, t, :], x[:, t, :], y[:, t:t + 1], view(6144, (D,)), ALU.mult, ALU.mult))
            own.sync()
            if stop < 2.5:
                return
            layer_norm(4)
            gain_rows(2, V_LN, V_LN + 8)
            if stop < 3:
                return
            for l in range(DEPTH):
                s0 = L_IN[l]
                if l:
                    layer_norm(6)
                    gain_rows(4, V_LN + 32, V_LN + 40)
                dve.wait_ge(gates_done, l + 1)
                for t in range(NT):
                    own(dve.tensor_scalar(gates[:, t, 0:NH], gates[:, t, 0:NH], const[:, C_ROW + t:C_ROW + t + 1],
                                          None, ALU.mult))
                dve.wait_ge(n_lo, 4 * (3 + 2 * l))
                dve.wait_ge(h_done, 1 + 2 * l)
                for s in range(s0, s0 + 11):
                    m, j = s - s0, s % 3
                    ps = g_ps[j][:, :].rearrange("p (a b) -> p a b", a=2)
                    if m == 2:
                        dve.wait_ge(used, s + 1)
                        for kind in range(2):
                            pos = V_POS + 32 * l + 16 * kind
                            for g in range(NKV):
                                for par in range(2):
                                    for half in range(2):
                                        src = ps[64 * g:64 * g + 64, kind, :].rearrange(
                                            "p (n r two) -> p r n two", two=2, r=8)[:, :, half:half + NCMP, par]
                                        to = slice(64 * par, 64 * par + 64)
                                        ins = dve.tensor_tensor(
                                            xc[to, kind, 8 * half:8 * half + 8, g * NCMP:(g + 1) * NCMP], src,
                                            vec[to, pos + 8 * half:pos + 8 * half + 8].unsqueeze(2)
                                            .to_broadcast([64, 8, NCMP]), ALU.add)
                                        if kind + g + par + half < 4:
                                            own(ins)
                        ins.then_inc(g_free[j], 1)
                        dve.wait_ge(g_free[j], g_nth[s] + 1)
                        dve.tensor_scalar(tiny[:, 250:251], tiny[:, 192:193], 0.0, None, ALU.mult).then_inc(xc_made, 1)
                    elif m in (7, 8):
                        k = 2 * (m - 7)
                        dve.wait_ge(used, s + 1)
                        dve.wait_ge(g_free[(s - 2) % 3], g_nth[s - 2] + 1)
                        dve.tensor_tensor(cz[:, k:k + 2, 2:2 + S], ps, cu[:, k:k + 2, :], ALU.mult).then_inc(g_free[j], 1)
                        dve.wait_ge(g_free[j], g_nth[s] + 1)
                    elif m in (9, 10):
                        k = 2 * (m - 9)
                        yp = part[:, m - 9, :].rearrange("p (a b) -> p a b", a=2)
                        part_free(Y_L[l] + m - 9)
                        dve.wait_ge(z_pad, 2 + l)
                        for tap in range(3):
                            for q in range(2):
                                w = vec[:, V_CONV + 12 * l + 4 * tap + k + q:V_CONV + 12 * l + 4 * tap + k + q + 1]
                                src = cz[:, k + q, tap:tap + S]
                                if tap == 0:
                                    own(dve.tensor_scalar(yp[:, q, :], src, w, None, ALU.mult))
                                else:
                                    own(dve.scalar_tensor_tensor(yp[:, q, :], src, w, yp[:, q, :], ALU.mult, ALU.add))
                            own.sync()
                        dve.wait_ge(used, s + 1)
                        dve.tensor_tensor(yp, yp, ps, ALU.mult).then_inc(g_free[j], 1)
                    ahead(s)
                for s in range(L_W1[l], L_W1[l] + 4):
                    ahead(s)
                dve.wait_ge(kv_full, l + 1)
                dve.tensor_scalar(kc2[:, :], a_ps[1][:, 0:30], vec[:, V_B2K + l:V_B2K + l + 1], None, ALU.add).then_inc(kc_done, 1)
                dve.tensor_tensor(vc2[:, :, :], a_ps[2][0:NCMP, 0:128].rearrange("p (a b) -> p a b", a=2),
                                  vec[0:NCMP, V_B2V + 64 * l:V_B2V + 64 * (l + 1)].unsqueeze(1).to_broadcast([NCMP, 2, HD]),
                                  ALU.add).then_inc(vc_done, 1)

                def to_part(g):
                    part_free(Y_L[l] + 2 + g)
                    dve.tensor_copy(part[:, g % 2, 0:S], o_ps[:, 0:S]).then_inc(y_made, 1)

                own.sync()
                attention(pairs_sparse(), A_L[l], to_part)
                add_residual(L_WO[l], 1, ALPHA)
                if stop < 4 + 4 * l:
                    return
                layer_norm(5 + 2 * l)
                gain_rows(3 + 2 * l, V_LN + 16 + 32 * l, V_LN + 24 + 32 * l)
                if stop < 5 + 4 * l:
                    return

                def hidden(s, u0, m, count):
                    j, yp = s % 3, part[:, m % 2, 0:S]
                    dve.wait_ge(gate_done, count)
                    dve.wait_ge(y_split, u0 - 1)
                    dve.tensor_tensor(yp, gate_view(s)[:, 0:S], g_ps[j][:, S:2 * S], ALU.mult).then_inc(g_free[j], 1)

                if l == 0:
                    for m in range(FT):
                        hidden(FFN_IN + m, Y_FFN + m, m, m + 1)
                        ahead(FFN_IN + m)
                    dve.wait_ge(h_done, 2)
                    for s in range(FFN_DOWN, FFN_DOWN + 11):
                        ahead(s)
                    dve.wait_ge(used, FFN_DOWN + 11)
                    for t in range(NT):
                        for n in range(2):
                            xs = x[:, t, n * 512:(n + 1) * 512]
                            own(dve.scalar_tensor_tensor(xs, xs, ALPHA, a_ps[2 * t + n][:, :], ALU.mult, ALU.add))
                    own.sync()
                    if stop < 6:
                        return
                    continue
                router()
                dve.memset(f_acc[:, :, :], 0.0).then_inc(m_acc, 1)
                select(slice(0, 2), 0)

                def next_x(q, count):
                    dve.wait_ge(m_xhi, count)
                    dve.tensor_tensor(x_lo[:, 2 * q:2 * q + 2, :], o_ps[:, :].rearrange("p (a b) -> p a b", a=2),
                                      x_hi[:, 2 * q:2 * q + 2, :].bitcast(F32), ALU.subtract).then_inc(m_xlo, 1)

                for q in range(4):
                    next_x(q, q + 1)

                def experts(i, last):
                    def y_low(c):
                        dve.wait_ge(m_yhi, c + 1 + FT // 2 * i)
                        dve.tensor_tensor(y_lo[:, 2 * c:2 * c + 2, 0:P],
                                          a_ps[2 + c % 2][:, 0:S].rearrange("p (a b) -> p a b", a=2),
                                          y_hi[:, 2 * c:2 * c + 2, 0:P].bitcast(F32), ALU.subtract).then_inc(m_y, 1)

                    for m in range(FT):
                        s = MOE + m
                        if m % 2 == 0 and m >= 4:
                            y_low((m - 4) // 2)
                        dve.wait_ge(gate_done, FT + m + 1 + FT * i)
                        if m >= 8:
                            dve.wait_ge(m_ytr, (m - 8) // 2 + 1 + FT // 2 * i)
                        dve.tensor_tensor(hidden_at(m), gate_view(s)[:, 0:P], g_ps[s % 3][:, P:2 * P],
                                          ALU.mult).then_inc(g_free[s % 3], 1)
                        ahead(s, 11 * i)
                    for c in range(11):
                        if c < 2:
                            y_low(9 + c)
                        if c == 0 and not last:
                            dve.wait_ge(m_tr, 1 + i)
                            select(bass.ds(2 * i + 2, 2), 1 + i)
                        if not (last and c >= 8):
                            ahead(MOE + FT + c, 11 * i)
                        if c in GATHER and not last:
                            q = GATHER.index(c)
                            next_x(q, 5 + q + 4 * i)
                    dve.wait_ge(m_sct, 1 + i)
                    dve.wait_ge(m_acc, 1 + 4 * i)
                    for t in range(NT):
                        for n in range(2):
                            fa = f_acc[:, t, n * 512:(n + 1) * 512]
                            dve.tensor_tensor(fa, fa, a_ps[2 * t + n][:, :], ALU.add).then_inc(m_acc, 1)

                before = loops_of(dve)
                with dve.Fori(0, before) as i:
                    experts(i, False)
                experts(before, True)
                dve.wait_ge(m_acc, 5 + 4 * before)
                for t in range(NT):
                    own(dve.scalar_tensor_tensor(x[:, t, :], x[:, t, :], ALPHA, f_acc[:, t, :], ALU.mult, ALU.add))
                own.sync()
            layer_norm(8)


def in_slots(w):
    n = w.shape[1] // S
    return w.reshape(KD, P, n, S).transpose(2, 1, 0, 3).reshape(n, P, SLOT)


def out_slots_of(w):
    h = w.shape[0] // D
    return w.reshape(h, KD, P, 4, S).transpose(3, 0, 2, 1, 4).reshape(4 * h, P, SLOT)


def ffn_slots(wg, wu, wd):
    gu = np.stack([wg.reshape(KD, P, FT, P), wu.reshape(KD, P, FT, P)], 3)
    return np.concatenate([gu.transpose(2, 1, 0, 3, 4).reshape(FT, P, SLOT),
                           wd.reshape(FT // 2, 2, P, D).transpose(0, 2, 1, 3).reshape(FT // 2, P, SLOT)])


def lay_out(i):
    i = {k: np.asarray(v, np.float32) if np.asarray(v).dtype != np.float32 else np.asarray(v) for k, v in i.items()}
    ev, od = i["even_w_in"][0], i["odd_w_in"][0]
    w = []
    for at in (0, 4096 + HF):
        w.append(in_slots(ev[:, at:at + 4096]))
    w.append(out_slots_of(i["even_w_out"][0]))
    qk = od[:, :2048].reshape(D, 8, P, 2).transpose(0, 1, 3, 2).reshape(D, 2048)
    w += [in_slots(np.ascontiguousarray(qk)), in_slots(od[:, 2048:]), out_slots_of(i["odd_w_out"][0])]
    small = [ev[:, 4096:4096 + HF]]
    for l in range(DEPTH):
        wi = i["w_in_2"][l]
        q, kc, vc, ks, vs, kw, vw, gt, u, bg, cg = np.split(wi, np.cumsum([512, 128, 128, 128, 128, 128, 128, 24, 512, 512]), 1)
        small.append(gt)
        w.append(in_slots(np.concatenate([q, kc, vc, ks, kw, vs, vw, u, cg, bg], 1)))
        for kind in range(2):
            w.append(i["cmp_w1_2"][l, kind].reshape(2, KD, P, S).transpose(0, 2, 1, 3).reshape(2, P, SLOT))
        w.append(out_slots_of(i["w_o_2"][l]))
        if l == 0:
            w.append(ffn_slots(i["ffn_wg_2"][0], i["ffn_wu_2"][0], i["ffn_wd_2"][0]))
        else:
            for e in range(0, NE, 2):
                wg, wu = (np.concatenate([i[k][0, e], i[k][0, e + 1]], 1) for k in ("moe_wg_2", "moe_wu_2"))
                w.append(ffn_slots(wg, wu, i["moe_wd_2"][0, e:e + 2].reshape(-1, D)))
    small.append(i["moe_router_2"][0])
    vec = np.zeros((P, N_VEC), np.float32)

    def tiles(a):
        return a.reshape(-1, P).T

    vec[:, V_EVEN:V_EVEN + 8], vec[:, V_ODD:V_ODD + 8] = tiles(i["even_norm"][0]), tiles(i["odd_norm"][0])
    norms = [("ln_in", None), ("ln1", 0), ("ln2", 0), ("ln1", 1), ("ln2", 1)]
    pick = [[i[f"{n}_{c}_2"] if l is None else i[f"{n}_{c}_2"][l] for c in "gb"] for n, l in norms]
    for j in range(4):
        for c in range(2):
            vec[:, V_LN + 16 * j + 8 * c:V_LN + 16 * j + 8 * c + 8] = tiles(pick[j][c])
    vec[:, V_BF:V_BF + HF] = i["even_b_f"][0][None]
    w2 = np.zeros((DEPTH, P, 2, 2, P), np.float32)
    for l in range(DEPTH):
        for kind in range(2):
            vec[:, V_POS + 32 * l + 16 * kind:V_POS + 32 * l + 16 * kind + 16] = tiles(i["cmp_pos_2"][l, kind])
            vec[:, V_B1 + 4 * l + 2 * kind:V_B1 + 4 * l + 2 * kind + 2] = tiles(i["cmp_b1_2"][l, kind])
            two = i["cmp_w2_2"][l, kind].reshape(2, P, HD).transpose(1, 0, 2)
            w2[l, :, kind, :, :HD] = two
            if kind == 0:
                w2[l, :, kind, :, HD:] = two
        vec[:, V_B2K + l] = np.tile(i["cmp_b2_2"][l, 0], 2)
        vec[:, V_B2V + 64 * l:V_B2V + 64 * (l + 1)] = i["cmp_b2_2"][l, 1][None]
        for tap in range(3):
            vec[:, V_CONV + 12 * l + 4 * tap:V_CONV + 12 * l + 4 * tap + 4] = tiles(i["conv_w_2"][l, tap])
    const, extra = shape_constants()
    return {
        "x": i["x"][0], "w": np.concatenate(w), "const": const, "extra": extra, "vec": vec, "w2": w2,
        "small": np.ascontiguousarray(np.concatenate(small, 1).reshape(KD, P, NSMALL).transpose(1, 0, 2)),
        "rows_final": np.ascontiguousarray(np.broadcast_to(i["final_norm"], (P, D))),
        "rows": np.ascontiguousarray(np.broadcast_to(np.array(pick)[:, :, None], (5, 2, P, D))),
    }


def kernel(**inputs):
    import concourse.bacc as bacc
    from concourse.bass_utils import run_bass_kernel_spmd

    arrays = lay_out(inputs)
    nc = bacc.Bacc("TRN2", target_bir_lowering=False, num_devices=1)
    aps = {k: nc.dram_tensor(k + "_dram", v.shape, F32, kind="ExternalInput").ap() for k, v in arrays.items()}
    out = nc.dram_tensor("out_dram", (1, S, D), F32, kind="ExternalOutput").ap()
    build(nc, aps, out)
    r = run_bass_kernel_spmd(nc, [{k + "_dram": v for k, v in arrays.items()}], core_ids=[0])
    return r.results[0]["out_dram"]
```

```python
from contextlib import ExitStack

import numpy as np

import concourse.bass as bass
from concourse import mybir

P = 128
S = 256
NT = S // P
D = 1024
KD = D // P
SLOT = 2048
RING = 3
HD = 64
AHEAD = 3
HF = 16
RH, RQK, RV = 4, 256, 512
NH, NKV = 8, 2
NCMP = 15
CB, CS = 32, 16
DEPTH = 2
FT = 22
NE = 8
PAIRS = NE // 2
NSMALL = 16 + 2 * 24 + NE
NEG = -1e30
SCALE = HD ** -0.5
ALPHA = (2 * DEPTH) ** 0.25
EPS, LN_EPS = 1e-6, 1e-5

F32 = mybir.dt.float32
F32R = mybir.dt.float32r
ALU = mybir.AluOpType
ACT = mybir.ActivationFunctionType
AX = mybir.AxisListType

EV_V, EV_G = (8, 20), (24, 28)
EV_OUT = 32
OD_QK, OD_V, OD_G, OD_OUT = 40, 48, 56, 64
L_IN = (72, 124)
I_KC, I_U, I_W1, I_C, I_B = 4, 5, 7, 11, 13
L_WO = (87, 139)
FFN_IN, FFN_DOWN = 91, 113
MOE = 143
N_SLOTS = MOE + PAIRS * 33

C_ID = 0
C_CAUSAL = C_ID + P
C_CMP = C_CAUSAL + 384
C_ROW = C_CMP + 2 * NCMP
C_RANK = C_ROW + 2
C_IOTA = C_RANK + NE
N_CONST = C_IOTA + P
E_DIL = 0
E_CUM = E_DIL + 384
O_RET = 0
O_COS = O_RET + RH * 384
O_SIN = O_COS + S
N_EXTRA = O_SIN + S

V_EVEN, V_ODD = 0, 8
V_LN = 16
V_BF = V_LN + 4 * 16
V_POS = V_BF + 16
V_B1 = V_POS + 64
V_B2K = V_B1 + 8
V_B2V = V_B2K + 2
V_CONV = V_B2V + 128
N_VEC = V_CONV + 24


def shape_constants():
    c = np.zeros((P, N_CONST), np.float32)
    even = np.zeros((P, N_EXTRA), np.float32)
    odd = np.zeros((P, N_EXTRA), np.float32)
    p = np.arange(P)
    c[:, C_ID:C_ID + P] = np.eye(P)
    t = np.concatenate([np.broadcast_to(p[:, None], (P, P)), np.broadcast_to(P + p[:, None], (P, S))], 1)
    k = np.concatenate([np.arange(P), np.arange(S)])[None, :]
    dist = t - k
    c[:, C_CAUSAL:C_CAUSAL + 384] = np.where(dist >= 0, 0.0, NEG)
    count = sum(((dist >= 0) & (dist % r == 0) & (dist <= w)).astype(np.float64)
                for w, r in ((128, 1), (512, 4), (2048, 16)))
    even[:, E_DIL:E_DIL + 384] = np.where(count > 0, np.log(np.maximum(count, 1)) / SCALE, NEG)
    ends = np.arange(NCMP) * CS + CB - 1
    for i in range(NT):
        seen = ends[None, :] <= (i * P + p)[:, None]
        c[:, C_CMP + i * NCMP:C_CMP + (i + 1) * NCMP] = np.where(seen, 0.0, NEG)
        c[:, C_ROW + i] = seen.any(1)
        even[:, E_CUM + i * S:E_CUM + (i + 1) * S] = (i * P + p)[:, None] <= np.arange(S)[None, :]
    tt = np.concatenate([np.arange(S), np.arange(P, S)])[None, :]
    kk = np.concatenate([np.broadcast_to(p[:, None], (P, S)), np.broadcast_to(P + p[:, None], (P, P))], 1)
    for h in range(RH):
        lg = np.log1p(-(2.0 ** (-5.0 - h)))
        decay = np.where(tt >= kk, np.exp(lg * np.maximum(tt - kk, 0)), 0.0)
        odd[:, O_RET + 384 * h:O_RET + 384 * (h + 1)] = decay * RQK ** -0.5
    inv = (1.0 / (10000.0 ** np.linspace(0.0, 1.0, P))).astype(np.float32)
    ang = inv[:, None] * np.arange(S, dtype=np.float32)[None, :]
    odd[:, O_COS:O_COS + S] = np.cos(ang.astype(np.float64))
    odd[:, O_SIN:O_SIN + S] = np.sin(ang.astype(np.float64))
    c[:, C_RANK:C_RANK + NE] = NE - np.arange(NE)
    c[:, C_IOTA:C_IOTA + P] = np.arange(P)
    return c, np.stack([even, odd])


class Ticks:

    def __init__(self, eng, sem):
        self.eng, self.sem, self.n = eng, sem, 0

    def __call__(self, ins):
        ins.then_inc(self.sem, 1)
        self.n += 1

    def sync(self):
        self.eng.wait_ge(self.sem, self.n)


def build(nc, a, out):
    ctx = ExitStack()
    with ctx:
        def sb(name, shape, dt=F32):
            return ctx.enter_context(nc.sbuf_tensor(name, shape, dt))

        def sem(name):
            return ctx.enter_context(nc.semaphore(name))

        raw = [sb(f"raw{j}", [P, SLOT]) for j in range(RING)]
        w_hi = [sb(f"w_hi{j}", [P, SLOT], F32R) for j in range(RING)]
        w_lo = [sb(f"w_lo{j}", [P, SLOT], F32R) for j in range(RING)]
        x_hi, x_lo = sb("x_hi", [P, KD, S], F32R), sb("x_lo", [P, KD, S], F32R)
        y_at = nc.sbuf_base
        y_hi, y_lo = sb("y_hi", [P, FT, S], F32R), sb("y_lo", [P, FT, S], F32R)
        y_spare = [nc.alloc_sbuf_tensor_at(f"y_spare{j}", [P, FT, S], F32, offset=y_at + 4 * FT * S * j) for j in range(2)]
        x = sb("x", [P, NT, D])
        const = sb("const", [P, N_CONST])
        vec = sb("vec", [P, N_VEC])
        small_hi, small_lo = sb("small_hi", [P, KD, NSMALL], F32R), sb("small_lo", [P, KD, NSMALL], F32R)
        arena = sb("arena", [P, 8192])
        prob = sb("prob", [P, 2 * AHEAD, 384])
        over = sb("over", [P, 2, NT, P])
        probT = sb("probT", [P, 2, 384])
        stat = sb("stat", [P, 2 * AHEAD, 6])
        tiny = sb("tiny", [P, 256])
        part = sb("part", [P, 2, 512])
        extra = sb("extra", [P, N_EXTRA])

        def view(at, shape):
            n = int(np.prod(shape))
            names = " ".join("abc"[:len(shape)])
            return arena[:, at:at + n].rearrange(f"p ({names}) -> p {names}", **dict(zip("abc", shape)))

        qT, kT = view(0, (KD, S)), view(2048, (KD, S))
        v = view(4096, (NT, D))
        oT = view(6144, (KD, S))
        z = view(0, (NT, D))
        xT = view(2048, (KD, S))
        row = view(4096, (2, D))
        rq, rk = view(0, (RH, 2, S)), view(2048, (RH, 2, S))
        rv = view(4096, (NT, 2 * D))
        sq = view(0, (4, S))
        skd = view(1024, (2, NKV, S))
        sv = view(2048, (NT, 2, P))
        xc = view(2560, (2, 16, NKV * NCMP))
        soT = view(3520, (8, S))
        cu = view(5568, (4, S))
        cz = view(6592, (4, S + 2))
        small_raw = view(6144, (KD, NSMALL))
        w2 = view(7624, (2, 2, 128))
        assert 7624 + 512 <= 8192
        xc_hi, xc_lo = (t[:, 8:12, :].rearrange("p a b -> p (a b)")[:, 0:960]
                        .rearrange("p (a b c) -> p a b c", a=2, b=16) for t in (y_hi, y_lo))
        hid = extra[:, 0:120].rearrange("p (a b c) -> p a b c", a=2, b=2)
        kc2 = extra[:, 120:150]
        hid_rows = extra[0:2 * NCMP, 512:1024]
        vc2 = extra[0:NCMP, 160:288].rearrange("p (a b) -> p a b", a=2)
        gates = extra[:, 288:336].rearrange("p (a b) -> p a b", a=NT)
        c8 = part[:, 0, 0:S]

        g_ps = [ctx.enter_context(nc.psum_tensor(f"g_ps{j}", [P, 512], F32)) for j in range(3)]
        a_ps = [ctx.enter_context(nc.psum_tensor(f"a_ps{j}", [P, 512], F32)) for j in range(4)]
        o_ps = ctx.enter_context(nc.psum_tensor("o_ps", [P, 512], F32))

        zero_col = sb("zero_col", [P, 1])
        logits = extra[0:NE, 512:512 + S]
        f_acc = view(0, (NT, D))
        o_sb = view(2048, (2, D))
        upto = view(6144, (NT, S))
        sel = view(6656, (NT, 2, P))
        sel_g = view(7168, (NT, 2, P))
        back = view(7680, (2, S))
        ranks = extra[:, 336:400].rearrange("p (a b c) -> p a b c", a=2, b=NT)
        ranks_now = extra[:, 400:408].rearrange("p (a b c) -> p a b c", a=2, b=NT)
        loops = sb("loops", [1, 1], mybir.dt.int32)

        def gate_view(s):
            flat = prob[:, :, :].rearrange("p a b -> p (a b)")
            return flat[:, (s % 3) * 512:(s % 3 + 1) * 512]

        oyT = view(0, (16, S))

        def hidden_at(m):
            return part[:, m % 8 // 4, (m % 4) * P:(m % 4 + 1) * P]

        ident = const[:, C_ID:C_ID + P]

        raw_in = [sem(f"raw_in{j}") for j in range(RING)]
        hi_done, lo_done = sem("hi_done"), sem("lo_done")
        used = sem("used")
        g_free = [sem(f"g_free{j}") for j in range(3)]
        const_in, vec_in, small_in, x_in = sem("const_in"), sem("vec_in"), sem("small_in"), sem("x_in")
        extra_in, rows_in, w2_in, final_in = sem("extra_in"), sem("rows_in"), sem("w2_in"), sem("final_in")
        small_hi_done, small_done = sem("small_hi_done"), sem("small_done")
        act_own, dve_own, pool_own = sem("act_own"), sem("dve_own"), sem("pool_own")
        n_z, root_in, root_done = sem("n_z"), sem("root_in"), sem("root_done")
        n_tr, n_ev, n_hi, n_lo, h_done = sem("n_tr"), sem("n_ev"), sem("n_hi"), sem("n_lo"), sem("h_done")
        narrow_full = sem("narrow_full")
        f_in, f_exp, f_ln, f_log, f_cum, f_c8 = (sem("f_" + n) for n in ("in", "exp", "ln", "log", "cum", "c8"))
        sc_full, mx_done, ex_done, over_done = (sem(n) for n in ("sc_full", "mx_done", "ex_done", "over_done"))
        tr_done, pv_done, o_free = (sem(n) for n in ("tr_done", "pv_done", "o_free"))
        pt_done = [sem("pt_even"), sem("pt_odd")]
        gate_done, y_made, y_split = sem("gate_done"), sem("y_made"), sem("y_split")
        r_sc, r_dec, r_out, r_norm, r_tr, r_hi, r_lo = (
            sem("r_" + n) for n in ("sc", "dec", "out", "norm", "tr", "hi", "lo"))
        r_y, r_ev = sem("r_y"), sem("r_ev")
        z_pad, xc_made, xc_hi_done, xc_split = sem("z_pad"), sem("xc_made"), sem("xc_hi_done"), sem("xc_split")
        hid_copied, hid_turned, kv_full, kc_done, gates_done = (
            sem(n) for n in ("hid_copied", "hid_turned", "kv_full", "kc_done", "gates_done"))
        m_logits, m_copied = sem("m_logits"), sem("m_copied")
        m_d, m_exp, m_on, m_rank, upto_in, m_loops = (sem("m_" + n) for n in ("d", "exp", "on", "rank", "upto_in", "loops"))
        m_now, m_sel, m_x, m_xhi, m_xlo = (sem("m_" + n) for n in ("now", "sel", "x", "xhi", "xlo"))
        m_tr, m_back, m_ytr, m_yhi, m_y, m_osb, m_sct, m_acc = (
            sem("m_" + n) for n in ("tr", "back", "ytr", "yhi", "y", "osb", "sct", "acc"))
        out_done = sem("out_done")

        g_slots = [s for a0, n in ([(0, 32), (40, 24), (91, 22)]
                                   + [(L_IN[l] + c, n) for l in range(DEPTH) for c, n in ((0, 7), (I_W1, 1), (I_W1 + 3, 1), (I_C, 4))]
                                   + [(MOE + 33 * i, 22) for i in range(PAIRS)]) for s in range(a0, a0 + n)]
        g_nth = {s: sum(1 for r in g_slots if r < s and r % 3 == s % 3) for s in g_slots}
        A_L = (16, 28)
        Y_L, Y_FFN = (8, 8 + 6 + FT), 8 + 6

        qT2, kT2 = (u[:, 8:16, :] for u in y_spare)
        v2 = [u[:, 16:20, :].rearrange("p a b -> p (a b)") for u in y_spare]
        qkv = [(qT, kT, [v[:, t, :] for t in range(NT)]), (qT2, kT2, v2)]
        oT2 = view(4096, (KD, S))

        def gate_even(u):
            return arena[:, 512 * u:512 * u + 512]

        def pairs_even(b):
            q_, k_, v_ = qkv[b]
            return [dict(q=[q_[b0:b0 + 64, p, :] for b0 in (0, 64)], k=[k_[b0:b0 + 64, p, :] for b0 in (0, 64)],
                         v=[[v_[t][:, HD * h:HD * h + HD] for t in range(NT)] for h in (2 * p, 2 * p + 1)],
                         mask="dil" if b else "causal", fox=None if b else 2 * p, gate=None, group=p,
                         first=True, last=True, k_ready=None, v_ready=None) for p in range(HF // 2)]

        def kv_turn(l):
            s = L_IN[l] + I_W1 + 3
            return s % 3, g_nth[s]

        def pairs_sparse(l):
            jobs = []
            for c in range(2):
                for p in range(NH // 2):
                    g = p // 2
                    for br in ((2,) if c else (0, 1)):
                        k = [skd[b:b + 64, br, g, :] if br < 2 else kc2[b:b + 64, g * NCMP:(g + 1) * NCMP] for b in (0, 64)]
                        vv = ([sv[:, t, br, g * HD:(g + 1) * HD] for t in range(NT)] if br < 2 else [vc2[0:NCMP, g, :]])
                        gate = 8 * (1 + br) + 2 * p if br < 2 else 2 * p
                        j, nth = kv_turn(l)
                        jobs.append(dict(q=[sq[b:b + 64, p, :] for b in (0, 64)], k=k, v=[vv, vv],
                                         mask="causal" if br < 2 else "cmp", fox=None, gate=gate, group=4 * c + p,
                                         first=br in (0, 2), last=br in (1, 2),
                                         k_ready=(kc_done, l + 1) if c else None,
                                         v_ready=(g_free[j], nth + 1) if c else None))
            return jobs

        def spans(jb):
            return ((0, NCMP), (NCMP, NCMP)) if jb["mask"] == "cmp" else ((0, P), (P, S))

        pair_g = [sum(1 for m in range(FT) if (MOE + m) % 3 == j) for j in range(3)]

        def loops_of(eng):
            eng.wait_ge(m_loops, 1)
            return eng.value_load(loops[0:1, 0:1], min_val=PAIRS - 1, max_val=2 * PAIRS - 1)

        T_BANK = (o_ps, a_ps[3])
        G_AFTER = ((0,), (1,), (2, 3), (4,))
        L_STEPS = {0: (4,), 1: (5,), 2: (6,), 3: (7, 8), 4: (9, 10), 5: (11,), 6: (12,), 8: (13,), 9: (14,)}
        STEP_ROWS, STEP_TURN, STEP_KV = 4, 5, 6
        GATHER = (1, 3, 5, 7)
        block = ctx.enter_context(nc.Block())
        from_x, from_y = (x_hi, x_lo), (y_hi, y_lo)

        @block.sync
        def _(sp):
            sp.dma_start(x[:, :, :], a["x"].rearrange("(t p) d -> p t d", p=P)).then_inc(x_in, 16)
            sp.dma_start(const[:, :], a["const"]).then_inc(const_in, 16)
            sp.dma_start(vec[:, :], a["vec"]).then_inc(vec_in, 16)
            for s in range(RING):
                sp.dma_start(raw[s][:, :], a["w"][s]).then_inc(raw_in[s], 16)
            with sp.Fori(1, N_SLOTS // RING) as i:
                for j in range(RING):
                    sp.wait_ge(lo_done, RING * (i - 1) + j + 1)
                    sp.dma_start(raw[j][:, :], a["w"][RING * i + j]).then_inc(raw_in[j], 16)
            for s in range(N_SLOTS // RING * RING, N_SLOTS):
                sp.wait_ge(lo_done, s - RING + 1)
                sp.dma_start(raw[s % RING][:, :], a["w"][s]).then_inc(raw_in[s % RING], 16)
            more = loops_of(sp) - (PAIRS - 1)
            with sp.Fori(0, more * (33 // RING)) as i:
                for j in range(RING):
                    sp.wait_ge(lo_done, N_SLOTS - RING + j + 1 + RING * i)
                    sp.dma_start(raw[(N_SLOTS + j) % RING][:, :], a["w"][MOE + j + RING * i]).then_inc(raw_in[(N_SLOTS + j) % RING], 16)
            sp.wait_ge(h_done, 6)
            sp.dma_start(out.rearrange("b (t p) d -> p (b t) d", p=P), x[:, :, :]).then_inc(out_done, 16)
            sp.wait_ge(out_done, 16)

        @block.gpsimd
        def _(pool):
            own = Ticks(pool, pool_own)
            pool.dma_start(small_raw, a["small"]).then_inc(small_in, 16)
            pool.dma_start(extra[:, :], a["extra"][0]).then_inc(extra_in, 16)
            own(pool.memset(zero_col[:, :], 0.0))
            own(pool.memset(tiny[:, 226:228], -0.5))
            own.sync()
            pool.memset(c8, 0.0).then_inc(z_pad, 1)

            roots = []

            def root():
                roots.append(0)
                pool.wait_ge(root_in, len(roots))
                pool.tensor_tensor(tiny[:, 228:230], tiny[:, 224:226], tiny[:, 226:228], ALU.pow).then_inc(root_done, 1)

            def split_x(i):
                for b in range(4):
                    pool.wait_ge(n_hi, 4 * i + b + 1)
                    pool.tensor_tensor(x_lo[:, 2 * b:2 * b + 2, :], xT[:, 2 * b:2 * b + 2, :],
                                       x_hi[:, 2 * b:2 * b + 2, :].bitcast(F32), ALU.subtract).then_inc(n_lo, 1)

            def split_y(made, count, src, at, n, turn=0):
                pool.wait_ge(made, count)
                own(pool.tensor_tensor(y_hi[:, at:at + n, :], src,
                                       zero_col[:, 0:1].unsqueeze(2).to_broadcast([P, n, S]), ALU.add))
                pool.wait_ge(pool_own, own.n + FT * turn)
                pool.tensor_tensor(y_lo[:, at:at + n, :], src, y_hi[:, at:at + n, :].bitcast(F32),
                                   ALU.subtract).then_inc(y_split, 1)

            def wide(u):
                return part[:, u % 2, :].rearrange("p (a b) -> p a b", a=2)

            def narrow(u):
                return part[:, u % 2:u % 2 + 1, 0:S]

            def token_h(i, tiles=range(NT)):
                pool.wait_ge(rows_in, 16 * (i - 1))
                pool.wait_ge(n_z, 2 * (i + 1))
                for t in tiles:
                    own(pool.tensor_tensor(x[:, t, :], z[:, t, :], row[:, 0, :], ALU.mult))
                own.sync()
                for t in tiles:
                    ins = pool.tensor_tensor(x[:, t, :], x[:, t, :], row[:, 1, :], ALU.add)
                ins.then_inc(h_done, 1)

            def load_rows(i):
                pool.dma_start(row[:, :, :], a["rows"][i - 2].rearrange("a p d -> p a d")).then_inc(rows_in, 16)

            root()
            split_x(0)
            for b in range(2):
                for u in range(4 * b, 4 * b + 4):
                    split_y(y_made, u + 1, wide(u), 2 * u, 2)
            pool.wait_ge(used, EV_OUT)
            pool.dma_start(extra[:, :], a["extra"][1]).then_inc(extra_in, 16)
            root()
            split_x(1)
            for h in range(RH):
                root()
            for b in range(8):
                pool.wait_ge(r_hi, b + 1)
                pool.tensor_tensor(y_lo[:, 2 * b:2 * b + 2, :], oyT[:, 2 * b:2 * b + 2, :],
                                   y_hi[:, 2 * b:2 * b + 2, :].bitcast(F32), ALU.subtract).then_inc(r_lo, 1)
            pool.wait_ge(used, OD_OUT + 8)
            pool.dma_start(view(6144, (D,)), a["rows_final"]).then_inc(final_in, 16)
            load_rows(2)
            root()
            root()
            split_x(2)
            token_h(2)
            for l in range(DEPTH):
                pool.wait_ge(n_lo, 4 * (3 + 2 * l))
                pool.wait_ge(h_done, 1 + 2 * l)
                pool.memset(cz[:, :, 0:2], 0.0).then_inc(z_pad, 1)
                pool.dma_start(w2[:, :, :, :], a["w2"][l]).then_inc(w2_in, 16)
                pool.wait_ge(xc_hi_done, l + 1)
                pool.tensor_tensor(xc_lo, xc, xc_hi.bitcast(F32), ALU.subtract).then_inc(xc_split, 1)
                for j in range(2):
                    s = L_IN[l] + I_B + j
                    split_y(g_free[s % 3], g_nth[s] + 1, wide(j), 4 + 2 * j, 2)
                for g in range(NH // 2):
                    split_y(y_made, 8 + 4 * l + g + 1, narrow(g), g, 1)
                pool.wait_ge(used, L_WO[l] + 4)
                load_rows(3 + 2 * l)
                if l:
                    pool.dma_start(upto[:, :, :], a["extra"][0][:, E_CUM:E_CUM + NT * S]
                                   .rearrange("p (a b) -> p a b", a=NT)).then_inc(upto_in, 16)
                root()
                split_x(3 + 2 * l)
                token_h(3 + 2 * l)
                if l == 0:
                    for m in range(FT):
                        s = FFN_IN + m
                        split_y(g_free[s % 3], g_nth[s] + 1, narrow(m), m, 1)
                    pool.wait_ge(used, FFN_DOWN + 11)
                    load_rows(4)
                    root()
                    split_x(4)
                    token_h(4)
                else:
                    pool.wait_ge(h_done, 4)
                    load_rows(6)
                    root()
                    token_h(6, (0,))

        @block.tensor
        def _(pe):
            def parts_mm(ps, lhs, rhs, start, stop):
                (lh, ll), (rh, rl) = lhs, rhs
                pe.matmul(ps, lh, rh, start=start, stop=False, skip_group_check=True)
                pe.matmul(ps, lh, rl, start=False, stop=False, skip_group_check=True)
                return pe.matmul(ps, ll, rh, start=False, stop=stop, skip_group_check=True)

            def mm32(ps, lhs, rhs, start=True, stop=True):
                return pe.matmul(ps, lhs, rhs, start=start, stop=stop, skip_group_check=True)

            def turned(ps, src):
                return pe.transpose(ps, src, ident)

            def pick(pair, f):
                return [f(t) for t in pair]

            def weights(s, shape):
                kw = dict(zip("kc", shape))
                return pick((w_hi[s % RING], w_lo[s % RING]), lambda t: t[:, :].rearrange("p (k c) -> p k c", **kw))

            coming = []

            def rows_slot(s):
                pe.wait_ge(lo_done, s + 1)
                if g_nth[s] > 0:
                    pe.wait_ge(g_free[s % 3], g_nth[s])
                w = weights(s, (KD, S))
                for m in range(2):
                    for k in range(KD):
                        parts_come(k)
                        mm = parts_mm(g_ps[s % 3][:, m * S:(m + 1) * S],
                                      pick(w, lambda t: t[:, k, m * P:(m + 1) * P]),
                                      pick(from_x, lambda t: t[:, k, :]), k == 0, k == KD - 1)
                mm.then_inc(used, 1)

            def token_mm(s, ps, src, k0, first, last):
                w = weights(s, (KD, S))
                for t in range(NT):
                    for k in range(KD):
                        mm = parts_mm(ps[:, t * S:(t + 1) * S], pick(src, lambda u: u[:, k0 + k, t * P:(t + 1) * P]),
                                      pick(w, lambda u: u[:, k, :]), first and k == 0 and t == 0, last and k == KD - 1)
                return mm

            def token_slot(s):
                pe.wait_ge(lo_done, s + 1)
                if g_nth[s] > 0:
                    pe.wait_ge(g_free[s % 3], g_nth[s])
                token_mm(s, g_ps[s % 3], from_x, 0, True, True).then_inc(used, 1)

            def out_slot(s0, halves, n):
                s, c, h = s0 + n, n % 4, n // 4
                pe.wait_ge(lo_done, s + 1)
                token_mm(s, a_ps[c], from_y, KD * h, h == 0, h == halves - 1).then_inc(used, 1)

            def transposed_norm(i):
                for b in range(4):
                    for j in range(2):
                        for t in range(NT):
                            if b == 0 and j == 0:
                                pe.wait_ge(n_z, 2 * i + t + 1)
                            k = 2 * b + j
                            tr = turned(a_ps[b][:, j * S + t * P:j * S + (t + 1) * P], z[:, t, k * P:(k + 1) * P])
                    tr.then_inc(n_tr, 1)
                coming.append(i)

            def parts_come(k):
                if coming and k % 2 == 0:
                    pe.wait_ge(n_lo, 4 * coming[0] + k // 2 + 1)
                if coming and k == KD - 1:
                    coming.pop()

            def narrow_product(at, n):
                for t in range(NT):
                    for k in range(KD):
                        parts_come(k)
                        mm = parts_mm(a_ps[0][:, t * 32:t * 32 + n], pick(from_x, lambda u: u[:, k, t * P:(t + 1) * P]),
                                      pick((small_hi, small_lo), lambda u: u[:, k, at:at + n]),
                                      k == 0 and t == 0, k == KD - 1)
                mm.then_inc(narrow_full, 1)

            def attention(jobs, a0, outs_read, between):
                def scores(i, jb):
                    n = a0 + i
                    if n >= 1:
                        pe.wait_ge(mx_done, 2 * n)
                    if jb["k_ready"]:
                        pe.wait_ge(*jb["k_ready"])
                    for t, (at, keys) in enumerate(spans(jb)):
                        for h in range(2):
                            mm = mm32(a_ps[h][:, at:at + keys], jb["q"][h][:, t * P:(t + 1) * P],
                                      jb["k"][h][:, 0:keys], stop=jb["fox"] is None)
                        if jb["fox"] is not None:
                            for h in range(2):
                                col = C_ID + 64 * h + jb["fox"] + h
                                mm = mm32(a_ps[h][:, at:at + keys],
                                          const[64 * h:64 * h + 64, col:col + 1].to_broadcast([64, P]),
                                          c8[64 * h:64 * h + 64, 0:keys], start=False)
                    mm.then_inc(sc_full, 1)

                def turn(i, jb):
                    n = a0 + i
                    pe.wait_ge(over_done, n + 1)
                    for h in range(2):
                        if n >= 1:
                            pe.wait_ge(pt_done[h], n)
                        ps, pr = a_ps[2 + h], prob[:, 2 * (n % AHEAD) + h, :]
                        if jb["mask"] == "cmp":
                            for t in range(NT):
                                tr = mm32(ps[0:NCMP, t * P:(t + 1) * P], pr[:, t * NCMP:(t + 1) * NCMP], over[:, h, t, :])
                        else:
                            for c in range(3):
                                tr = mm32(ps[:, c * P:(c + 1) * P], pr[:, c * P:(c + 1) * P], over[:, h, min(c, 1), :])
                        tr.then_inc(tr_done, 1)

                def values(i, jb):
                    for h in range(2):
                        pe.wait_ge(pt_done[h], a0 + i + 1)
                    if jb["first"] and jb["group"] >= 1:
                        pe.wait_ge(*outs_read(jb["group"] - 1))
                    if jb["v_ready"]:
                        pe.wait_ge(*jb["v_ready"])
                    for t in range(len(jb["v"][0])):
                        for h in range(2):
                            out_ = o_ps[64 * h:64 * h + 64, t * P:S]
                            if jb["mask"] == "cmp":
                                mm = mm32(out_, jb["v"][h][0], probT[0:NCMP, h, 0:S])
                            else:
                                mm = mm32(out_, jb["v"][h][t], probT[:, h, t * S:S + t * P],
                                          jb["first"] and t == 0, jb["last"] and t == 1)
                    mm.then_inc(pv_done, 1)

                for i in range(len(jobs) + 3):
                    if i < len(jobs):
                        scores(i, jobs[i])
                    if 2 <= i < len(jobs) + 2:
                        turn(i - 2, jobs[i - 2])
                    if i >= 3:
                        values(i - 3, jobs[i - 3])
                    between(i)

            def even_slot(s):
                (token_slot if s in range(EV_V[0], EV_V[0] + 4) or s in range(EV_V[1], EV_V[1] + 4) else rows_slot)(s)

            pe.wait_ge(const_in, 16)
            pe.wait_ge(z_pad, 1)
            transposed_norm(0)
            for s in range(4):
                even_slot(s)
            pe.wait_ge(small_done, 1)
            narrow_product(0, HF)
            for s in range(4, 8):
                even_slot(s)
            pe.wait_ge(extra_in, 16)
            pe.wait_ge(f_log, 1)
            for t in range(NT):
                mm = mm32(a_ps[1][0:HF, 0:S], tiny[:, 160 + HF * t:160 + HF * (t + 1)],
                          extra[:, E_CUM + t * S:E_CUM + (t + 1) * S], t == 0, t == 1)
            mm.then_inc(f_cum, 1)
            def among(s0, n):
                return lambda i: even_slot(s0 + i) if i < n else None

            for s in range(8, 12):
                even_slot(s)
            for s in range(9, 12):
                pe.wait_ge(g_free[s % 3], g_nth[s] + 1)
            pe.wait_ge(f_c8, 1)
            attention(pairs_even(0), 0, lambda g: (o_free, g + 1), among(12, 11))
            even_slot(23)
            for s in range(21, 24):
                pe.wait_ge(g_free[s % 3], g_nth[s] + 1)

            def gates_and_out(i):
                if i < 8:
                    even_slot(24 + i)
                elif i < 12:
                    if i == 8:
                        pe.wait_ge(mx_done, 32)
                        pe.wait_ge(y_split, 4)
                    if i >= 10:
                        pe.wait_ge(pt_done[i - 10], 16)
                    out_slot(EV_OUT, 2, i - 8)

            attention(pairs_even(1), 8, lambda g: (o_free, 8 + g + 1), gates_and_out)
            gates_and_out(11)
            pe.wait_ge(y_split, 8)
            for n in range(4, 8):
                out_slot(EV_OUT, 2, n)

            transposed_norm(1)
            for s in range(OD_QK, OD_QK + 8):
                rows_slot(s)
            for s in range(OD_V, OD_V + 8):
                token_slot(s)
            for s in range(OD_V + 5, OD_V + 8):
                pe.wait_ge(g_free[s % 3], g_nth[s] + 1)
            for h in range(RH):
                if h:
                    pe.wait_ge(r_dec, h)
                for half in range(2):
                    mm32(a_ps[0][:, 0:S], rk[:, h, half, 0:P], rq[:, h, half, :], half == 0, half == 1)
                for half in range(2):
                    mm = mm32(a_ps[0][:, S:S + P], rk[:, h, half, P:S], rq[:, h, half, P:S], half == 0, half == 1)
                mm.then_inc(r_sc, 1)
                for m in G_AFTER[h]:
                    token_slot(OD_G + m)
                pe.wait_ge(r_dec, h + 1)
                if h:
                    pe.wait_ge(r_norm, h)
                sT, hv = prob[:, 4 + h % 2, :], slice(h * RV, (h + 1) * RV)
                mm32(a_ps[1][:, :], sT[:, 0:P], rv[:, 0, hv])
                mm32(a_ps[2][:, :], sT[:, P:S], rv[:, 0, hv], True, False)
                mm32(a_ps[2][:, :], sT[:, S:S + P], rv[:, 1, hv], False, True).then_inc(r_out, 1)

            def turn_outputs(b):
                pe.wait_ge(r_y, b + 1)
                if b >= 2:
                    pe.wait_ge(r_ev, b - 1)
                for j in range(2):
                    for t in range(NT):
                        k = 2 * b + j
                        tr = turned(T_BANK[b % 2][:, j * S + t * P:j * S + (t + 1) * P], rv[:, t, k * P:(k + 1) * P])
                tr.then_inc(r_tr, 1)

            for m in range(5, 8):
                token_slot(OD_G + m)
                for b in (2 * (m - 5), 2 * (m - 5) + 1):
                    turn_outputs(b)
            pe.wait_ge(r_norm, RH)
            pe.wait_ge(r_lo, 4)
            for n in range(8):
                if n == 3:
                    pe.wait_ge(r_ev, 8)
                if n == 4:
                    pe.wait_ge(r_lo, 8)
                out_slot(OD_OUT, 2, n)
                if n < 2:
                    turn_outputs(6 + n)

            def feed_forward(s0):
                for m in range(FT):
                    rows_slot(s0 + m)
                for c in range(FT // 2):
                    s = s0 + FT + c
                    pe.wait_ge(lo_done, s + 1)
                    pe.wait_ge(y_split, Y_FFN + 2 * c + 2)
                    w = weights(s, (2, D))
                    for k in range(2):
                        for t in range(NT):
                            for n in range(2):
                                mm = parts_mm(a_ps[2 * t + n][:, :],
                                              pick(from_y, lambda u: u[:, 2 * c + k, t * P:(t + 1) * P]),
                                              pick(w, lambda u: u[:, k, n * 512:(n + 1) * 512]), c == 0 and k == 0,
                                              c == FT // 2 - 1 and k == 1)
                    mm.then_inc(used, 1)

            transposed_norm(2)
            for l in range(DEPTH):
                s0 = L_IN[l]
                if l:
                    transposed_norm(4)
                for s in range(s0, s0 + 4):
                    (token_slot if s == s0 + 3 else rows_slot)(s)
                    if s == s0 + 1:
                        narrow_product(HF + 24 * l, 24)

                def compress(kind, h):
                    s, first = s0 + I_W1 + 2 * kind + h, s0 + I_W1
                    if kind == 0 and h == 0:
                        pe.wait_ge(xc_split, l + 1)
                        pe.wait_ge(g_free[first % 3], g_nth[first])
                    pe.wait_ge(lo_done, s + 1)
                    w = weights(s, (KD, S))
                    for k in range(KD):
                        mm = parts_mm(g_ps[first % 3][0:2 * NCMP, kind * S:(kind + 1) * S],
                                      pick((xc_hi, xc_lo), lambda t: t[:, kind, KD * h + k, :]),
                                      pick(w, lambda t: t[:, k, :]), kind == 0 and h == 0 and k == 0,
                                      h == 1 and k == KD - 1)
                    mm.then_inc(used, 1)

                def turn_rows():
                    pe.wait_ge(hid_copied, l + 1)
                    for c in range(4):
                        tr = pe.transpose(g_ps[(s0 + I_W1) % 3][:, c * 32:c * 32 + 2 * NCMP],
                                          hid_rows[:, c * P:(c + 1) * P], ident[0:2 * NCMP, 0:2 * NCMP])
                    tr.then_inc(hid_turned, 1)

                def compressed():
                    first = s0 + I_W1
                    j, nth = kv_turn(l)
                    pe.wait_ge(w2_in, 16 * (l + 1))
                    pe.wait_ge(g_free[first % 3], g_nth[first] + 1)
                    pe.wait_ge(g_free[j], nth)
                    for m in range(2):
                        mm32(g_ps[j][:, 0:30], w2[:, 0, m, :], hid[:, 0, m, :], m == 0, m == 1)
                    for g in range(NKV):
                        for m in range(2):
                            mm = mm32(g_ps[j][0:NCMP, 128 + g * HD:128 + (g + 1) * HD], hid[:, 1, m, g * NCMP:(g + 1) * NCMP],
                                      w2[:, 1, m, 0:HD], m == 0, m == 1)
                    mm.then_inc(kv_full, 1)

                def between(i):
                    for m in L_STEPS.get(i, ()):
                        if m in range(I_W1, I_W1 + 4):
                            compress((m - I_W1) // 2, (m - I_W1) % 2)
                        else:
                            rows_slot(s0 + m)
                    if i == STEP_TURN:
                        turn_rows()
                    if i == STEP_KV:
                        compressed()

                for s in range(s0 + 1, s0 + 4):
                    pe.wait_ge(g_free[s % 3], g_nth[s] + 1)
                pe.wait_ge(gates_done, l + 1)
                attention(pairs_sparse(l), A_L[l], lambda g: (o_free, 16 + 4 * l + g + 1) if g < 4 else
                          (y_made, 8 + 4 * l + g - 3), between)
                for h in range(2):
                    pe.wait_ge(pt_done[h], A_L[l] + 12)
                pe.wait_ge(y_split, Y_L[l] + 6)
                for n in range(4):
                    out_slot(L_WO[l], 1, n)
                transposed_norm(3 + 2 * l)
                if l == 0:
                    feed_forward(FFN_IN)
            for k in range(KD):
                parts_come(k)
                mm = parts_mm(o_ps[0:NE, 0:S], pick((small_hi, small_lo), lambda u: u[:, k, HF + 48:HF + 48 + NE]),
                              pick(from_x, lambda u: u[:, k, :]), k == 0, k == KD - 1)
            mm.then_inc(m_logits, 1)
            pe.wait_ge(m_copied, 1)
            for t in range(NT):
                tr = pe.transpose(a_ps[0][:, 32 * t:32 * t + NE], logits[:, t * P:(t + 1) * P], ident[0:NE, 0:NE])
            tr.then_inc(narrow_full, 1)
            on = [tiny[:, 16 + NE * t:16 + NE * (t + 1)] for t in range(NT)]
            pe.wait_ge(upto_in, 16)
            pe.wait_ge(m_on, 1)
            for t in range(NT):
                for u in range(t + 1):
                    mm32(a_ps[1][:, 16 * t:16 * t + NE], upto[:, u, t * P:(t + 1) * P], on[u], u == 0, u == t)
            for u in range(NT):
                mm = mm32(a_ps[1][0:1, 32:32 + NE], upto[:, u, S - 1:S], on[u], u == 0, u == NT - 1)
            mm.then_inc(m_rank, 1)

            def gather(q, bank):
                for k in (0, 1):
                    for t in range(NT):
                        mm = mm32(bank[:, k * S:(k + 1) * S], x[:, t, (2 * q + k) * P:(2 * q + k + 1) * P],
                                  sel[:, t, :, :].rearrange("p e r -> p (e r)"), t == 0, t == NT - 1)
                mm.then_inc(m_x, 1)

            pe.wait_ge(m_sel, 8)
            pe.wait_ge(h_done, 4)
            for q in range(4):
                gather(q, a_ps[q])

            def experts(i, last):
                pe.wait_ge(m_xlo, 4 + 4 * i)
                for e in range(2):
                    for t in range(NT):
                        tr = turned(o_ps[:, e * S + t * P:e * S + (t + 1) * P], sel_g[:, t, e, :])
                tr.then_inc(m_tr, 1)

                def turn_hidden(c):
                    if c == 0:
                        pe.wait_ge(m_acc, 1 + 4 * i)
                    if c >= 2:
                        pe.wait_ge(m_y, c - 1 + FT // 2 * i)
                    for m in (2 * c, 2 * c + 1):
                        j = (MOE + m) % 3
                        pe.wait_ge(g_free[j], g_nth[MOE + m] + 1 + pair_g[j] * i)
                        tr = turned(a_ps[2 + c % 2][:, (m % 2) * P:(m % 2 + 1) * P], hidden_at(m))
                    tr.then_inc(m_ytr, 1)

                for m in range(FT):
                    s, e = MOE + m, m // 11
                    pe.wait_ge(lo_done, s + 1 + 33 * i)
                    pe.wait_ge(g_free[s % 3], g_nth[s] + pair_g[s % 3] * i)
                    w = weights(s, (KD, S))
                    for k in range(KD):
                        mm = parts_mm(g_ps[s % 3][:, 0:S], pick(from_x, lambda u: u[:, k, e * P:(e + 1) * P]),
                                      pick(w, lambda u: u[:, k, :]), k == 0, k == KD - 1)
                    mm.then_inc(used, 1)
                    if m % 2 and m >= 3:
                        turn_hidden((m - 3) // 2)
                for c in range(FT // 2):
                    s = MOE + FT + c
                    pe.wait_ge(lo_done, s + 1 + 33 * i)
                    pe.wait_ge(m_y, c + 1 + FT // 2 * i)
                    w = weights(s, (2, D))
                    for k in range(2):
                        m = 2 * c + k
                        for n in range(2):
                            mm = parts_mm(a_ps[2 * (m // 11) + n][:, :], pick(from_y, lambda u: u[:, m, 0:P]),
                                          pick(w, lambda u: u[:, k, n * 512:(n + 1) * 512]), m % 11 == 0, m % 11 == 10)
                    mm.then_inc(used, 1)
                    if c == 0:
                        turn_hidden(FT // 2 - 1)
                    if c in GATHER and not last:
                        q = GATHER.index(c)
                        if q == 0:
                            pe.wait_ge(m_sel, 16 + 8 * i)
                            pe.wait_ge(m_back, 1 + i)
                        else:
                            pe.wait_ge(m_xlo, 4 + q + 4 * i)
                        gather(q, o_ps)
                pe.wait_ge(m_back, 1 + i)
                pe.wait_ge(m_osb, 4 + 4 * i)
                for t in range(NT):
                    for n in range(2):
                        for e in range(2):
                            mm = mm32(a_ps[2 * t + n][:, :], back[:, e, t * P:(t + 1) * P],
                                      o_sb[:, e, n * 512:(n + 1) * 512], e == 0, e == 1)
                mm.then_inc(m_sct, 1)

            before = loops_of(pe)
            with pe.Fori(0, before) as i:
                experts(i, False)
            experts(before, True)

        @block.scalar
        def _(act):
            own = Ticks(act, act_own)

            def split_hi(s, turn, slot):
                if s >= N_SLOTS:
                    return
                act.wait_ge(raw_in[s % RING], 16 * (s // RING + 1) + 16 * turn)
                if s >= RING:
                    act.wait_ge(used, slot - RING + 1)
                act.activation(w_hi[s % RING][:, :], raw[s % RING][:, :], ACT.Copy).then_inc(hi_done, 1)

            def ahead(s, turn=0):
                split_hi(s + RING, turn, s + RING * (1 + turn))

            def copy_slot(s, dst):
                act.wait_ge(used, s + 1)
                src = g_ps[s % 3][:, :].rearrange("p (a b) -> p a b", a=2)
                act.activation(dst, src, ACT.Copy).then_inc(g_free[s % 3], 1)
                ahead(s)

            def hi_x(i):
                for b in range(4):
                    act.wait_ge(n_ev, 4 * i + b + 1)
                    act.activation(x_hi[:, 2 * b:2 * b + 2, :], xT[:, 2 * b:2 * b + 2, :], ACT.Copy).then_inc(n_hi, 1)

            def attention(jobs, a0, between):
                def exps(i, h):
                    n, slot = 2 * (a0 + i) + h, 2 * ((a0 + i) % AHEAD) + h
                    act.wait_ge(mx_done, n + 1)
                    for t, (at, keys) in enumerate(spans(jobs[i])):
                        pr = prob[:, slot, at:at + keys]
                        ins = act.activation(pr, pr, ACT.Exp, bias=stat[:, slot, t:t + 1], scale=-1.0,
                                             accum_out=stat[:, slot, 2 + t:3 + t])
                    ins.then_inc(ex_done, 1)

                def copy_odd(i):
                    m = a0 + i
                    act.wait_ge(tr_done, 2 * m + 2)
                    if m >= 1:
                        act.wait_ge(pv_done, m)
                    p, w = (NCMP, S) if jobs[i]["mask"] == "cmp" else (P, 384)
                    act.activation(probT[0:p, 1, 0:w], a_ps[3][0:p, 0:w], ACT.Copy).then_inc(pt_done[1], 1)

                for i in range(len(jobs) + 4):
                    if i < len(jobs):
                        exps(i, 0)
                    if 2 <= i < len(jobs) + 2:
                        copy_odd(i - 2)
                    if i < len(jobs):
                        exps(i, 1)
                    if i:
                        between(i - 1)

            split_hi(0, 0, 0)
            hi_x(0)
            for s in (1, 2):
                split_hi(s, 0, s)
            act.wait_ge(small_in, 16)
            act.activation(small_hi[:, :, :], small_raw, ACT.Copy).then_inc(small_hi_done, 1)
            act.wait_ge(n_lo, 4)

            def even_slot(s):
                b, m = s // 12, s % 12
                act.wait_ge(used, s + 1)
                src = g_ps[s % 3][:, :].rearrange("p (a b) -> p a b", a=2)
                if s >= EV_G[0]:
                    ins = act.activation(gate_even(s - EV_G[0]), g_ps[s % 3][:, :], ACT.Silu)
                elif m < 8:
                    ins = act.activation(qkv[b][m // 4][:, 2 * (m % 4):2 * (m % 4) + 2, :], src, ACT.Copy)
                else:
                    for t in range(NT):
                        ins = act.activation(qkv[b][2][t][:, (m - 8) * S:(m - 7) * S], src[:, t, :], ACT.Copy)
                ins.then_inc(g_free[s % 3], 1)
                ahead(s)

            def among(s0, n):
                return lambda i: even_slot(s0 + i) if i < n else None

            for s in range(4):
                even_slot(s)
            act.wait_ge(f_in, 1)
            act.activation(tiny[:, 96:128], tiny[:, 64:96], ACT.Exp, scale=-1.0).then_inc(f_exp, 1)
            act.wait_ge(f_ln, 1)
            act.activation(tiny[:, 128:160], tiny[:, 96:128], ACT.Ln).then_inc(f_exp, 1)
            for s in range(4, 8):
                even_slot(s)
            act.wait_ge(f_cum, 1)
            act.wait_ge(z_pad, 1)
            for b in (0, 64):
                ins = act.activation(c8[b:b + HF, :], a_ps[1][0:HF, 0:S], ACT.Copy, scale=-1.0 / SCALE)
            ins.then_inc(f_c8, 1)
            for s in range(8, 12):
                even_slot(s)
            attention(pairs_even(0), 0, among(12, 11))
            even_slot(23)
            attention(pairs_even(1), 8, lambda i: even_slot(24 + i) if i < 8 else ahead(EV_OUT + i - 8))
            for n in range(3, 8):
                ahead(EV_OUT + n)

            hi_x(1)
            act.wait_ge(n_lo, 8)
            for s in range(OD_QK, OD_QK + 8):
                ahead(s)
            for m in range(8):
                copy_slot(OD_V + m, rv[:, :, m * S:(m + 1) * S])

            def gate_slot(u):
                s = OD_G + u
                act.wait_ge(used, s + 1)
                if u >= 3:
                    act.wait_ge(r_y, u - 2)
                act.activation(gate_view(s), g_ps[s % 3][:, :], ACT.Silu).then_inc(g_free[s % 3], 1)
                ahead(s)

            for h in range(RH):
                for u in G_AFTER[h]:
                    gate_slot(u)

            def copy_turned(b):
                act.wait_ge(r_tr, b + 1)
                act.activation(oyT[:, 2 * b:2 * b + 2, :], T_BANK[b % 2][:, :].rearrange("p (a b) -> p a b", a=2),
                               ACT.Copy).then_inc(r_ev, 1)

            for u in range(5, 8):
                gate_slot(u)
                for b in (2 * (u - 5), 2 * (u - 5) + 1):
                    copy_turned(b)
            for n in range(8):
                ahead(OD_OUT + n)
                if n < 2:
                    copy_turned(6 + n)

            hi_x(2)
            for l in range(DEPTH):
                s0 = L_IN[l]
                if l:
                    hi_x(4)
                act.wait_ge(n_lo, 4 * (3 + 2 * l))
                act.wait_ge(h_done, 1 + 2 * l)
                for m in range(2):
                    copy_slot(s0 + m, sq[:, 2 * m:2 * m + 2, :])
                act.wait_ge(narrow_full, 2 + l)
                act.activation(gates[:, :, :], a_ps[0][:, 0:64].rearrange("p (a b) -> p a b", a=2)[:, :, 0:24],
                               ACT.Sigmoid).then_inc(gates_done, 1)
                s = s0 + 2
                act.wait_ge(used, s + 1)
                for g in range(NKV):
                    for d in range(2):
                        ins = act.activation(skd[64 * d:64 * d + 64, :, g, :],
                                             g_ps[s % 3][64 * g:64 * g + 64, :].rearrange("p (a b) -> p a b", a=2),
                                             ACT.Copy)
                ins.then_inc(g_free[s % 3], 1)
                ahead(s)
                copy_slot(s0 + 3, sv[:, :, :, :].rearrange("p t b d -> p t (b d)"))

                def between(i):
                    first = s0 + I_W1
                    for m in L_STEPS.get(i, ()):
                        if m == I_U:
                            act.wait_ge(xc_made, l + 1)
                            act.activation(xc_hi, xc, ACT.Copy).then_inc(xc_hi_done, 1)
                        if m in (I_U, I_U + 1):
                            copy_slot(s0 + m, cu[:, 2 * (m - I_U):2 * (m - I_U) + 2, :])
                        else:
                            ahead(s0 + m)
                    if i == STEP_ROWS:
                        act.wait_ge(used, first + 4)
                        act.activation(hid_rows, g_ps[first % 3][0:2 * NCMP, :], ACT.Copy).then_inc(hid_copied, 1)
                    if i == STEP_TURN:
                        act.wait_ge(hid_turned, l + 1)
                        for kind in range(2):
                            for c in range(2):
                                b1 = V_B1 + 4 * l + 2 * kind + c
                                at = (2 * kind + c) * 32
                                ins = act.activation(hid[:, kind, c, :], g_ps[first % 3][:, at:at + 30],
                                                     ACT.Gelu_apprx_tanh, bias=vec[:, b1:b1 + 1])
                        ins.then_inc(g_free[first % 3], 1)

                attention(pairs_sparse(l), A_L[l], between)
                for s in range(L_WO[l], L_WO[l] + 4):
                    ahead(s)
                hi_x(3 + 2 * l)

                def hidden(s, slot):
                    act.wait_ge(used, slot + 1)
                    act.activation(gate_view(s)[:, 0:S], g_ps[s % 3][:, 0:S], ACT.Silu).then_inc(gate_done, 1)

                if l == 0:
                    for m in range(FT):
                        hidden(FFN_IN + m, FFN_IN + m)
                        ahead(FFN_IN + m)
                    for s in range(FFN_DOWN, FFN_DOWN + 11):
                        ahead(s)
                else:
                    act.wait_ge(m_d, 1)
                    act.activation(tiny[:, 100:102], tiny[:, 98:100], ACT.Exp).then_inc(m_exp, 1)
                    def next_x(q, count, bank=o_ps):
                        act.wait_ge(m_x, count)
                        act.activation(x_hi[:, 2 * q:2 * q + 2, :], bank[:, :].rearrange("p (a b) -> p a b", a=2),
                                       ACT.Copy).then_inc(m_xhi, 1)

                    before = loops_of(act)
                    for q in range(4):
                        next_x(q, q + 1, a_ps[q])

                    def experts(i, last):
                        act.wait_ge(m_tr, 1 + i)
                        act.activation(back[:, :, :], o_ps[:, :].rearrange("p (a b) -> p a b", a=2), ACT.Copy).then_inc(m_back, 1)

                        def y_high(c):
                            act.wait_ge(m_ytr, c + 1 + FT // 2 * i)
                            act.activation(y_hi[:, 2 * c:2 * c + 2, 0:P],
                                           a_ps[2 + c % 2][:, 0:S].rearrange("p (a b) -> p a b", a=2), ACT.Copy).then_inc(m_yhi, 1)

                        for m in range(FT):
                            s = MOE + m
                            if m % 2 == 0 and m >= 4:
                                y_high((m - 4) // 2)
                            act.wait_ge(used, s + 1 + 33 * i)
                            act.activation(gate_view(s)[:, 0:P], g_ps[s % 3][:, 0:P], ACT.Silu).then_inc(gate_done, 1)
                            ahead(s, 11 * i)
                        for c in range(11):
                            if c < 2:
                                y_high(9 + c)
                            if c in (6, 10):
                                e = c // 10
                                act.wait_ge(used, MOE + FT + (6 if e == 0 else 11) + 33 * i)
                                act.activation(o_sb[:, e, 0:512], a_ps[2 * e][:, :], ACT.Copy).then_inc(m_osb, 1)
                            if not (last and c >= 8):
                                ahead(MOE + FT + c, 11 * i)
                            if c in GATHER and not last:
                                q = GATHER.index(c)
                                next_x(q, 5 + q + 4 * i)

                    with act.Fori(0, before) as i:
                        experts(i, False)
                    experts(before, True)

        @block.vector
        def _(dve):
            own = Ticks(dve, dve_own)

            def split_lo(s, turn, slot):
                if s >= N_SLOTS:
                    return
                dve.wait_ge(hi_done, slot + 1)
                if s >= RING:
                    dve.wait_ge(used, slot - RING + 1)
                dve.tensor_tensor(w_lo[s % RING][:, :], raw[s % RING][:, :], w_hi[s % RING][:, :].bitcast(F32),
                                  ALU.subtract).then_inc(lo_done, 1)

            def ahead(s, turn=0):
                split_lo(s + RING, turn, s + RING * (1 + turn))

            def chain(*steps):
                for step in steps:
                    own(step())
                    own.sync()

            roots = []

            def inverse_root():
                a_, y, t = (tiny[:, c:c + 2] for c in (224, 228, 230))
                roots.append(0)
                dve.wait_ge(root_done, len(roots))
                chain(lambda: dve.tensor_tensor(t, y, y, ALU.mult),
                      lambda: dve.tensor_tensor(t, t, a_, ALU.mult),
                      lambda: dve.tensor_scalar(t, t, -0.5, 1.5, ALU.mult, ALU.add),
                      lambda: dve.tensor_tensor(y, y, t, ALU.mult))
                return y

            def rms():
                for t in range(NT):
                    own(dve.tensor_tensor_reduce(z[:, t, :], x[:, t, :], x[:, t, :], 1.0, 0.0, ALU.mult, ALU.add,
                                                 tiny[:, 192 + t:193 + t]))
                own.sync()
                dve.tensor_scalar(tiny[:, 224:226], tiny[:, 192:194], 1.0 / D, EPS, ALU.mult, ALU.add).then_inc(root_in, 1)
                return inverse_root()

            def moments(src, eps):
                stats = tiny[:, 200:224]
                for t in range(NT):
                    for c, piece in enumerate(src(t)):
                        own(dve.bn_stats(stats[:, 12 * t + 6 * c:12 * t + 6 * c + 6], piece))
                own.sync()
                for t in range(NT):
                    own(dve.bn_aggr(tiny[:, 192 + 2 * t:194 + 2 * t], stats[:, 12 * t:12 * t + 6 * len(src(t))]))
                own.sync()
                var = tiny[:, 192:196].rearrange("p (t two) -> p t two", two=2)[:, :, 1]
                dve.tensor_scalar(tiny[:, 224:226], var, eps, None, ALU.add).then_inc(root_in, 1)

            def layer_norm():
                moments(lambda t: [x[:, t, 0:512], x[:, t, 512:D]], LN_EPS)
                y = inverse_root()
                for t in range(NT):
                    dve.tensor_scalar(z[:, t, :], x[:, t, :], tiny[:, 192 + 2 * t:193 + 2 * t], y[:, t:t + 1],
                                      ALU.subtract, ALU.mult).then_inc(n_z, 1)

            def gain_rows(i, gain, bias):
                for b in range(4):
                    dve.wait_ge(n_tr, 4 * i + b + 1)
                    for j in range(2):
                        k = 2 * b + j
                        ins = dve.tensor_scalar(xT[:, k, :], a_ps[b][:, j * S:(j + 1) * S], vec[:, gain + k:gain + k + 1],
                                                None if bias is None else vec[:, bias + k:bias + k + 1],
                                                ALU.mult, *(() if bias is None else (ALU.add,)))
                    ins.then_inc(n_ev, 1)
                while later:
                    ahead(later.pop())

            later = []

            def add_residual(s0, halves, scale, between=None):
                for n in range(4 * halves):
                    if n >= 4 * (halves - 1):
                        c = n % 4
                        dve.wait_ge(used, s0 + n + 1)
                        xs = x[:, :, c * S:(c + 1) * S]
                        own(dve.scalar_tensor_tensor(xs, xs, scale, a_ps[c][:, :].rearrange("p (a b) -> p a b", a=2),
                                                     ALU.mult, ALU.add))
                    if n == 4 * halves - 1:
                        later.append(s0 + n)
                    else:
                        ahead(s0 + n)
                    if between:
                        between(n)
                own.sync()

            def router():
                def t3(at):
                    return tiny[:, at:at + 2 * NE].rearrange("p (t e) -> p t e", e=NE)

                lg, on1, on2, eq, gate = t3(16), t3(32), t3(48), t3(64), t3(0)
                mx = [tiny[:, c:c + 2] for c in (92, 94)]
                rank = const[:, C_RANK:C_RANK + NE].unsqueeze(1).to_broadcast([P, NT, NE])

                def wide(c):
                    return c.unsqueeze(2).to_broadcast([P, NT, NE])

                def best(on, m):
                    r = tiny[:, 96:98]
                    chain(lambda: dve.tensor_reduce(m, lg, AX.X, ALU.max),
                          lambda: dve.tensor_tensor(eq, lg, wide(m), ALU.is_equal),
                          lambda: dve.tensor_tensor(eq, eq, rank, ALU.mult),
                          lambda: dve.tensor_reduce(r, eq, AX.X, ALU.max),
                          lambda: dve.tensor_tensor(on, eq, wide(r), ALU.is_equal))

                dve.wait_ge(m_logits, 1)
                dve.tensor_copy(logits, o_ps[0:NE, 0:S]).then_inc(m_copied, 1)
                dve.wait_ge(narrow_full, 4)
                chain(lambda: dve.tensor_copy(lg, a_ps[0][:, 0:64].rearrange("p (a b) -> p a b", a=2)[:, :, 0:NE]))
                best(on1, mx[0])
                chain(lambda: dve.scalar_tensor_tensor(lg, on1, NEG, lg, ALU.mult, ALU.add))
                best(on2, mx[1])
                dve.tensor_tensor(tiny[:, 98:100], mx[1], mx[0], ALU.subtract).then_inc(m_d, 1)
                dve.tensor_tensor(lg, on1, on2, ALU.add).then_inc(m_on, 1)
                dve.wait_ge(m_exp, 1)
                w1_, w2_, den = tiny[:, 102:104], tiny[:, 104:106], tiny[:, 106:108]
                chain(lambda: dve.tensor_scalar(den, tiny[:, 100:102], 1.0, None, ALU.add),
                      lambda: dve.reciprocal(w1_, den),
                      lambda: dve.tensor_tensor(w2_, w1_, tiny[:, 100:102], ALU.mult),
                      lambda: dve.tensor_tensor(on1, on1, wide(w1_), ALU.mult),
                      lambda: dve.tensor_tensor(on2, on2, wide(w2_), ALU.mult))
                for half in range(2):
                    own(dve.tensor_tensor(ranks[:, 1, :, half * NE:(half + 1) * NE], on1, on2, ALU.add))
                dve.wait_ge(h_done, 4)
                dve.memset(f_acc[:, :, :], 0.0).then_inc(m_acc, 1)
                dve.wait_ge(m_rank, 1)
                most = tiny[0:1, 110:111]
                chain(lambda: dve.tensor_tensor(gate, a_ps[1][:, 0:32].rearrange("p (a b) -> p a b", a=2)[:, :, 0:NE], lg, ALU.mult),
                      lambda: dve.tensor_scalar(ranks[:, 0, :, 0:NE], gate, -1.0, None, ALU.add),
                      lambda: dve.tensor_scalar(ranks[:, 0, :, NE:2 * NE], gate, -1.0 - P, None, ALU.add),
                      lambda: dve.tensor_reduce(most, a_ps[1][0:1, 32:32 + NE], AX.X, ALU.max),
                      lambda: dve.tensor_scalar(most, most, P + 0.5, float(PAIRS), ALU.is_gt, ALU.mult))
                dve.tensor_scalar(loops[0:1, 0:1], most, float(PAIRS - 1), None, ALU.add).then_inc(m_loops, 1)

            def select(at, count):
                dve.tensor_copy(ranks_now[:, :, :, :], ranks[:, :, :, at]).then_inc(m_now, 1)
                dve.wait_ge(m_now, 1 + count)
                iota = const[:, C_IOTA:C_IOTA + P]
                for t in range(NT):
                    for e in range(2):
                        r, g = (ranks_now[:, c, t, e:e + 1] for c in range(2))
                        dve.tensor_scalar(sel[:, t, e, :], iota, r, None, ALU.is_equal).then_inc(m_sel, 1)
                        dve.tensor_scalar(sel_g[:, t, e, :], iota, r, g, ALU.is_equal, ALU.mult).then_inc(m_sel, 1)

            def attention(jobs, a0, group_out, between):
                def largest(i, jb):
                    dve.wait_ge(sc_full, a0 + i + 1)
                    table = {"causal": const[:, C_CAUSAL:C_CAUSAL + 384], "dil": extra[:, E_DIL:E_DIL + 384],
                             "cmp": const[:, C_CMP:C_CMP + 2 * NCMP]}[jb["mask"]]
                    for h in range(2):
                        n, slot = a0 + i, 2 * ((a0 + i) % AHEAD) + h
                        if n >= AHEAD:
                            dve.wait_ge(tr_done, 2 * (n - AHEAD + 1))
                        for t, (at, keys) in enumerate(spans(jb)):
                            ins = dve.tensor_tensor_reduce(prob[:, slot, at:at + keys], a_ps[h][:, at:at + keys],
                                                           table[:, at:at + keys], -SCALE, 3e38, ALU.add, ALU.min,
                                                           stat[:, slot, t:t + 1])
                        ins.then_inc(mx_done, 1)

                def inverse_sums(i, jb):
                    m = a0 + i
                    slots = slice(2 * (m % AHEAD), 2 * (m % AHEAD) + 2)
                    dve.wait_ge(ex_done, 2 * m + 2)
                    rs = stat[:, slots, 4:6]
                    chain(lambda: dve.reciprocal(rs, stat[:, slots, 2:4]))
                    if jb["gate"] is not None:
                        gt = gates[:, :, jb["gate"]:jb["gate"] + 2].rearrange("p t h -> p h t")
                        chain(lambda: dve.tensor_tensor(rs, rs, gt, ALU.mult))
                    if m >= 1:
                        dve.wait_ge(tr_done, 2 * m)
                    dve.tensor_tensor(over[:, :, :, :], ident.unsqueeze(1).unsqueeze(1).to_broadcast([P, 2, NT, P]),
                                      rs.unsqueeze(3).to_broadcast([P, 2, NT, P]), ALU.mult).then_inc(over_done, 1)

                def copy_even(i, jb):
                    m = a0 + i
                    dve.wait_ge(tr_done, 2 * m + 1)
                    if m >= 1:
                        dve.wait_ge(pv_done, m)
                    p, w = (NCMP, S) if jb["mask"] == "cmp" else (P, 384)
                    dve.tensor_copy(probT[0:p, 0, 0:w], a_ps[2][0:p, 0:w]).then_inc(pt_done[0], 1)

                for i in range(len(jobs) + 4):
                    if i >= 4 and jobs[i - 4]["last"]:
                        dve.wait_ge(pv_done, a0 + i - 3)
                        group_out(jobs[i - 4]["group"])
                    if i < len(jobs):
                        largest(i, jobs[i])
                    if 1 <= i <= len(jobs):
                        inverse_sums(i - 1, jobs[i - 1])
                    if 2 <= i < len(jobs) + 2:
                        copy_even(i - 2, jobs[i - 2])
                    if i:
                        between(i - 1)

            def part_free(u):
                if u >= 2:
                    dve.wait_ge(y_split, u - 1)

            dve.wait_ge(x_in, 16)
            y = rms()
            for t in range(NT):
                dve.tensor_scalar(z[:, t, :], x[:, t, :], y[:, t:t + 1], None, ALU.mult).then_inc(n_z, 1)
            dve.wait_ge(vec_in, 16)
            dve.wait_ge(const_in, 16)
            gain_rows(0, V_EVEN, None)
            for s in range(RING):
                split_lo(s, 0, s)
            dve.wait_ge(small_hi_done, 1)
            dve.tensor_tensor(small_lo[:, :, :], small_raw, small_hi[:, :, :].bitcast(F32), ALU.subtract).then_inc(small_done, 1)
            for s in range(4):
                ahead(s)
            f, u_, ab, e_, l_, lf = (tiny[:, c:c + 32] for c in (0, 32, 64, 96, 128, 160))
            dve.wait_ge(narrow_full, 1)
            for t in range(NT):
                own(dve.tensor_tensor(f[:, HF * t:HF * t + HF], a_ps[0][:, 32 * t:32 * t + HF], vec[:, V_BF:V_BF + HF], ALU.add))
            own.sync()
            chain(lambda: dve.tensor_scalar(ab, f, -1.0, None, ALU.mult),
                  lambda: dve.tensor_tensor(ab, ab, f, ALU.max))
            dve.tensor_scalar(u_, f, 0.0, None, ALU.min).then_inc(f_in, 1)
            dve.wait_ge(f_exp, 1)
            dve.tensor_scalar(e_, e_, 1.0, None, ALU.add).then_inc(f_ln, 1)
            dve.wait_ge(f_exp, 2)
            dve.tensor_tensor(lf, u_, l_, ALU.subtract).then_inc(f_log, 1)
            dve.wait_ge(extra_in, 16)
            for s in range(4, 12):
                ahead(s)

            def even_y(u, o):
                s = EV_G[0] + u
                dve.wait_ge(g_free[s % 3], g_nth[s] + 1)
                part_free(u)
                dve.tensor_tensor(part[:, u % 2, :], o[:, 2 * (u % 4):2 * (u % 4) + 2, :].rearrange("p a b -> p (a b)"),
                                  gate_even(u), ALU.mult).then_inc(y_made, 1)

            def outputs_to(o):
                return lambda g: dve.tensor_copy(o[:, g, :], o_ps[:, 0:S]).then_inc(o_free, 1)

            def with_gates(i):
                if i < 8:
                    if i < 4:
                        even_y(i, oT)
                    ahead(EV_G[0] + i)
                else:
                    ahead(EV_OUT + i - 8)
                    if i > 8:
                        even_y(i - 5, oT2)

            attention(pairs_even(0), 0, outputs_to(oT), lambda i: ahead(12 + i) if i < 11 else None)
            ahead(23)
            dve.wait_ge(o_free, 8)
            attention(pairs_even(1), 8, outputs_to(oT2), with_gates)
            dve.wait_ge(o_free, 16)
            for u in range(6, 8):
                even_y(u, oT2)
            ahead(EV_OUT + 3)
            add_residual(EV_OUT + 4, 1, 1.0)

            y = rms()
            for t in range(NT):
                dve.tensor_scalar(z[:, t, :], x[:, t, :], y[:, t:t + 1], None, ALU.mult).then_inc(n_z, 1)
            gain_rows(1, V_ODD, None)
            dve.wait_ge(extra_in, 32)
            dve.wait_ge(n_lo, 8)
            cos, sin = (extra[:, c:c + S].unsqueeze(1).to_broadcast([P, 2, S]) for c in (O_COS, O_SIN))
            for s in range(OD_QK, OD_QK + 8):
                m, j = s - OD_QK, s % 3
                dst = (rq if m < 4 else rk)[:, m % 4, :, :]
                ps = g_ps[j][:, :].rearrange("p (a b) -> p a b", a=2)
                cc, ss = (part[:, c, :].rearrange("p (a b) -> p a b", a=2) for c in range(2))
                dve.wait_ge(used, s + 1)
                own(dve.tensor_tensor(cc, ps, cos, ALU.mult))
                dve.tensor_tensor(ss, ps, sin, ALU.mult).then_inc(g_free[j], 1)
                own.sync()
                dve.wait_ge(g_free[j], g_nth[s] + 1)
                own(dve.tensor_tensor(dst[:, 0, :], cc[:, 0, :], ss[:, 1, :], ALU.subtract))
                own(dve.tensor_tensor(dst[:, 1, :], ss[:, 0, :], cc[:, 1, :], ALU.add))
                own.sync()
                ahead(s)
            for s in range(OD_V, OD_V + 8):
                ahead(s)

            def decayed(h):
                dve.wait_ge(r_sc, h + 1)
                dve.tensor_tensor(prob[:, 4 + h % 2, :], a_ps[0][:, 0:384], extra[:, O_RET + 384 * h:O_RET + 384 * (h + 1)],
                                  ALU.mult).then_inc(r_dec, 1)

            def gate_slot(u):
                s = OD_G + u
                dve.wait_ge(r_norm, u // 2 + 1)
                dve.wait_ge(g_free[s % 3], g_nth[s] + 1)
                dst = rv[:, :, u * S:(u + 1) * S]
                dve.tensor_tensor(dst, dst, gate_view(s).rearrange("p (a b) -> p a b", a=2), ALU.mult).then_inc(r_y, 1)

            def high_part(b):
                dve.wait_ge(r_ev, b + 1)
                dve.tensor_copy(y_hi[:, 2 * b:2 * b + 2, :], oyT[:, 2 * b:2 * b + 2, :]).then_inc(r_hi, 1)

            gated = 0
            for h in range(RH):
                decayed(h)
                for u in G_AFTER[h]:
                    ahead(OD_G + u)
                    while gated <= u and gated < 2 * h:
                        gate_slot(gated)
                        gated += 1
                dve.wait_ge(r_out, h + 1)
                moments(lambda t: [a_ps[1 + t][:, :]], EPS)
                y = inverse_root()
                for t in range(NT):
                    ins = dve.tensor_scalar(rv[:, t, h * RV:(h + 1) * RV], a_ps[1 + t][:, :],
                                            tiny[:, 192 + 2 * t:193 + 2 * t], y[:, t:t + 1], ALU.subtract, ALU.mult)
                ins.then_inc(r_norm, 1)
            for u in range(5, 8):
                ahead(OD_G + u)
                while gated <= u:
                    gate_slot(gated)
                    gated += 1
                for b in (2 * (u - 5), 2 * (u - 5) + 1):
                    high_part(b)
            add_residual(OD_OUT, 2, 1.0, lambda n: high_part(6 + n) if n < 2 else None)

            y = rms()
            dve.wait_ge(final_in, 16)
            for t in range(NT):
                own(dve.scalar_tensor_tensor(x[:, t, :], x[:, t, :], y[:, t:t + 1], view(6144, (D,)), ALU.mult, ALU.mult))
            own.sync()
            layer_norm()
            gain_rows(2, V_LN, V_LN + 8)
            for l in range(DEPTH):
                s0 = L_IN[l]
                if l:
                    layer_norm()
                    gain_rows(4, V_LN + 32, V_LN + 40)
                dve.wait_ge(n_lo, 4 * (3 + 2 * l))
                dve.wait_ge(h_done, 1 + 2 * l)
                for s in range(s0, s0 + 4):
                    ahead(s)
                dve.wait_ge(gates_done, l + 1)
                for t in range(NT):
                    own(dve.tensor_scalar(gates[:, t, 0:NH], gates[:, t, 0:NH], const[:, C_ROW + t:C_ROW + t + 1],
                                          None, ALU.mult))

                def blocks(s, ps):
                    dve.wait_ge(used, s + 1)
                    for kind in range(2):
                        pos = V_POS + 32 * l + 16 * kind
                        for g in range(NKV):
                            for par in range(2):
                                for half in range(2):
                                    src = ps[64 * g:64 * g + 64, kind, :].rearrange(
                                        "p (n r two) -> p r n two", two=2, r=8)[:, :, half:half + NCMP, par]
                                    to = slice(64 * par, 64 * par + 64)
                                    ins = dve.tensor_tensor(
                                        xc[to, kind, 8 * half:8 * half + 8, g * NCMP:(g + 1) * NCMP], src,
                                        vec[to, pos + 8 * half:pos + 8 * half + 8].unsqueeze(2)
                                        .to_broadcast([64, 8, NCMP]), ALU.add)
                                    if kind + g + par + half < 4:
                                        own(ins)
                    ins.then_inc(g_free[s % 3], 1)
                    dve.wait_ge(g_free[s % 3], g_nth[s] + 1)
                    dve.tensor_scalar(tiny[:, 250:251], tiny[:, 192:193], 0.0, None, ALU.mult).then_inc(xc_made, 1)

                def gated_input(s, ps, k):
                    dve.wait_ge(used, s + 1)
                    u = s0 + I_U + k // 2
                    dve.wait_ge(g_free[u % 3], g_nth[u] + 1)
                    dve.tensor_tensor(cz[:, k:k + 2, 2:2 + S], ps, cu[:, k:k + 2, :], ALU.mult).then_inc(g_free[s % 3], 1)
                    dve.wait_ge(g_free[s % 3], g_nth[s] + 1)

                def convolved(s, ps, k):
                    yp = part[:, k // 2, :].rearrange("p (a b) -> p a b", a=2)
                    part_free(Y_L[l] + k // 2)
                    dve.wait_ge(z_pad, 2 + l)
                    for tap in range(3):
                        for q in range(2):
                            w = vec[:, V_CONV + 12 * l + 4 * tap + k + q:V_CONV + 12 * l + 4 * tap + k + q + 1]
                            src = cz[:, k + q, tap:tap + S]
                            if tap == 0:
                                own(dve.tensor_scalar(yp[:, q, :], src, w, None, ALU.mult))
                            else:
                                own(dve.scalar_tensor_tensor(yp[:, q, :], src, w, yp[:, q, :], ALU.mult, ALU.add))
                        own.sync()
                    dve.wait_ge(used, s + 1)
                    dve.tensor_tensor(yp, yp, ps, ALU.mult).then_inc(g_free[s % 3], 1)

                def between(i):
                    if i == STEP_KV:
                        j, _ = kv_turn(l)
                        dve.wait_ge(kv_full, l + 1)
                        dve.tensor_scalar(kc2[:, :], g_ps[j][:, 0:30], vec[:, V_B2K + l:V_B2K + l + 1], None,
                                          ALU.add).then_inc(kc_done, 1)
                        dve.tensor_tensor(vc2[:, :, :], g_ps[j][0:NCMP, 128:256].rearrange("p (a b) -> p a b", a=2),
                                          vec[0:NCMP, V_B2V + 64 * l:V_B2V + 64 * (l + 1)].unsqueeze(1)
                                          .to_broadcast([NCMP, 2, HD]), ALU.add).then_inc(g_free[j], 1)
                    for m in L_STEPS.get(i, ()):
                        s = s0 + m
                        ps = g_ps[s % 3][:, :].rearrange("p (a b) -> p a b", a=2)
                        if m == I_KC:
                            blocks(s, ps)
                        elif m in (I_C, I_C + 1):
                            gated_input(s, ps, 2 * (m - I_C))
                        elif m in (I_B, I_B + 1):
                            convolved(s, ps, 2 * (m - I_B))
                        ahead(s)
                def outputs(g):
                    if g < 4:
                        dve.tensor_copy(soT[:, g, :], o_ps[:, 0:S]).then_inc(o_free, 1)
                    else:
                        g -= 4
                        part_free(Y_L[l] + 2 + g)
                        dve.wait_ge(o_free, 16 + 4 * l + 4)
                        dve.tensor_tensor(part[:, g % 2, 0:S], o_ps[:, 0:S], soT[:, g, :], ALU.add).then_inc(y_made, 1)

                own.sync()
                attention(pairs_sparse(l), A_L[l], outputs, between)
                add_residual(L_WO[l], 1, ALPHA)
                layer_norm()
                gain_rows(3 + 2 * l, V_LN + 16 + 32 * l, V_LN + 24 + 32 * l)

                def hidden(s, u0, m, count):
                    j, yp = s % 3, part[:, m % 2, 0:S]
                    dve.wait_ge(gate_done, count)
                    dve.wait_ge(y_split, u0 - 1)
                    dve.tensor_tensor(yp, gate_view(s)[:, 0:S], g_ps[j][:, S:2 * S], ALU.mult).then_inc(g_free[j], 1)

                if l == 0:
                    for m in range(FT):
                        hidden(FFN_IN + m, Y_FFN + m, m, m + 1)
                        ahead(FFN_IN + m)
                    dve.wait_ge(h_done, 2)
                    for s in range(FFN_DOWN, FFN_DOWN + 10):
                        ahead(s)
                    later.append(FFN_DOWN + 10)
                    dve.wait_ge(used, FFN_DOWN + 11)
                    for t in range(NT):
                        for n in range(2):
                            xs = x[:, t, n * 512:(n + 1) * 512]
                            own(dve.scalar_tensor_tensor(xs, xs, ALPHA, a_ps[2 * t + n][:, :], ALU.mult, ALU.add))
                    own.sync()
                    continue
                router()
                select(slice(0, 2), 0)
                before = loops_of(dve)

                def next_x(q, count, bank=o_ps):
                    dve.wait_ge(m_xhi, count)
                    dve.tensor_tensor(x_lo[:, 2 * q:2 * q + 2, :], bank[:, :].rearrange("p (a b) -> p a b", a=2),
                                      x_hi[:, 2 * q:2 * q + 2, :].bitcast(F32), ALU.subtract).then_inc(m_xlo, 1)

                for q in range(4):
                    next_x(q, q + 1, a_ps[q])

                def experts(i, last):
                    def y_low(c):
                        dve.wait_ge(m_yhi, c + 1 + FT // 2 * i)
                        dve.tensor_tensor(y_lo[:, 2 * c:2 * c + 2, 0:P],
                                          a_ps[2 + c % 2][:, 0:S].rearrange("p (a b) -> p a b", a=2),
                                          y_hi[:, 2 * c:2 * c + 2, 0:P].bitcast(F32), ALU.subtract).then_inc(m_y, 1)

                    for m in range(FT):
                        s = MOE + m
                        if m % 2 == 0 and m >= 4:
                            y_low((m - 4) // 2)
                        dve.wait_ge(gate_done, FT + m + 1 + FT * i)
                        if m >= 8:
                            dve.wait_ge(m_ytr, (m - 8) // 2 + 1 + FT // 2 * i)
                        dve.tensor_tensor(hidden_at(m), gate_view(s)[:, 0:P], g_ps[s % 3][:, P:2 * P],
                                          ALU.mult).then_inc(g_free[s % 3], 1)
                        ahead(s, 11 * i)
                        if m == 11 and not last:
                            dve.wait_ge(m_tr, 1 + i)
                            select(bass.ds(2 * i + 2, 2), 1 + i)
                    for c in range(11):
                        if c < 2:
                            y_low(9 + c)
                        if c in (6, 10):
                            e = c // 10
                            dve.wait_ge(used, MOE + FT + (6 if e == 0 else 11) + 33 * i)
                            dve.tensor_copy(o_sb[:, e, 512:D], a_ps[2 * e + 1][:, :]).then_inc(m_osb, 1)
                        if not (last and c >= 8):
                            ahead(MOE + FT + c, 11 * i)
                        if c in GATHER and not last:
                            q = GATHER.index(c)
                            next_x(q, 5 + q + 4 * i)
                    dve.wait_ge(m_sct, 1 + i)
                    dve.wait_ge(m_acc, 1 + 4 * i)
                    for t in range(NT):
                        for n in range(2):
                            fa = f_acc[:, t, n * 512:(n + 1) * 512]
                            dve.tensor_tensor(fa, fa, a_ps[2 * t + n][:, :], ALU.add).then_inc(m_acc, 1)

                with dve.Fori(0, before) as i:
                    experts(i, False)
                experts(before, True)
                dve.wait_ge(m_acc, 5 + 4 * before)
                for t in range(NT):
                    own(dve.scalar_tensor_tensor(x[:, t, :], x[:, t, :], ALPHA, f_acc[:, t, :], ALU.mult, ALU.add))
                own.sync()
            layer_norm()
            dve.wait_ge(rows_in, 80)
            dve.wait_ge(n_z, 14)
            own(dve.tensor_tensor(x[:, 1, :], z[:, 1, :], row[:, 0, :], ALU.mult))
            own.sync()
            dve.tensor_tensor(x[:, 1, :], x[:, 1, :], row[:, 1, :], ALU.add).then_inc(h_done, 1)


def in_slots(w):
    n = w.shape[1] // S
    return w.reshape(KD, P, n, S).transpose(2, 1, 0, 3).reshape(n, P, SLOT)


def out_slots_of(w):
    h = w.shape[0] // D
    return w.reshape(h, KD, P, 4, S).transpose(0, 3, 2, 1, 4).reshape(4 * h, P, SLOT)


def ffn_slots(wg, wu, wd):
    gu = np.stack([wg.reshape(KD, P, FT, P), wu.reshape(KD, P, FT, P)], 3)
    return np.concatenate([gu.transpose(2, 1, 0, 3, 4).reshape(FT, P, SLOT),
                           wd.reshape(FT // 2, 2, P, D).transpose(0, 2, 1, 3).reshape(FT // 2, P, SLOT)])


def lay_out(i):
    i = {k: np.asarray(v, np.float32) if np.asarray(v).dtype != np.float32 else np.asarray(v) for k, v in i.items()}
    ev, od = i["even_w_in"][0], i["odd_w_in"][0]
    w = []
    fox, dil = (in_slots(ev[:, at:at + 4096]) for at in (0, 4096 + HF))
    w += [fox[:12], dil[:12], fox[12:], dil[12:]]
    w.append(out_slots_of(i["even_w_out"][0]))
    qk = od[:, :2048].reshape(D, 8, P, 2).transpose(0, 1, 3, 2).reshape(D, 2048)
    w += [in_slots(np.ascontiguousarray(qk)), in_slots(od[:, 2048:]), out_slots_of(i["odd_w_out"][0])]
    small = [ev[:, 4096:4096 + HF]]
    for l in range(DEPTH):
        wi = i["w_in_2"][l]
        q, kc, vc, ks, vs, kw, vw, gt, u, bg, cg = np.split(wi, np.cumsum([512, 128, 128, 128, 128, 128, 128, 24, 512, 512]), 1)
        small.append(gt)
        w.append(in_slots(np.concatenate([q, ks, kw, vs, vw, kc, vc, u], 1)))
        for kind in range(2):
            w.append(i["cmp_w1_2"][l, kind].reshape(2, KD, P, S).transpose(0, 2, 1, 3).reshape(2, P, SLOT))
        w.append(in_slots(np.concatenate([cg, bg], 1)))
        w.append(out_slots_of(i["w_o_2"][l]))
        if l == 0:
            w.append(ffn_slots(i["ffn_wg_2"][0], i["ffn_wu_2"][0], i["ffn_wd_2"][0]))
        else:
            for e in range(0, NE, 2):
                wg, wu = (np.concatenate([i[k][0, e], i[k][0, e + 1]], 1) for k in ("moe_wg_2", "moe_wu_2"))
                w.append(ffn_slots(wg, wu, i["moe_wd_2"][0, e:e + 2].reshape(-1, D)))
    small.append(i["moe_router_2"][0])
    vec = np.zeros((P, N_VEC), np.float32)

    def tiles(a):
        return a.reshape(-1, P).T

    vec[:, V_EVEN:V_EVEN + 8], vec[:, V_ODD:V_ODD + 8] = tiles(i["even_norm"][0]), tiles(i["odd_norm"][0])
    norms = [("ln_in", None), ("ln1", 0), ("ln2", 0), ("ln1", 1), ("ln2", 1)]
    pick = [[i[f"{n}_{c}_2"] if l is None else i[f"{n}_{c}_2"][l] for c in "gb"] for n, l in norms]
    for j in range(4):
        for c in range(2):
            vec[:, V_LN + 16 * j + 8 * c:V_LN + 16 * j + 8 * c + 8] = tiles(pick[j][c])
    vec[:, V_BF:V_BF + HF] = i["even_b_f"][0][None]
    w2 = np.zeros((DEPTH, P, 2, 2, P), np.float32)
    for l in range(DEPTH):
        for kind in range(2):
            vec[:, V_POS + 32 * l + 16 * kind:V_POS + 32 * l + 16 * kind + 16] = tiles(i["cmp_pos_2"][l, kind])
            vec[:, V_B1 + 4 * l + 2 * kind:V_B1 + 4 * l + 2 * kind + 2] = tiles(i["cmp_b1_2"][l, kind])
            two = i["cmp_w2_2"][l, kind].reshape(2, P, HD).transpose(1, 0, 2)
            w2[l, :, kind, :, :HD] = two
            if kind == 0:
                w2[l, :, kind, :, HD:] = two
        vec[:, V_B2K + l] = np.tile(i["cmp_b2_2"][l, 0], 2)
        vec[:, V_B2V + 64 * l:V_B2V + 64 * (l + 1)] = i["cmp_b2_2"][l, 1][None]
        for tap in range(3):
            vec[:, V_CONV + 12 * l + 4 * tap:V_CONV + 12 * l + 4 * tap + 4] = tiles(i["conv_w_2"][l, tap])
    const, extra = shape_constants()
    return {
        "x": i["x"][0], "w": np.concatenate(w), "const": const, "extra": extra, "vec": vec, "w2": w2,
        "small": np.ascontiguousarray(np.concatenate(small, 1).reshape(KD, P, NSMALL).transpose(1, 0, 2)),
        "rows_final": np.ascontiguousarray(np.broadcast_to(i["final_norm"], (P, D))),
        "rows": np.ascontiguousarray(np.broadcast_to(np.array(pick)[:, :, None], (5, 2, P, D))),
    }


def kernel(**inputs):
    import concourse.bacc as bacc
    from concourse.bass_utils import run_bass_kernel_spmd

    arrays = lay_out(inputs)
    nc = bacc.Bacc("TRN2", target_bir_lowering=False, num_devices=1)
    aps = {k: nc.dram_tensor(k + "_dram", v.shape, F32, kind="ExternalInput").ap() for k, v in arrays.items()}
    out = nc.dram_tensor("out_dram", (1, S, D), F32, kind="ExternalOutput").ap()
    build(nc, aps, out)
    r = run_bass_kernel_spmd(nc, [{k + "_dram": v for k, v in arrays.items()}], core_ids=[0])
    return r.results[0]["out_dram"]
```
